# Optimizing a Trainium2 kernel written in Bass

```python
import math, functools
import jax, jax.numpy as jnp
from jax import lax
import numpy as np

D_MODEL = 1024
BATCH = 1
SEQ = 512
DEPTH = 1
DEC_BATCH = 8
DEC_SEQ = 1
PAST_LEN = 2048
PAGE_SIZE = 128

MLA_HEADS = 8
D_NOPE = 128
D_ROPE = 64
D_QK = D_NOPE + D_ROPE
D_V = 128
D_LATENT = 512
ROPE_THETA = 10000.0
Q_BLOCK = 128
D_INNER = 2 * D_MODEL
SSM_HEADDIM = 64
SSM_HEADS = D_INNER // SSM_HEADDIM
SSM_GROUPS = 4
D_STATE = 128
CONV_W = 4
CONV_DIM = D_INNER + 2 * SSM_GROUPS * D_STATE
SSD_CHUNK = 128
PEER_HEADS = 8
N_KEYS = 128
N_EXPERTS = N_KEYS * N_KEYS
D_KEY = 256
PEER_TOPK = 16
TOK_BLOCK = 128
N_ADA = 6
EPS = 1e-6
IN_SPLITS = (MLA_HEADS * D_QK, D_LATENT, D_ROPE, D_INNER, CONV_DIM, SSM_HEADS, D_MODEL, D_MODEL)
IN_DIM = sum(IN_SPLITS)
IN_OFFSETS = tuple(int(v) for v in np.cumsum(IN_SPLITS)[:-1])

kernel_name = "hybrid_mla_ssd_peer_adaln_step"

def rms_norm(x, g):
    x32 = x.astype(jnp.float32)
    y = x32 * lax.rsqrt(jnp.mean(x32 * x32, axis=-1, keepdims=True) + EPS)
    return (y * g.astype(jnp.float32)).astype(x.dtype)

def rope(x, pos):
    half = D_ROPE // 2
    inv = ROPE_THETA ** (-jnp.arange(half, dtype=jnp.float32) / half)
    ang = pos.astype(jnp.float32)[:, None] * inv[None, :]
    ang = ang.reshape(ang.shape[:1] + (1,) * (x.ndim - 3) + ang.shape[1:])
    cos = jnp.cos(ang).astype(x.dtype)
    sin = jnp.sin(ang).astype(x.dtype)
    x1, x2 = x[..., :half], x[..., half:]
    return jnp.concatenate([x1 * cos - x2 * sin, x2 * cos + x1 * sin], axis=-1)

def mla_keys(ckv, kpe, w_uk, g_k):
    k_nope = jnp.einsum('...c,chd->...hd', ckv, w_uk)
    k_pe = jnp.broadcast_to(kpe[..., None, :], k_nope.shape[:-1] + (D_ROPE,))
    return rms_norm(jnp.concatenate([k_nope, k_pe], axis=-1), g_k)

def mla_prompt(q, ckv, kpe, w_uk, w_uv, g_k):
    b, s = q.shape[:2]
    k = mla_keys(ckv, kpe, w_uk, g_k)
    qb_len = math.gcd(s, Q_BLOCK)
    nblk = s // qb_len
    q_blocks = jnp.moveaxis(q.reshape(b, nblk, qb_len, MLA_HEADS, D_QK), 1, 0)
    starts = jnp.arange(nblk, dtype=jnp.int32) * qb_len
    key_pos = jnp.arange(s, dtype=jnp.int32)
    scale = D_QK ** -0.5

    def one_block(args):
        qi, s0 = args
        q_pos = s0 + jnp.arange(qb_len, dtype=jnp.int32)
        sc = jnp.einsum('bqhd,bkhd->bhqk', qi, k).astype(jnp.float32) * scale
        sc = jnp.where(key_pos[None, :] <= q_pos[:, None], sc, -jnp.inf)
        p = jax.nn.softmax(sc, axis=-1).astype(ckv.dtype)
        o_lat = jnp.einsum('bhqk,bkc->bqhc', p, ckv)
        return jnp.einsum('bqhc,chv->bqhv', o_lat, w_uv)

    o = lax.map(one_block, (q_blocks, starts))
    return jnp.moveaxis(o, 0, 1).reshape(b, s, MLA_HEADS * D_V)

def mla_sample(q, ckv, kpe, cache_ckv, cache_kpe, page_table, w_uk, w_uv, g_k):
    db, t = q.shape[:2]
    past = page_table.shape[1] * cache_ckv.shape[1]
    key_pos = jnp.arange(past + t, dtype=jnp.int32)
    q_pos = past + jnp.arange(t, dtype=jnp.int32)
    mask = key_pos[None, :] <= q_pos[:, None]
    scale = D_QK ** -0.5

    def one_seq(args):
        qi, ckv_i, kpe_i, pages = args
        ckv_all = jnp.concatenate([cache_ckv[pages].reshape(past, D_LATENT), ckv_i], axis=0)
        kpe_all = jnp.concatenate([cache_kpe[pages].reshape(past, D_ROPE), kpe_i], axis=0)
        k = mla_keys(ckv_all, kpe_all, w_uk, g_k)
        sc = jnp.einsum('qhd,khd->hqk', qi, k).astype(jnp.float32) * scale
        sc = jnp.where(mask[None], sc, -jnp.inf)
        p = jax.nn.softmax(sc, axis=-1).astype(ckv_all.dtype)
        o_lat = jnp.einsum('hqk,kc->qhc', p, ckv_all)
        return jnp.einsum('qhc,chv->qhv', o_lat, w_uv)

    o = lax.map(one_seq, (q, ckv, kpe, page_table))
    return o.reshape(db, t, MLA_HEADS * D_V)

def causal_conv(xbc, conv_state, w, bias):
    t = xbc.shape[1]
    xpad = jnp.concatenate([conv_state, xbc], axis=1)
    y = bias
    for k in range(CONV_W):
        y = y + xpad[:, k:k + t] * w[k]
    return jax.nn.silu(y), xpad[:, -(CONV_W - 1):]

def ssd_scan(x, dt, a, bmat, cmat, h0):
    b, t = x.shape[:2]
    r = SSM_HEADS // SSM_GROUPS
    q = math.gcd(t, SSD_CHUNK)
    nc = t // q

    def chunks(z):
        return jnp.moveaxis(z.reshape((b, nc, q) + z.shape[2:]), 1, 0)

    xs = (chunks(x.astype(jnp.float32).reshape(b, t, SSM_GROUPS, r, SSM_HEADDIM)),
          chunks(dt.reshape(b, t, SSM_GROUPS, r)),
          chunks(bmat.astype(jnp.float32)),
          chunks(cmat.astype(jnp.float32)))
    a_gr = a.reshape(SSM_GROUPS, r)
    causal = jnp.tril(jnp.ones((q, q), dtype=bool))

    def step(h, inp):
        xc, dtc, bc, cc = inp
        acs = jnp.cumsum(dtc * a_gr, axis=1)
        seg = acs[:, :, None] - acs[:, None, :]
        decay = jnp.exp(jnp.where(causal[None, :, :, None, None], seg, -jnp.inf))
        cb = jnp.einsum('bign,bjgn->bijg', cc, bc)
        w = cb[..., None] * decay * dtc[:, None]
        y_diag = jnp.einsum('bijgr,bjgrp->bigrp', w, xc)
        y_off = jnp.einsum('bign,bgrpn->bigrp', cc, h) * jnp.exp(acs)[..., None]
        to_end = jnp.exp(acs[:, -1:] - acs) * dtc
        h_new = jnp.exp(acs[:, -1])[..., None, None] * h + jnp.einsum('bjgn,bjgr,bjgrp->bgrpn', bc, to_end, xc)
        return h_new, y_diag + y_off

    h_init = h0.astype(jnp.float32).reshape(b, SSM_GROUPS, r, SSM_HEADDIM, D_STATE)
    h_fin, ys = lax.scan(step, h_init, xs)
    y = jnp.moveaxis(ys, 0, 1).reshape(b, t, SSM_HEADS, SSM_HEADDIM)
    return y, h_fin.reshape(b, SSM_HEADS, SSM_HEADDIM, D_STATE)

def ssm_branch(z, xbc_raw, dt_raw, conv_state, ssm_state, conv_w, conv_b, dt_bias, a_log, d_skip, g_ssm):
    xbc, new_conv = causal_conv(xbc_raw, conv_state, conv_w, conv_b)
    b, t = xbc.shape[:2]
    xs, bm, cm = jnp.split(xbc, [D_INNER, D_INNER + SSM_GROUPS * D_STATE], axis=-1)
    xs = xs.reshape(b, t, SSM_HEADS, SSM_HEADDIM)
    bm = bm.reshape(b, t, SSM_GROUPS, D_STATE)
    cm = cm.reshape(b, t, SSM_GROUPS, D_STATE)
    dt = jax.nn.softplus(dt_raw.astype(jnp.float32) + dt_bias.astype(jnp.float32))
    a = -jnp.exp(a_log.astype(jnp.float32))
    y, new_ssm = ssd_scan(xs, dt, a, bm, cm, ssm_state)
    y = y + d_skip.astype(jnp.float32)[:, None] * xs.astype(jnp.float32)
    y = y.reshape(b, t, D_INNER).astype(z.dtype)
    y = rms_norm(y * jax.nn.silu(z), g_ssm)
    return y, new_conv, new_ssm.astype(ssm_state.dtype)

def peer_ffn(h, wq, keys1, keys2, u_tab, v_tab):
    shp = h.shape
    tok = h.reshape(-1, D_MODEL)
    n = tok.shape[0]
    tok = jnp.pad(tok, ((0, (-n) % TOK_BLOCK), (0, 0)))
    blocks = tok.reshape(-1, TOK_BLOCK, D_MODEL)
    half = D_KEY // 2

    def one_block(hb):
        qh = (hb @ wq).reshape(TOK_BLOCK, PEER_HEADS, D_KEY)
        s1 = jnp.einsum('thd,hnd->thn', qh[..., :half], keys1).astype(jnp.float32)
        s2 = jnp.einsum('thd,hnd->thn', qh[..., half:], keys2).astype(jnp.float32)
        v1, i1 = lax.top_k(s1, PEER_TOPK)
        v2, i2 = lax.top_k(s2, PEER_TOPK)
        cand = (v1[..., :, None] + v2[..., None, :]).reshape(TOK_BLOCK, PEER_HEADS, PEER_TOPK * PEER_TOPK)
        cid = (i1[..., :, None] * N_KEYS + i2[..., None, :]).reshape(TOK_BLOCK, PEER_HEADS, PEER_TOPK * PEER_TOPK)
        top_s, j = lax.top_k(cand, PEER_TOPK)
        ids = jnp.take_along_axis(cid, j, axis=-1)
        g = jax.nn.softmax(top_s, axis=-1).astype(hb.dtype)
        act = jax.nn.gelu(jnp.einsum('thkd,td->thk', u_tab[ids], hb), approximate=False)
        return jnp.einsum('thk,thkd->td', g * act, v_tab[ids])

    out = lax.map(one_block, blocks).reshape(-1, D_MODEL)[:n]
    return out.reshape(shp)

def trunk_layer(x, c, positions, conv_state, ssm_state, attend, lp):
    b, t = x.shape[:2]
    ada = (c @ lp['w_ada'] + lp['b_ada'])[:, None, :]
    sh1, sc1, gt1, sh2, sc2, gt2 = jnp.split(ada, N_ADA, axis=-1)
    h = rms_norm(x, lp['g_mix']) * (1 + sc1) + sh1
    proj = h @ lp['w_in']
    q_raw, ckv_raw, kpe_raw, z, xbc_raw, dt_raw, gate_a, gate_b = jnp.split(proj, IN_OFFSETS, axis=-1)
    q = q_raw.reshape(b, t, MLA_HEADS, D_QK)
    q = rms_norm(jnp.concatenate([q[..., :D_NOPE], rope(q[..., D_NOPE:], positions)], axis=-1), lp['g_q'])
    ckv = rms_norm(ckv_raw, lp['g_ckv'])
    kpe = rope(kpe_raw, positions)
    o_a = attend(q, ckv, kpe)
    y_b, new_conv, new_ssm = ssm_branch(z, xbc_raw, dt_raw, conv_state, ssm_state, lp['conv_w'], lp['conv_b'],
                                        lp['dt_bias'], lp['a_log'], lp['d_skip'], lp['g_ssm'])
    merged = jax.nn.sigmoid(gate_a) * (o_a @ lp['w_br_a']) + jax.nn.sigmoid(gate_b) * (y_b @ lp['w_br_b'])
    x = x + gt1 * (merged @ lp['w_out'])
    h2 = rms_norm(x, lp['g_ffn']) * (1 + sc2) + sh2
    x = x + gt2 * peer_ffn(h2, lp['peer_wq'], lp['peer_keys1'], lp['peer_keys2'], lp['peer_u'], lp['peer_v'])
    return x, ckv, kpe, new_conv, new_ssm

def setup_inputs(seed: int = 0) -> dict:
    key = jax.random.key(seed)
    ks = iter(jax.random.split(key, 48))

    def nrm(shape, scale):
        return jax.random.normal(next(ks), shape, jnp.float32) * scale

    def gain(shape):
        return 1.0 + nrm(shape, 0.02)

    n_pages = PAST_LEN // PAGE_SIZE
    n_used = DEC_BATCH * n_pages
    n_pool = n_used + n_used // 4
    page_table = jax.random.permutation(next(ks), n_pool)[:n_used].reshape(DEC_BATCH, n_pages).astype(jnp.int32)
    dt0 = jnp.exp(jax.random.uniform(next(ks), (DEPTH, SSM_HEADS), jnp.float32, math.log(1e-3), math.log(1e-1)))
    return {
        'x_prompt': nrm((BATCH, SEQ, D_MODEL), 1.0),
        'x_sample': nrm((DEC_BATCH, DEC_SEQ, D_MODEL), 1.0),
        'c_prompt': nrm((BATCH, D_MODEL), 1.0),
        'c_sample': nrm((DEC_BATCH, D_MODEL), 1.0),
        'cache_ckv': nrm((DEPTH, n_pool, PAGE_SIZE, D_LATENT), 1.0),
        'cache_kpe': nrm((DEPTH, n_pool, PAGE_SIZE, D_ROPE), 1.0),
        'page_table': page_table,
        'state_conv': nrm((DEPTH, DEC_BATCH, CONV_W - 1, CONV_DIM), 1.0),
        'state_ssm': nrm((DEPTH, DEC_BATCH, SSM_HEADS, SSM_HEADDIM, D_STATE), 0.5),
        'w_ada': nrm((DEPTH, D_MODEL, N_ADA * D_MODEL), 0.5 * D_MODEL ** -0.5),
        'b_ada': nrm((DEPTH, N_ADA * D_MODEL), 0.01),
        'g_mix': gain((DEPTH, D_MODEL)),
        'w_in': nrm((DEPTH, D_MODEL, IN_DIM), D_MODEL ** -0.5),
        'g_q': gain((DEPTH, D_QK)),
        'g_ckv': gain((DEPTH, D_LATENT)),
        'w_uk': nrm((DEPTH, D_LATENT, MLA_HEADS, D_NOPE), D_LATENT ** -0.5),
        'w_uv': nrm((DEPTH, D_LATENT, MLA_HEADS, D_V), D_LATENT ** -0.5),
        'g_k': gain((DEPTH, D_QK)),
        'conv_w': nrm((DEPTH, CONV_W, CONV_DIM), CONV_W ** -0.5),
        'conv_b': nrm((DEPTH, CONV_DIM), 0.01),
        'dt_bias': dt0 + jnp.log(-jnp.expm1(-dt0)),
        'a_log': jnp.log(jax.random.uniform(next(ks), (DEPTH, SSM_HEADS), jnp.float32, 1.0, 16.0)),
        'd_skip': 1.0 + nrm((DEPTH, SSM_HEADS), 0.1),
        'g_ssm': gain((DEPTH, D_INNER)),
        'w_br_a': nrm((DEPTH, MLA_HEADS * D_V, D_MODEL), (MLA_HEADS * D_V) ** -0.5),
        'w_br_b': nrm((DEPTH, D_INNER, D_MODEL), D_INNER ** -0.5),
        'w_out': nrm((DEPTH, D_MODEL, D_MODEL), D_MODEL ** -0.5),
        'g_ffn': gain((DEPTH, D_MODEL)),
        'peer_wq': nrm((DEPTH, D_MODEL, PEER_HEADS * D_KEY), D_MODEL ** -0.5),
        'peer_keys1': nrm((DEPTH, PEER_HEADS, N_KEYS, D_KEY // 2), (D_KEY // 2) ** -0.5),
        'peer_keys2': nrm((DEPTH, PEER_HEADS, N_KEYS, D_KEY // 2), (D_KEY // 2) ** -0.5),
        'peer_u': nrm((DEPTH, N_EXPERTS, D_MODEL), D_MODEL ** -0.5),
        'peer_v': nrm((DEPTH, N_EXPERTS, D_MODEL), 0.5),
    }

def reference(x_prompt, x_sample, c_prompt, c_sample, cache_ckv, cache_kpe, page_table, state_conv, state_ssm,
              w_ada, b_ada, g_mix, w_in, g_q, g_ckv, w_uk, w_uv, g_k, conv_w, conv_b, dt_bias, a_log, d_skip,
              g_ssm, w_br_a, w_br_b, w_out, g_ffn, peer_wq, peer_keys1, peer_keys2, peer_u, peer_v):
    past = page_table.shape[1] * cache_ckv.shape[2]
    pos_p = jnp.arange(x_prompt.shape[1], dtype=jnp.int32)
    pos_s = past + jnp.arange(x_sample.shape[1], dtype=jnp.int32)
    xp, xs = x_prompt, x_sample
    ckv_p, kpe_p, conv_p, ssm_p = [], [], [], []
    ckv_s, kpe_s, conv_s, ssm_s = [], [], [], []
    for l in range(DEPTH):
        lp = {'w_ada': w_ada[l], 'b_ada': b_ada[l], 'g_mix': g_mix[l], 'w_in': w_in[l], 'g_q': g_q[l],
              'g_ckv': g_ckv[l], 'conv_w': conv_w[l], 'conv_b': conv_b[l], 'dt_bias': dt_bias[l],
              'a_log': a_log[l], 'd_skip': d_skip[l], 'g_ssm': g_ssm[l], 'w_br_a': w_br_a[l], 'w_br_b': w_br_b[l],
              'w_out': w_out[l], 'g_ffn': g_ffn[l], 'peer_wq': peer_wq[l], 'peer_keys1': peer_keys1[l],
              'peer_keys2': peer_keys2[l], 'peer_u': peer_u[l], 'peer_v': peer_v[l]}
        zero_conv = jnp.zeros((xp.shape[0], CONV_W - 1, CONV_DIM), xp.dtype)
        zero_ssm = jnp.zeros((xp.shape[0], SSM_HEADS, SSM_HEADDIM, D_STATE), state_ssm.dtype)
        attend_p = functools.partial(mla_prompt, w_uk=w_uk[l], w_uv=w_uv[l], g_k=g_k[l])
        xp, a1, a2, a3, a4 = trunk_layer(xp, c_prompt, pos_p, zero_conv, zero_ssm, attend_p, lp)
        ckv_p.append(a1); kpe_p.append(a2); conv_p.append(a3); ssm_p.append(a4)
        attend_s = functools.partial(mla_sample, cache_ckv=cache_ckv[l], cache_kpe=cache_kpe[l],
                                     page_table=page_table, w_uk=w_uk[l], w_uv=w_uv[l], g_k=g_k[l])
        xs, b1, b2, b3, b4 = trunk_layer(xs, c_sample, pos_s, state_conv[l], state_ssm[l], attend_s, lp)
        ckv_s.append(b1); kpe_s.append(b2); conv_s.append(b3); ssm_s.append(b4)
    return (xp, xs, jnp.stack(ckv_p), jnp.stack(kpe_p), jnp.stack(conv_p), jnp.stack(ssm_p),
            jnp.stack(ckv_s), jnp.stack(kpe_s), jnp.stack(conv_s), jnp.stack(ssm_s))


_drawn_inputs = setup_inputs


def setup_inputs(seed=0):
    import zlib

    import numpy as np

    out = dict(_drawn_inputs(seed))
    spreads = {}
    factors = {'cache_ckv': 3.886,
     'cache_kpe': 4.429,
     'b_ada': 2.888,
     'g_q': 8.0,
     'g_ckv': 2.855,
     'g_k': 8.0,
     'conv_b': 3.793,
     'd_skip': 3.542,
     'g_ssm': 4.558,
     'g_ffn': 3.065}
    for name, (base, spread) in spreads.items():
        noise = np.random.default_rng([zlib.crc32(name.encode()), seed]).standard_normal(out[name].shape)
        drawn = base * np.exp(spread * noise) if base else spread * noise
        out[name] = __import__('jax').numpy.asarray(drawn.astype(out[name].dtype))
    for name, factor in factors.items():
        out[name] = (out[name] * factor).astype(out[name].dtype)
    return out
```

```python
from contextlib import ExitStack, contextmanager

import numpy as np

import concourse.bass as bass
from concourse import mybir

F32 = mybir.dt.float32
I32 = mybir.dt.int32
U32 = mybir.dt.uint32
ALU = mybir.AluOpType
ACT = mybir.ActivationFunctionType
X = mybir.AxisListType.X

P = 128
D = 1024
KD = D // P
TP = 512
TS = 8
T = TP + TS
TT = TP // P
H = 8
NOPE, ROPE, DV, LAT = 128, 64, 128, 512
DQK = NOPE + ROPE
KL = LAT // P
PAST, PAGE = 2048, 128
NT = PAST // PAGE
DI, HD, SH, G, N = 2048, 64, 32, 4, 128
KI = DI // P
CD = DI + 2 * G * N
KC = CD // P
CW = 4
PH, NK, DK, TK = 8, 128, 256, 16
SL = PH * TK
IN = H * DQK + LAT + ROPE + DI + CD + SH + 2 * D
EPS = 1e-6
HALF = T // 2
NEG = -1e30

SEGMENTS = ((0, 8, 0), (9, 20, -64), (29, 8, -160))
ODD_PAIR = 8
PAIRS = 37
C_Q, C_CKV, C_KPE, C_Z, C_XBC, C_DT, C_GA, C_GB = 0, 12, 16, 17, 33, 57, 58, 66


def over_pairs(eng, body):
    first, n, shift = SEGMENTS[0]
    for first, n, shift in SEGMENTS:
        if first == ODD_PAIR + 1:
            body(ODD_PAIR, ODD_PAIR % 2, ODD_PAIR // 2, None)
        with eng.Fori(0, n // 2) as i:
            for u in range(2):
                pair = i * 2 + (first + u)
                body(pair, (first + u) % 2, i + (first + u) // 2, pair * 256 + shift)


class Chain:

    def __init__(self, eng, sem):
        self.eng, self.sem, self.n = eng, sem, 0

    def __call__(self, ins):
        self.n += 1
        ins.then_inc(self.sem, 1)
        self.eng.wait_ge(self.sem, self.n)


class Mem:

    def __init__(self, nc, ctx, tag):
        self.nc, self.ctx, self.tag = nc, ctx, tag

    def sb(self, name, shape, dt=F32):
        return self.ctx.enter_context(self.nc.sbuf_tensor(f"{self.tag}_{name}", shape, dt))

    def ps(self, name, shape, dt=F32):
        return self.ctx.enter_context(self.nc.psum_tensor(f"{self.tag}_{name}", shape, dt))

    def sem(self, name):
        return self.nc.alloc_semaphore(f"{self.tag}_{name}")


@contextmanager
def own_semaphores(nc):
    before = nc.snapshot_sems()
    yield
    nc.clear_and_free_semaphores(nc.allocated_since(before))
    nc.all_engine_barrier()


def rows(t):
    return P if t < TT else TS


def constants(nc, K):
    with ExitStack() as ctx:
        m = Mem(nc, ctx, "cst")
        filled, made = m.sem("filled"), m.sem("made")
        block = ctx.enter_context(nc.Block())

        @block.gpsimd
        def _(pool):
            for tile, value in ((K["ident"], 0.0), (K["ones"], 1.0), (K["bias"], 0.0), (K["keep"], 1.0),
                                (K["swap"], 0.0), (K["last"], 0.0), (K["eps"], EPS)):
                pool.memset(tile[:], value).then_inc(filled, 1)
            pool.wait_ge(filled, 7)
            pool.affine_select(out=K["ident"][:, :], in_=K["ident"][:, :], compare_op=ALU.not_equal, fill=1.0,
                               base=0, pattern=[[-1, P]], channel_multiplier=1).then_inc(made, 1)
            pool.affine_select(out=K["bias"][:, :], in_=K["bias"][:, :], compare_op=ALU.is_ge, fill=NEG,
                               base=0, pattern=[[-1, P]], channel_multiplier=1).then_inc(made, 1)
            pool.affine_select(out=K["keep"][:, :], in_=K["keep"][:, :], compare_op=ALU.is_ge, fill=0.0,
                               base=0, pattern=[[1, P]], channel_multiplier=-1).then_inc(made, 1)
            pool.affine_select(out=K["swap"][:, :], in_=K["swap"][:, :], compare_op=ALU.not_equal, fill=-1.0,
                               base=-ROPE // 2, pattern=[[-1, ROPE]], channel_multiplier=1).then_inc(made, 1)
            pool.affine_select(out=K["last"][:, :], in_=K["last"][:, :], compare_op=ALU.not_equal, fill=1.0,
                               base=-TS, pattern=[[0, P]], channel_multiplier=1).then_inc(made, 1)
            pool.wait_ge(made, 5)
            pool.affine_select(out=K["swap"][:, :], in_=K["swap"][:, :], compare_op=ALU.not_equal, fill=1.0,
                               base=ROPE // 2, pattern=[[-1, ROPE]], channel_multiplier=1).then_inc(made, 1)
            pool.wait_ge(made, 6)


def head_channels(nc, K):
    with ExitStack() as ctx:
        m = Mem(nc, ctx, "hch")
        made = m.sem("made")
        block = ctx.enter_context(nc.Block())

        @block.gpsimd
        def _(pool):
            pool.memset(K["spread"][:, :], 1.0).then_inc(made, 1)
            pool.wait_ge(made, 1)
            pool.affine_select(out=K["spread"][:, :], in_=K["spread"][:, :], compare_op=ALU.is_ge, fill=0.0,
                               base=0, pattern=[[1, DI]], channel_multiplier=-HD).then_inc(made, 1)
            pool.wait_ge(made, 2)
            pool.affine_select(out=K["spread"][:, :], in_=K["spread"][:, :], compare_op=ALU.is_ge, fill=0.0,
                               base=HD - 1, pattern=[[-1, DI]], channel_multiplier=HD)


def conditioning(nc, A, K):
    NG = 6 * D // 512
    with ExitStack() as ctx:
        m = Mem(nc, ctx, "ada")
        c_rows, cT = m.sb("c_rows", [TS + 1, D]), m.sb("cT", [P, KD, TS + 1])
        bias = m.sb("bias", [TS + 1, 6 * D])
        w = m.sb("w", [P, 2, KD, 512])
        psT, psA = m.ps("psT", [P, KD, TS + 1]), m.ps("psA", [TS + 1, 2, 512])
        c_in, bias_in = m.sem("c_in"), m.sem("bias_in")
        w_in = [m.sem(f"w_in{b}") for b in range(2)]
        turned, cT_ready = m.sem("turned"), m.sem("cT_ready")
        summed = [m.sem(f"summed{b}") for b in range(2)]
        added = [m.sem(f"added{b}") for b in range(2)]
        block = ctx.enter_context(nc.Block())
        w_view = A["w_ada"].rearrange("l (k p) n -> p (l k) n", p=P)

        @block.sync
        def _(sp):
            sp.dma_start(c_rows[0:TS, :], A["c_sample"]).then_inc(c_in, 16)
            sp.dma_start(c_rows[TS:TS + 1, :], A["c_prompt"]).then_inc(c_in, 16)
            sp.dma_start(bias[:, :], A["b_ada"].to_broadcast([TS + 1, 6 * D])).then_inc(bias_in, 16)
            with sp.Fori(0, NG // 2) as i:
                for b in range(2):
                    sp.wait_ge(summed[b], i)
                    sp.dma_start(w[:, b], w_view[:, :, bass.ds(i * 1024 + b * 512, 512)]).then_inc(w_in[b], 16)

        @block.tensor
        def _(pe):
            pe.wait_ge(c_in, 32)
            for k in range(KD):
                last = pe.transpose(psT[:, k, :], c_rows[:, k * P:(k + 1) * P], K["ident"][0:TS + 1, 0:TS + 1])
            last.then_inc(turned, 1)
            pe.wait_ge(cT_ready, 1)
            with pe.Fori(0, NG // 2) as i:
                for b in range(2):
                    pe.wait_ge(w_in[b], i * 16 + 16)
                    pe.wait_ge(added[b], i)
                    for k in range(KD):
                        last = pe.matmul(psA[:, b, :], cT[:, k, :], w[:, b, k, :], start=(k == 0), stop=(k == KD - 1))
                    last.then_inc(summed[b], 1)

        @block.vector
        def _(dve):
            dve.wait_ge(turned, 1)
            dve.tensor_copy(cT[:, :, :], psT[:, :, :]).then_inc(cT_ready, 1)
            dve.wait_ge(bias_in, 16)
            with dve.Fori(0, NG // 2) as i:
                for b in range(2):
                    dve.wait_ge(summed[b], i + 1)
                    at = bass.ds(i * 1024 + b * 512, 512)
                    dve.tensor_tensor(K["ada"][:, at], psA[:, b, :], bias[:, at], ALU.add).then_inc(added[b], 1)


def modulated(nc, K, tag, load, x, gain, shift_at, scale_at, out, outT, prompt=True, samples=True):
    NP = TT if prompt else 0
    tiles = [P] * NP + [TS] * samples
    NA = len(tiles)
    with ExitStack() as ctx:
        m = Mem(nc, ctx, tag)
        gain_bc = m.sb("gain", [P, D])
        mul_p, add_p, mul_s = m.sb("mul_p", [P, D]), m.sb("add_p", [P, D]), m.sb("mul_s", [TS, D])
        squares = m.sb("squares", [P, D])
        ss, ms, rms, rstd = (m.sb(n, [P, NA]) for n in ("ss", "ms", "rms", "rstd"))
        psB = m.ps("psB", [P, 4, 512])
        psT = m.ps("psT", [P, 2, 4, P])
        x_in, gain_in, spread = m.sem("x_in"), m.sem("gain_in"), m.sem("spread")
        summed, meaned, rooted = m.sem("summed"), m.sem("meaned"), m.sem("rooted")
        normed, turned, copied, chain = m.sem("normed"), m.sem("turned"), m.sem("copied"), m.sem("chain")
        stats = [(P, slice(0, NP))] * prompt + [(TS, slice(NP, NA))] * samples
        block = ctx.enter_context(nc.Block())

        @block.sync
        def _(sp):
            sp.dma_start(gain_bc[:, :], gain.to_broadcast([P, D])).then_inc(gain_in, 16)
            for dst, src in load:
                sp.dma_start(dst, src).then_inc(x_in, 16)

        @block.scalar
        def _(act):
            act.wait_ge(x_in, 16 * len(load)) if load else None
            for t, n in enumerate(tiles):
                if t:
                    act.wait_ge(summed, t)
                act.activation(squares[0:n, :], x[0:n, t, :], ACT.Square, accum_out=ss[0:n, t:t + 1]).then_inc(summed, 1)
            act.wait_ge(meaned, len(stats))
            for n, cols in stats:
                act.activation(rms[0:n, cols], ms[0:n, cols], ACT.Sqrt).then_inc(rooted, 1)

        @block.tensor
        def _(pe):
            for j, at in enumerate((shift_at, scale_at)):
                for c in range(2):
                    last = pe.matmul(psB[:, 2 * j + c, :], K["last"][:, :], K["ada"][:, at + c * 512:at + (c + 1) * 512],
                                     start=True, stop=True)
            last.then_inc(spread, 1)
            for t, n in enumerate(tiles):
                pe.wait_ge(normed, t + 1)
                for c in range(2):
                    j = 2 * t + c
                    if j >= 2:
                        pe.wait_ge(copied, j - 1)
                    for k in range(4):
                        last = pe.transpose(psT[:, j % 2, k, 0:n], out[0:n, t, (4 * c + k) * P:(4 * c + k + 1) * P],
                                            K["ident"][0:n, 0:n])
                    last.then_inc(turned, 1)

        @block.vector
        def _(dve):
            then = Chain(dve, chain)
            dve.wait_ge(gain_in, 16)
            dve.wait_ge(spread, 1)
            dve.tensor_copy(add_p[:, :].rearrange("p (c n) -> p c n", c=2), psB[:, 0:2, :])
            dve.scalar_tensor_tensor(mul_p[:, :].rearrange("p (c n) -> p c n", c=2), psB[:, 2:4, :], 1.0,
                                     gain_bc[:, :].rearrange("p (c n) -> p c n", c=2), ALU.add, ALU.mult)
            dve.scalar_tensor_tensor(mul_s[:, :], K["ada"][0:TS, scale_at:scale_at + D], 1.0, gain_bc[0:TS, :],
                                     ALU.add, ALU.mult)
            dve.wait_ge(summed, NA)
            for n, cols in stats:
                dve.tensor_scalar(ms[0:n, cols], ss[0:n, cols], 1.0 / D, EPS, ALU.mult, ALU.add).then_inc(meaned, 1)
            dve.wait_ge(rooted, len(stats))
            for n, cols in stats:
                then(dve.reciprocal(rstd[0:n, cols], rms[0:n, cols]))

            def copy(j):
                t, c = j // 2, j % 2
                n = tiles[t]
                dve.wait_ge(turned, j + 1)
                dve.tensor_copy(outT[:, 4 * c:4 * c + 4, t * P:t * P + n], psT[:, j % 2, :, 0:n]).then_inc(copied, 1)

            for t, n in enumerate(tiles):
                mul, add = (mul_p, add_p[:, :]) if t < NP else (mul_s, K["ada"][0:TS, shift_at:shift_at + D])
                then(dve.scalar_tensor_tensor(out[0:n, t, :], x[0:n, t, :], rstd[0:n, t:t + 1], mul[0:n, :],
                                              ALU.mult, ALU.mult))
                dve.tensor_tensor(out[0:n, t, :], out[0:n, t, :], add, ALU.add).then_inc(normed, 1)
                if t:
                    copy(2 * t - 2)
                    copy(2 * t - 1)
            copy(2 * NA - 2)
            copy(2 * NA - 1)


def projection(nc, A, hT, proj):
    with ExitStack() as ctx:
        m = Mem(nc, ctx, "prj")
        w, out = m.sb("w", [P, 2, KD, 256]), m.sb("out", [P, 2, 2, 2, HALF])
        ps = m.ps("ps", [P, 2, 2, 2, 512])
        w_in, summed, copied, stored = ([m.sem(f"{n}{b}") for b in range(2)]
                                        for n in ("w_in", "summed", "copied", "stored"))
        block = ctx.enter_context(nc.Block())
        w_view = A["w_in"].rearrange("l (k p) n -> p (l k) n", p=P)
        proj_view = proj.rearrange("c p t -> p c t")

        @block.sync
        def _(sp):
            def load(pair, b, used, col):
                sp.wait_ge(summed[b], used)
                if col is None:
                    for half, at in enumerate((2048, 2112)):
                        sp.dma_start(w[:, b, :, half * P:(half + 1) * P], w_view[:, :, at:at + P]).then_inc(w_in[b], 16)
                else:
                    for half in range(2):
                        sp.dma_start(w[:, b, :, half * P:(half + 1) * P], w_view[:, :, bass.ds(col + half * P, P)]).then_inc(w_in[b], 16)
            over_pairs(sp, load)

        @block.tensor
        def _(pe):
            def product(pair, b, used, col):
                pe.wait_ge(w_in[b], used * 32 + 32)
                pe.wait_ge(copied[b], used)
                for c in range(2):
                    for k in range(KD):
                        for s in range(2):
                            last = pe.matmul(ps[:, b, c, s, 0:HALF], w[:, b, k, c * P:(c + 1) * P],
                                             hT[:, k, s * HALF:(s + 1) * HALF], start=(k == 0), stop=(k == KD - 1))
                last.then_inc(summed[b], 1)
            over_pairs(pe, product)

        @block.vector
        def _(dve):
            def copy(pair, b, used, col):
                dve.wait_ge(stored[b], used * 16)
                dve.wait_ge(summed[b], used + 1)
                dve.tensor_copy(out[:, b], ps[:, b, :, :, 0:HALF]).then_inc(copied[b], 1)
            over_pairs(dve, copy)

        @block.scalar
        def _(act):
            def store(pair, b, used, col):
                act.wait_ge(copied[b], used + 1)
                act.dma_start(proj_view[:, bass.ds(pair * 2, 2), :],
                              out[:, b].rearrange("p c s t -> p c (s t)")).then_inc(stored[b], 16)
            over_pairs(act, store)
            for b in range(2):
                act.wait_ge(stored[b], 16 * ((PAIRS + 1 - b) // 2))


SCALE = float(DQK) ** -0.5


class Steps:

    def __init__(self, eng, sem, n, turn):
        self.eng, self.sem, self.size, self.base, self.n = eng, sem, n, turn * n, 0

    def __call__(self, ins):
        self.n += 1
        ins.then_inc(self.sem, 1)
        self.eng.wait_ge(self.sem, self.base + self.n)

    def full(self):
        assert self.n == self.size, self.n


def latents(nc, A, K, M, proj, outs):
    with ExitStack() as ctx:
        m = Mem(nc, ctx, "lat")
        raw, sq = m.sb("raw", [P, KL, T]), m.sb("sq", [P, KL, T])
        rstd, turned = m.sb("rstd", [P, 2, HALF]), m.sb("turned", [ROPE, 2, HALF])
        gain = m.sb("gain", [P, KL])
        by_token, kpe_by_token = m.sb("by_token", [P, 2, LAT]), m.sb("kpe_by_token", [P, 2, ROPE])
        psN, psR = m.ps("psN", [P, 2, 512]), m.ps("psR", [ROPE, 2, 512])
        psT, psK = m.ps("psT", [P, 2, 512]), m.ps("psK", [P, 2, 512])
        raw_in, squared, summed, swapped = m.sem("raw_in"), m.sem("squared"), m.sem("summed"), m.sem("swapped")
        rooted, ready, chain = m.sem("rooted"), m.sem("ready"), m.sem("chain")
        moved, copied = m.sem("moved"), m.sem("copied")
        stored = [m.sem(f"stored{b}") for b in range(2)]
        block = ctx.enter_context(nc.Block())
        flat = proj.rearrange("c p t -> (c p) t")
        halves = lambda ap: ap.rearrange("p (s t) -> p s t", s=2)

        @block.sync
        def _(sp):
            sp.dma_start(raw[:, :, :], proj[C_CKV:C_CKV + KL].rearrange("c p t -> p c t")).then_inc(raw_in, 16)
            sp.dma_start(M["kpeT"][:, :], proj[C_KPE, 0:ROPE, :]).then_inc(raw_in, 16)
            sp.dma_start(gain[:, :], A["g_ckv"].rearrange("l (k p) -> p (l k)", p=P), allow_slow_non_contiguous=True).then_inc(raw_in, 16)
            sp.dma_start(M["cos"][:, :], A["rope_cos"]).then_inc(raw_in, 16)
            sp.dma_start(M["sin"][:, :], A["rope_sin"]).then_inc(raw_in, 16)
            for t in range(TT + 1):
                n, b = rows(t), t % 2
                sp.wait_ge(copied, 2 * t + 2)
                where = (outs["ckv_p"][0, 0, t * P:t * P + n, :], outs["kpe_p"][0, 0, t * P:t * P + n, :]) if t < TT else \
                    (outs["ckv_s"][0, :, 0, :], outs["kpe_s"][0, :, 0, :])
                sp.dma_start(where[0], by_token[0:n, b, :]).then_inc(stored[b], 16)
                sp.dma_start(where[1], kpe_by_token[0:n, b, :]).then_inc(stored[b], 16)
            sp.wait_ge(stored[0], 96)
            sp.wait_ge(stored[1], 64)

        @block.scalar
        def _(act):
            act.wait_ge(raw_in, 80)
            act.activation(sq[:, :, :], raw[:, :, :], ACT.Square).then_inc(squared, 1)
            act.wait_ge(summed, 1)
            act.activation(rstd[:, :, :], psN[:, :, 0:HALF], ACT.Sqrt, scale=1.0 / LAT, bias=K["eps"][:, :]).then_inc(rooted, 1)
            act.wait_ge(ready, 1)
            act.activation(M["kpe_sq"][:, :], M["kpeT"][:, :], ACT.Square).then_inc(rooted, 1)

        @block.tensor
        def _(pe):
            pe.wait_ge(raw_in, 80)
            for s in range(2):
                last = pe.matmul(psR[:, s, 0:HALF], K["swap"][:, :], M["kpeT"][:, s * HALF:(s + 1) * HALF], start=True, stop=True)
            last.then_inc(swapped, 1)
            pe.wait_ge(squared, 1)
            for s in range(2):
                for k in range(KL):
                    last = pe.matmul(psN[:, s, 0:HALF], K["ones"][:, :], sq[:, k, s * HALF:(s + 1) * HALF],
                                     start=(k == 0), stop=(k == KL - 1))
            last.then_inc(summed, 1)
            pe.wait_ge(ready, 2)
            for t in range(TT + 1):
                n, b = rows(t), t % 2
                if t >= 2:
                    pe.wait_ge(copied, 2 * t - 2)
                for k in range(KL):
                    pe.transpose(psT[0:n, b, k * P:(k + 1) * P], M["ckvT"][:, k, t * P:t * P + n], K["ident"][:, :])
                pe.transpose(psK[0:n, b, 0:ROPE], M["kpeT"][:, t * P:t * P + n], K["ident"][0:ROPE, 0:ROPE]).then_inc(moved, 1)

        @block.vector
        def _(dve):
            then = Chain(dve, chain)
            dve.wait_ge(raw_in, 80)
            dve.wait_ge(swapped, 1)
            dve.tensor_tensor(turned[:, :, :], psR[:, :, 0:HALF], halves(M["sin"][:, :]), ALU.mult)
            then(dve.tensor_tensor(M["kpeT"][:, :], M["kpeT"][:, :], M["cos"][:, :], ALU.mult))
            dve.tensor_tensor(halves(M["kpeT"][:, :]), halves(M["kpeT"][:, :]), turned[:, :, :], ALU.add).then_inc(ready, 1)
            dve.wait_ge(rooted, 1)
            then(dve.reciprocal(rstd[:, :, :], rstd[:, :, :]))
            for k in range(KL):
                last = dve.scalar_tensor_tensor(halves(M["ckvT"][:, k, :]), halves(raw[:, k, :]), gain[:, k:k + 1],
                                                rstd[:, :, :], ALU.mult, ALU.mult)
            last.then_inc(ready, 1)
            for t in range(TT + 1):
                n, b = rows(t), t % 2
                dve.wait_ge(moved, t + 1)
                if t >= 2:
                    dve.wait_ge(stored[b], 32 * (t // 2))
                dve.tensor_copy(by_token[0:n, b, :], psT[0:n, b, :]).then_inc(copied, 1)
                dve.tensor_copy(kpe_by_token[0:n, b, :], psK[0:n, b, 0:ROPE]).then_inc(copied, 1)
                if t == TT:
                    dve.wait_ge(copied, 2 * t + 2)
                    dve.tensor_copy(M["ckv_s"][:, :], by_token[0:n, b, :])


def prompt_attention(nc, A, K, M, proj, oT):
    with ExitStack() as ctx:
        m = Mem(nc, ctx, "att")
        q_n, q_r = m.sb("q_n", [P, 2, T]), m.sb("q_r", [ROPE, 2, T])
        w_uk, w_uv = m.sb("w_uk", [P, 2, KL, NOPE]), m.sb("w_uv", [P, 2, KL, DV])
        turned, sq_n, sq_r = m.sb("turned", [ROPE, T]), m.sb("sq_n", [P, T]), m.sb("sq_r", [ROPE, T])
        sq_k = m.sb("sq_k", [P, TP])
        root_q, root_k = m.sb("root_q", [P, T]), m.sb("root_k", [P, TP])
        k_n, k_r, v = m.sb("k_n", [P, TP]), m.sb("k_r", [ROPE, TP]), m.sb("v", [P, TT, DV])
        probs, probsT = m.sb("probs", [P, TT, TP]), m.sb("probsT", [P, 2, TT, P])
        top, shift, total, share = (m.sb(n, [P, TT]) for n in ("top", "shift", "total", "share"))
        bank = [m.ps(f"bank{b}", [P, 512]) for b in range(8)]
        psV, psT, psO = bank[4], bank[5:7], bank[7]
        gq_n, gq_r, gk_n, gk_r = m.sb("gq_n", [P, 1]), m.sb("gq_r", [ROPE, 1]), m.sb("gk_n", [P, 1]), m.sb("gk_r", [ROPE, 1])
        gains_in, chain = m.sem("gains_in"), m.sem("chain")
        head_in = [m.sem(f"head_in{b}") for b in range(2)]
        head_done = [m.sem(f"head_done{b}") for b in range(2)]
        (swapped, keyed, valued, q_sq, r_roped, r_sq, k_sq, q_summed, k_summed, q_rooted, k_rooted, prepared, v_copied,
         scored, shifted, exped, shared, turned_p, copied_p, weighed) = (m.sem(n) for n in (
             "swapped", "keyed", "valued", "q_sq", "r_roped", "r_sq", "k_sq", "q_summed", "k_summed", "q_rooted",
             "k_rooted", "prepared", "v_copied", "scored", "shifted", "exped", "shared", "turned_p", "copied_p", "weighed"))
        block = ctx.enter_context(nc.Block())
        q_view = proj.rearrange("c p t -> (c p) t")

        def heads(eng, body):
            with eng.Fori(0, H // 2) as i:
                for b in range(2):
                    body(i, b, i * 2 + b)

        @block.sync
        def _(sp):
            for tile, src in ((gq_n, A["g_q"][0, 0:NOPE]), (gq_r, A["g_q"][0, NOPE:DQK]),
                              (gk_n, A["g_k"][0, 0:NOPE]), (gk_r, A["g_k"][0, NOPE:DQK])):
                sp.dma_start(tile[:, :], src.rearrange("(p a) -> p a", a=1)).then_inc(gains_in, 16)

            def load(i, b, h):
                sp.wait_ge(head_done[b], i)
                sp.dma_start(q_n[:, b, :], q_view[bass.ds(h * DQK, NOPE), :]).then_inc(head_in[b], 16)
                sp.dma_start(q_r[:, b, :], q_view[bass.ds(h * DQK + NOPE, ROPE), :]).then_inc(head_in[b], 16)
                sp.dma_start(w_uk[:, b], A["w_uk"].rearrange("l (k p) h d -> p (l k) (h d)", p=P)[:, :, bass.ds(h * NOPE, NOPE)]).then_inc(head_in[b], 16)
                sp.dma_start(w_uv[:, b], A["w_uv"].rearrange("l (k p) h d -> p (l k) (h d)", p=P)[:, :, bass.ds(h * DV, DV)]).then_inc(head_in[b], 16)
            heads(sp, load)

        @block.tensor
        def _(pe):
            def head(i, b, h):
                pe.wait_ge(head_in[b], i * 64 + 64)
                pe.wait_ge(exped, h * TT)
                for k in range(KL):
                    last = pe.matmul(bank[2][:, :], w_uk[:, b, k, :], M["ckvT"][:, k, 0:TP], start=(k == 0), stop=(k == KL - 1))
                last.then_inc(keyed, 1)
                for s in range(2):
                    last = pe.matmul(bank[s][0:ROPE, 0:HALF], K["swap"][:, :], q_r[:, b, s * HALF:(s + 1) * HALF], start=True, stop=True)
                last.then_inc(swapped, 1)
                pe.wait_ge(v_copied, h)
                for t in range(TT):
                    for k in range(KL):
                        last = pe.matmul(psV[:, t * DV:(t + 1) * DV], M["ckvT"][:, k, t * P:(t + 1) * P], w_uv[:, b, k, :],
                                         start=(k == 0), stop=(k == KL - 1))
                last.then_inc(valued, 1)
                pe.wait_ge(k_sq, h + 1)
                pe.matmul(bank[3][:, :], K["ones"][:, :], sq_k[:, :], start=True, stop=False)
                pe.matmul(bank[3][:, :], K["ones"][0:ROPE, :], M["kpe_sq"][:, 0:TP], start=False, stop=True).then_inc(k_summed, 1)
                pe.wait_ge(q_sq, h + 1)
                pe.wait_ge(r_sq, h + 1)
                for s in range(2):
                    pe.matmul(bank[s][:, 0:HALF], K["ones"][:, :], sq_n[:, s * HALF:(s + 1) * HALF], start=True, stop=False)
                    last = pe.matmul(bank[s][:, 0:HALF], K["ones"][0:ROPE, :], sq_r[:, s * HALF:(s + 1) * HALF], start=False, stop=True)
                last.then_inc(q_summed, 1)
                pe.wait_ge(prepared, h + 1)
                for q in range(TT):
                    w = (q + 1) * P
                    pe.matmul(bank[q][:, 0:w], q_n[:, b, q * P:w], k_n[:, 0:w], start=True, stop=False)
                    pe.matmul(bank[q][:, 0:w], q_r[:, b, q * P:w], k_r[:, 0:w], start=False, stop=True).then_inc(scored, 1)

                def turn(q):
                    pe.wait_ge(shared, h * TT + (q + 1))
                    if q >= 2:
                        pe.wait_ge(copied_p, h * TT + (q - 1))
                    for k in range(q + 1):
                        last = pe.transpose(psT[q % 2][:, k * P:(k + 1) * P], probs[:, q, k * P:(k + 1) * P], K["ident"][:, :])
                    last.then_inc(turned_p, 1)

                def weigh(q):
                    pe.wait_ge(copied_p, h * TT + (q + 1))
                    if q == 0:
                        pe.wait_ge(v_copied, h + 1)
                        pe.wait_ge(head_done[1 - b], i + b)
                    for k in range(q + 1):
                        last = pe.matmul(psO[:, q * P:(q + 1) * P], v[:, k, :], probsT[:, q % 2, k, :], start=(k == 0), stop=(k == q))
                    last.then_inc(weighed, 1)

                turn(0)
                turn(1)
                weigh(0)
                turn(2)
                weigh(1)
                turn(3)
                weigh(2)
                weigh(3)
            heads(pe, head)

        @block.scalar
        def _(act):
            def head(i, b, h):
                act.wait_ge(head_in[b], i * 64 + 64)
                act.activation(sq_n[:, :], q_n[:, b, :], ACT.Square).then_inc(q_sq, 1)
                act.wait_ge(keyed, h + 1)
                act.activation(sq_k[:, :], bank[2][:, :], ACT.Square).then_inc(k_sq, 1)
                act.wait_ge(r_roped, h + 1)
                act.activation(sq_r[:, :], q_r[:, b, :], ACT.Square).then_inc(r_sq, 1)
                act.wait_ge(k_summed, h + 1)
                act.activation(root_k[:, :], bank[3][:, :], ACT.Sqrt, scale=1.0 / DQK, bias=K["eps"][:, :]).then_inc(k_rooted, 1)
                act.wait_ge(q_summed, h + 1)
                for s in range(2):
                    act.activation(root_q[:, s * HALF:(s + 1) * HALF], bank[s][:, 0:HALF], ACT.Sqrt, scale=1.0 / DQK,
                                   bias=K["eps"][:, :]).then_inc(q_rooted, 1)
                act.wait_ge(valued, h + 1)
                act.activation(v[:, :, :].rearrange("p t d -> p (t d)"), psV[:, :], ACT.Copy).then_inc(v_copied, 1)
                for q in range(TT):
                    w = (q + 1) * P
                    act.wait_ge(shifted, h * TT + (q + 1))
                    act.activation(probs[:, q, 0:w], bank[q][:, 0:w], ACT.Exp, bias=shift[:, q:q + 1], scale=SCALE,
                                   accum_out=total[:, q:q + 1]).then_inc(exped, 1)
                for q in range(TT):
                    w = (q + 1) * P
                    act.wait_ge(turned_p, h * TT + (q + 1))
                    if q >= 2:
                        act.wait_ge(weighed, h * TT + (q - 1))
                    act.activation(probsT[:, q % 2, 0:q + 1, :].rearrange("p k q -> p (k q)"), psT[q % 2][:, 0:w], ACT.Copy).then_inc(copied_p, 1)
            heads(act, head)

        @block.vector
        def _(dve):
            dve.wait_ge(gains_in, 64)

            def head(i, b, h):
                then = Steps(dve, chain, 15, h)
                dve.wait_ge(head_in[b], i * 64 + 64)
                dve.wait_ge(swapped, h + 1)
                for s in range(2):
                    dve.tensor_tensor(turned[:, s * HALF:(s + 1) * HALF], bank[s][0:ROPE, 0:HALF], M["sin"][:, s * HALF:(s + 1) * HALF], ALU.mult)
                then(dve.tensor_tensor(q_r[:, b, :], q_r[:, b, :], M["cos"][:, :], ALU.mult))
                then(dve.tensor_tensor(q_r[:, b, :], q_r[:, b, :], turned[:, :], ALU.add))
                dve.sem_inc(r_roped, 1)
                dve.wait_ge(k_rooted, h + 1)
                then(dve.reciprocal(root_k[:, :], root_k[:, :]))
                dve.scalar_tensor_tensor(k_n[:, :], bank[2][:, :], gk_n[:, :], root_k[:, :], ALU.mult, ALU.mult)
                dve.scalar_tensor_tensor(k_r[:, :], M["kpeT"][:, 0:TP], gk_r[:, :], root_k[0:ROPE, :], ALU.mult, ALU.mult)
                dve.wait_ge(q_rooted, h * 2 + 2)
                then(dve.reciprocal(root_q[:, :], root_q[:, :]))
                dve.scalar_tensor_tensor(q_n[:, b, :], q_n[:, b, :], gq_n[:, :], root_q[:, :], ALU.mult, ALU.mult)
                then(dve.scalar_tensor_tensor(q_r[:, b, :], q_r[:, b, :], gq_r[:, :], root_q[0:ROPE, :], ALU.mult, ALU.mult))
                dve.sem_inc(prepared, 1)
                dve.tensor_copy(M["qs_n"][:, bass.ds(h * TS, TS)], q_n[:, b, TP:T])
                dve.tensor_copy(M["qs_r"][:, bass.ds(h * TS, TS)], q_r[:, b, TP:T])
                for q in range(TT):
                    w = (q + 1) * P
                    dve.wait_ge(scored, h * TT + (q + 1))
                    then(dve.tensor_tensor(bank[q][:, w - P:w], bank[q][:, w - P:w], K["bias"][:, :], ALU.add))
                    then(dve.tensor_reduce(top[:, q:q + 1], bank[q][:, 0:w], X, ALU.max))
                    dve.tensor_scalar(shift[:, q:q + 1], top[:, q:q + 1], -SCALE, None, ALU.mult).then_inc(shifted, 1)
                dve.wait_ge(exped, h * TT + TT)
                then(dve.reciprocal(share[:, :], total[:, :]))
                for q in range(TT):
                    w = (q + 1) * P
                    dve.tensor_scalar(probs[:, q, 0:w], probs[:, q, 0:w], share[:, q:q + 1], None, ALU.mult).then_inc(shared, 1)
                dve.wait_ge(weighed, h * TT + TT)
                then(dve.tensor_copy(oT[:, bass.ds(h * T, TP)], psO[:, :]))
                dve.sem_inc(head_done[b], 1)
                then.full()
            heads(dve, head)


XB, XC_ = KI, KI + G
NR = TS * (CW - 1)
LAST = CW - 1 + TS


def convolution(nc, A, K, S, proj, outs):
    with ExitStack() as ctx:
        m = Mem(nc, ctx, "cnv")
        NB = 3
        held = m.sb("held", [NR + CW + 1, CD])
        params = m.sb("params", [P, KC, NR + CW + 1])
        raw, y = m.sb("raw", [P, NB, CW - 1 + T]), m.sb("y", [P, NB, T])
        rows_out = m.sb("rows_out", [LAST, CD])
        psP, psR = m.ps("psP", [P, 2, 512]), m.ps("psR", [LAST, 2, 512])
        held_in, padded, turned, placed = m.sem("held_in"), m.sem("padded"), m.sem("turned"), m.sem("placed")
        raw_in = [m.sem(f"raw_in{b}") for b in range(NB)]
        began, summed, done, chain = m.sem("began"), m.sem("summed"), m.sem("done"), m.sem("chain")
        rows_turned, rows_copied, stored = m.sem("rows_turned"), m.sem("rows_copied"), m.sem("stored")
        block = ctx.enter_context(nc.Block())
        PC = KC // 2

        @block.sync
        def _(sp):
            sp.dma_start(held[0:NR, :], A["state_conv"].rearrange("l b w c -> (l b w) c")).then_inc(held_in, 16)
            sp.dma_start(held[NR:NR + CW, :], A["conv_w"].rearrange("l w c -> (l w) c")).then_inc(held_in, 16)
            sp.dma_start(held[NR + CW:NR + CW + 1, :], A["conv_b"]).then_inc(held_in, 16)
            for c in range(KC):
                if c >= NB:
                    sp.wait_ge(summed, c - NB + 1)
                    sp.wait_ge(rows_turned, c - NB + 1)
                sp.dma_start(raw[:, c % NB, CW - 1:], proj[C_XBC + c]).then_inc(raw_in[c % NB], 16)
            sp.dma_start(outs["conv_s"][0, :, 0:CW - 2, :], A["state_conv"][0, :, 1:CW - 1, :]).then_inc(stored, 16)
            sp.wait_ge(rows_copied, KC // 4)
            sp.dma_start(outs["conv_p"][0, 0], rows_out[0:CW - 1, :]).then_inc(stored, 16)
            sp.dma_start(outs["conv_s"][0, :, CW - 2, :], rows_out[CW - 1:LAST, :]).then_inc(stored, 16)
            sp.wait_ge(stored, 48)

        @block.gpsimd
        def _(pool):
            pool.memset(raw[:, :, 0:CW - 1], 0.0).then_inc(padded, 1)

        @block.tensor
        def _(pe):
            pe.wait_ge(held_in, 48)
            n = NR + CW + 1
            for c in range(KC):
                last = pe.transpose(psP[:, c // PC, (c % PC) * n:(c % PC) * n + n], held[:, c * P:(c + 1) * P], K["ident"][0:n, 0:n])
            last.then_inc(turned, 1)
            for c in range(KC):
                pe.wait_ge(raw_in[c % NB], 16 * (c // NB + 1))
                if c >= 8:
                    pe.wait_ge(rows_copied, c // 4 - 1)
                pe.transpose(psR[:, c // 4 % 2, (c % 4) * P:(c % 4 + 1) * P], raw[:, c % NB, TP:], K["ident"][:, :]).then_inc(rows_turned, 1)

        @block.scalar
        def _(act):
            act.wait_ge(placed, 1)
            act.wait_ge(padded, 1)
            b0 = NR + CW
            for c in range(KC + 1):
                if c < KC:
                    s = c % NB
                    act.wait_ge(raw_in[s], 16 * (c // NB + 1))
                    if c >= NB:
                        act.wait_ge(done, c - NB + 1)
                    act.activation(y[:, s, 0:TP], raw[:, s, 0:TP], ACT.Identity, scale=params[:, c, NR:NR + 1],
                                   bias=params[:, c, b0:b0 + 1])
                    act.activation(y[:, s, TP:], params[:, c, 0:NR:CW - 1], ACT.Identity, scale=params[:, c, NR:NR + 1],
                                   bias=params[:, c, b0:b0 + 1]).then_inc(began, 1)
                if c:
                    act.wait_ge(summed, c)
                    act.activation(S["x"][:, c - 1, :], y[:, (c - 1) % NB, :], ACT.Silu).then_inc(done, 1)

        @block.vector
        def _(dve):
            then = Chain(dve, chain)
            dve.wait_ge(turned, 1)
            n = NR + CW + 1
            dve.tensor_copy(params[:, :, :].rearrange("p (h c) n -> p h (c n)", h=2), psP[:, :, 0:PC * n]).then_inc(placed, 1)
            dve.wait_ge(placed, 1)
            dve.wait_ge(padded, 1)
            for c in range(KC):
                s = c % NB
                dve.wait_ge(raw_in[s], 16 * (c // NB + 1))
                dve.wait_ge(began, c + 1)
                for w in range(1, CW):
                    tap = params[:, c, NR + w:NR + w + 1]
                    p = dve.scalar_tensor_tensor(y[:, s, 0:TP], raw[:, s, w:w + TP], tap, y[:, s, 0:TP], ALU.mult, ALU.add)
                    held_w = params[:, c, w:NR:CW - 1] if w < CW - 1 else raw[:, s, CW - 1 + TP:]
                    q = dve.scalar_tensor_tensor(y[:, s, TP:], held_w, tap, y[:, s, TP:], ALU.mult, ALU.add)
                    if w < CW - 1:
                        then(q)
                q.then_inc(summed, 1)
                if c % 4 == 3:
                    g = c // 4
                    dve.wait_ge(rows_turned, c + 1)
                    dve.tensor_copy(rows_out[:, g * 512:(g + 1) * 512], psR[:, g % 2, :]).then_inc(rows_copied, 1)


def time_steps(nc, A, K, S, proj, acs_dram):
    ORDER = 9
    with ExitStack() as ctx:
        m = Mem(nc, ctx, "dts")
        x, e, s, s2, p = (m.sb(n, [SH, T]) for n in ("x", "e", "s", "s2", "p"))
        bias, a_log = m.sb("bias", [SH, 1]), m.sb("a_log", [SH, 1])
        psT = m.ps("psT", [P, 2, TT, SH])
        loaded, biased, magnitude, exped, a_made, ready = (m.sem(n) for n in ("loaded", "biased", "magnitude", "exped", "a_made", "ready"))
        turned, stored, chain = m.sem("turned"), m.sem("stored"), m.sem("chain")
        block = ctx.enter_context(nc.Block())

        @block.sync
        def _(sp):
            sp.dma_start(x[:, :], proj[C_DT, 0:SH, :]).then_inc(loaded, 16)
            sp.dma_start(bias[:, :], A["dt_bias"].rearrange("l h -> h l")).then_inc(loaded, 16)
            sp.dma_start(a_log[:, :], A["a_log"].rearrange("l h -> h l")).then_inc(loaded, 16)
            sp.wait_ge(ready, 1)
            sp.dma_start(acs_dram, S["acs"][:, 0:TP]).then_inc(stored, 16)
            sp.wait_ge(stored, 16)

        @block.scalar
        def _(act):
            act.wait_ge(loaded, 48)
            act.activation(S["a"][:, :], a_log[:, :], ACT.Exp).then_inc(a_made, 1)
            act.wait_ge(biased, 1)
            act.activation(e[:, :], x[:, :], ACT.Abs).then_inc(magnitude, 1)
            act.wait_ge(magnitude, 1)
            act.activation(e[:, :], e[:, :], ACT.Exp, scale=-1.0).then_inc(exped, 1)
            act.wait_ge(ready, 1)
            act.activation(S["decay_s"][:, :], S["acs"][:, TP:], ACT.Exp).then_inc(exped, 1)

        @block.tensor
        def _(pe):
            pe.wait_ge(ready, 1)
            for c in range(TT):
                pe.transpose(psT[:, 0, c, :], S["dt"][:, c * P:(c + 1) * P], K["ident"][0:SH, 0:SH])
                last = pe.transpose(psT[:, 1, c, :], S["acs"][:, c * P:(c + 1) * P], K["ident"][0:SH, 0:SH])
            last.then_inc(turned, 1)

        @block.vector
        def _(dve):
            then = Chain(dve, chain)
            dve.wait_ge(loaded, 48)
            dve.tensor_scalar(x[:, :], x[:, :], bias[:, :], None, ALU.add).then_inc(biased, 1)
            dve.wait_ge(exped, 1)
            then(dve.tensor_scalar(s[:, :], e[:, :], 2.0, None, ALU.add))
            then(dve.reciprocal(s[:, :], s[:, :]))
            then(dve.tensor_tensor(s[:, :], s[:, :], e[:, :], ALU.mult))
            then(dve.tensor_tensor(s2[:, :], s[:, :], s[:, :], ALU.mult))
            then(dve.tensor_scalar(p[:, :], s2[:, :], 2.0 / (2 * ORDER + 1), None, ALU.mult))
            for k in range(ORDER - 1, 0, -1):
                then(dve.scalar_tensor_tensor(p[:, :], p[:, :], 2.0 / (2 * k + 1), s2[:, :], ALU.add, ALU.mult))
            then(dve.scalar_tensor_tensor(p[:, :], p[:, :], 2.0, s[:, :], ALU.add, ALU.mult))
            then(dve.scalar_tensor_tensor(S["dt"][:, :], x[:, :], 0.0, p[:, :], ALU.max, ALU.add))
            dve.wait_ge(a_made, 1)
            then(dve.tensor_scalar(S["a"][:, :], S["a"][:, :], -1.0, None, ALU.mult))
            then(dve.tensor_scalar(p[:, :], S["dt"][:, :], S["a"][:, :], None, ALU.mult))
            for c in range(TT):
                dve.tensor_tensor_scan(S["acs"][:, c * P:(c + 1) * P], K["ones"][0:SH, :], p[:, c * P:(c + 1) * P], 0.0, ALU.mult, ALU.add)
            dve.tensor_copy(S["acs"][:, TP:], p[:, TP:]).then_inc(ready, 1)
            dve.wait_ge(turned, 1)
            dve.tensor_copy(S["dt_tok"][:, :, :], psT[:, 0, :, :])
            dve.tensor_copy(S["acs_tok"][:, :, :], psT[:, 1, :, :])


def prompt_scan(nc, A, K, S, acs_dram, outs):
    HP = SH // G
    with ExitStack() as ctx:
        m = Mem(nc, ctx, "scn")
        seg, ce = m.sb("seg", [P, SH, P]), m.sb("ce", [P, SH, P])
        x_tok, b_tok, xw = m.sb("x_tok", [P, DI]), m.sb("b_tok", [P, G * N]), m.sb("xw", [P, DI])
        cb = m.sb("cb", [P, G, P])
        state, state_out = m.sb("state", [P, DI]), m.sb("state_out", [P, 2, 512])
        to_end, end = m.sb("to_end", [P, SH]), m.sb("end", [P, SH])
        bank = [m.ps(f"bank{b}", [P, 512]) for b in range(8)]
        read_in, turned, copied, cb_made = m.sem("read_in"), m.sem("turned"), m.sem("copied"), m.sem("cb_made")
        cb_masked, seg_made, decayed, exped, weighted = (m.sem(n) for n in ("cb_masked", "seg_made", "decayed", "exped", "weighted"))
        ce_made, x_weighted, summed, y_done, grown, state_done = (m.sem(n) for n in ("ce_made", "x_weighted", "summed", "y_done", "grown", "state_done"))
        end_exped, end_in, chain = m.sem("end_exped"), m.sem("end_in"), m.sem("chain")
        out_turned, out_copied = m.sem("out_turned"), m.sem("out_copied")
        stored = [m.sem(f"stored{b}") for b in range(2)]
        block = ctx.enter_context(nc.Block())
        acs_all = acs_dram.rearrange("(a h) t -> a h t", a=1)
        heads_of = lambda ap, g: ap[:, g * HP:(g + 1) * HP, :]

        @block.sync
        def _(sp):
            for c in range(TT):
                if c:
                    sp.wait_ge(summed, 4 * c)
                    sp.wait_ge(exped, c)
                sp.dma_start(ce[:, :, :], acs_all[:, :, c * P:(c + 1) * P].to_broadcast([P, SH, P])).then_inc(read_in, 16)
            for q in range(4):
                sp.wait_ge(out_copied, q + 1)
                sp.dma_start(outs["ssm_p"][0, 0].rearrange("(k a) p n -> (a p) k n", a=2)[:, 4 * q:4 * q + 4, :],
                             state_out[:, q % 2, :].rearrange("p (k n) -> p k n", k=4)).then_inc(stored[q % 2], 16)
            sp.wait_ge(stored[0], 32)
            sp.wait_ge(stored[1], 32)

        @block.tensor
        def _(pe):
            for c in range(TT):
                at = slice(c * P, (c + 1) * P)
                for q in range(5):
                    if c:
                        pe.wait_ge(y_done if q < 4 else state_done, 4 * c if q < 4 else c)
                    for k in range(4):
                        last = pe.transpose(bank[q][:, k * P:(k + 1) * P], S["x"][:, 4 * q + k, at], K["ident"][:, :])
                    last.then_inc(turned, 1)
                if c:
                    pe.wait_ge(cb_masked, c)
                for g in range(G):
                    last = pe.matmul(bank[5][:, g * P:(g + 1) * P], S["x"][:, XB + g, at], S["x"][:, XC_ + g, at], start=True, stop=True)
                last.then_inc(cb_made, 1)
                pe.wait_ge(copied, 5 * c + 5)
                for q in range(4):
                    pe.wait_ge(weighted, 4 * c + q + 1)
                    if c:
                        pe.wait_ge(ce_made, 4 * c + q + 1)
                        pe.wait_ge(state_done, c)
                    for h in range(8 * q, 8 * q + 8):
                        out = bank[q][HD * (h % 2):HD * (h % 2) + HD, (h // 2 % 4) * P:(h // 2 % 4 + 1) * P]
                        last = pe.matmul(out, x_tok[:, h * HD:(h + 1) * HD], seg[:, h, :], start=True, stop=(c == 0))
                        if c:
                            last = pe.matmul(out, state[:, h * HD:(h + 1) * HD], ce[:, h, :], start=False, stop=True)
                    last.then_inc(summed, 1)
                pe.wait_ge(x_weighted, c + 1)
                for g in range(G):
                    if g == 0 and c:
                        pe.wait_ge(state_done, c)
                    dst = bank[4 if g == 0 else 5 + (g - 1)]
                    if g == 1:
                        pe.wait_ge(cb_masked, c + 1)
                    last = pe.matmul(dst[:, :], b_tok[:, g * N:(g + 1) * N], xw[:, g * 512:(g + 1) * 512], start=True, stop=True)
                last.then_inc(grown, 1)
            pe.wait_ge(state_done, TT)
            for q in range(4):
                if q >= 2:
                    pe.wait_ge(out_copied, q - 1)
                if q == 0:
                    pe.wait_ge(y_done, 4 * TT)
                for k in range(4):
                    last = pe.transpose(bank[q % 2][:, k * P:(k + 1) * P], state[:, (4 * q + k) * P:(4 * q + k + 1) * P], K["ident"][:, :])
                last.then_inc(out_turned, 1)

        @block.scalar
        def _(act):
            for c in range(TT):
                for q in range(5):
                    act.wait_ge(turned, 5 * c + q + 1)
                    if c and q == 0:
                        act.wait_ge(summed, 4 * c)
                        act.wait_ge(x_weighted, c)
                        act.wait_ge(grown, c)
                    act.activation(x_tok[:, q * 512:(q + 1) * 512] if q < 4 else b_tok[:, :], bank[q][:, :], ACT.Copy).then_inc(copied, 1)
                act.wait_ge(seg_made, c + 1)
                act.activation(seg[:, :, :], seg[:, :, :], ACT.Exp).then_inc(decayed, 1)
                act.wait_ge(end_in, c + 1)
                act.activation(to_end[:, :], to_end[:, :], ACT.Exp).then_inc(end_exped, 1)
                act.activation(end[:, :], ce[:, :, P - 1], ACT.Exp).then_inc(end_exped, 1)
                act.wait_ge(end_exped, 2 * c + 2)
                act.activation(ce[:, :, :], ce[:, :, :], ACT.Exp).then_inc(exped, 1)

        @block.vector
        def _(dve):
            then = Chain(dve, chain)
            for c in range(TT):
                at = slice(c * P, (c + 1) * P)
                dve.wait_ge(read_in, 16 * c + 16)
                for h in range(SH):
                    last = dve.tensor_scalar(seg[:, h, :], ce[:, h, :], S["acs_tok"][:, c, h:h + 1], 0.0, ALU.subtract, ALU.min)
                last.then_inc(seg_made, 1)
                dve.tensor_tensor(to_end[:, :], ce[:, :, P - 1], S["acs_tok"][:, c, :], ALU.subtract).then_inc(end_in, 1)
                dve.wait_ge(cb_made, c + 1)
                if c:
                    dve.wait_ge(weighted, 4 * c)
                dve.tensor_tensor(cb[:, :, :], bank[5][:, :].rearrange("p (g i) -> p g i", g=G),
                                  K["keep"][:, :].rearrange("p (a i) -> p a i", a=1).to_broadcast([P, G, P]), ALU.mult).then_inc(cb_masked, 1)
                dve.wait_ge(cb_masked, c + 1)
                dve.wait_ge(decayed, c + 1)
                for q in range(4):
                    for h in range(8 * q, 8 * q + 8):
                        last = dve.scalar_tensor_tensor(seg[:, h, :], seg[:, h, :], S["dt_tok"][:, c, h:h + 1], cb[:, h // HP, :], ALU.mult, ALU.mult)
                    last.then_inc(weighted, 1)
                if c:
                    dve.wait_ge(exped, c + 1)
                    for g in range(G):
                        dve.tensor_tensor(heads_of(ce, g), heads_of(ce, g),
                                          S["x"][:, XC_ + g:XC_ + g + 1, at].to_broadcast([P, HP, P]), ALU.mult).then_inc(ce_made, 1)
                else:
                    dve.sem_inc(ce_made, G)
                dve.wait_ge(end_exped, 2 * c + 2)
                then(dve.tensor_tensor(to_end[:, :], to_end[:, :], S["dt_tok"][:, c, :], ALU.mult))
                dve.wait_ge(copied, 5 * c + 4)
                dve.tensor_tensor(xw[:, :].rearrange("p (h d) -> p h d", h=SH), x_tok[:, :].rearrange("p (h d) -> p h d", h=SH),
                                  to_end[:, :].rearrange("p (h a) -> p h a", a=1).to_broadcast([P, SH, HD]), ALU.mult).then_inc(x_weighted, 1)
                for q in range(4):
                    dve.wait_ge(summed, 4 * c + q + 1)
                    for k in range(4 * q, 4 * q + 4):
                        last = dve.scalar_tensor_tensor(S["x"][:, k, at], S["x"][:, k, at], S["skip"][:, k:k + 1],
                                                        bank[q][:, (k % 4) * P:(k % 4 + 1) * P], ALU.mult, ALU.add)
                    last.then_inc(y_done, 1)
                dve.wait_ge(grown, c + 1)
                view = lambda ap: ap.rearrange("p (h d) -> p h d", d=HD)
                if c:
                    then(dve.tensor_tensor(view(state[:, :]), view(state[:, :]),
                                           end[:, :].rearrange("p (h a) -> p h a", a=1).to_broadcast([P, SH, HD]), ALU.mult))
                for g in range(G):
                    part, new = state[:, g * 512:(g + 1) * 512], bank[4 + g][:, :]
                    last = dve.tensor_tensor(part, part, new, ALU.add) if c else dve.tensor_copy(part, new)
                last.then_inc(state_done, 1)
            for q in range(4):
                dve.wait_ge(out_turned, q + 1)
                if q >= 2:
                    dve.wait_ge(stored[q % 2], 16)
                dve.tensor_copy(state_out[:, q % 2, :], bank[q % 2][:, :]).then_inc(out_copied, 1)


def sample_scan(nc, A, K, S, outs):
    with ExitStack() as ctx:
        m = Mem(nc, ctx, "stp")
        NB = 2
        st, tmp = m.sb("st", [P, NB, KI, N]), m.sb("tmp", [P, KI, N])
        rates_in, rates, dtx = m.sb("rates_in", [SH, 2 * TS]), m.sb("rates", [P, KI, 2 * TS]), m.sb("dtx", [P, KI, TS])
        y = m.sb("y", [P, KI, TS])
        bc = m.sb("bc", [P, 2, 2, P])
        psS, psB = m.ps("psS", [P, KI, 2 * TS]), m.ps("psB", [P, 2, 2, 512])
        wide = m.sb("wide", [P, 2 * G, P])
        st_in = [m.sem(f"st_in{b}") for b in range(NB)]
        stored = [m.sem(f"stored{b}") for b in range(NB)]
        set_, spread, widened, bc_made, decayed, updated, summed, chain = (m.sem(n) for n in (
            "set", "spread", "widened", "bc_made", "decayed", "updated", "summed", "chain"))
        dtx_made = m.sem("dtx_made")
        block = ctx.enter_context(nc.Block())
        view_in = A["state_ssm"][0].rearrange("b (k a) p n -> b (a p) k n", a=2)
        view_out = outs["ssm_s"][0].rearrange("b (k a) p n -> b (a p) k n", a=2)

        @block.sync
        def _(sp):
            for b in range(TS):
                if b >= NB:
                    sp.wait_ge(stored[b % NB], 16 * (b // NB))
                    sp.wait_ge(summed, b - NB + 1)
                sp.dma_start(st[:, b % NB], view_in[b]).then_inc(st_in[b % NB], 16)

        @block.scalar
        def _(act):
            for b in range(TS):
                act.wait_ge(updated, b + 1)
                act.dma_start(view_out[b], st[:, b % NB]).then_inc(stored[b % NB], 16)
            for b in range(NB):
                act.wait_ge(stored[b], 16 * (TS // NB))

        @block.gpsimd
        def _(pool):
            pool.wait_ge(dtx_made, 1)
            for b in range(TS):
                pool.wait_ge(st_in[b % NB], 16 * (b // NB + 1))
                pool.tensor_tensor(st[:, b % NB], st[:, b % NB], rates[:, :, TS + b:TS + b + 1].to_broadcast([P, KI, N]), ALU.mult).then_inc(decayed, 1)

        @block.tensor
        def _(pe):
            pe.wait_ge(set_, 2)
            for k in range(KI):
                last = pe.matmul(psS[:, k, :], K["spread"][:, k * P:(k + 1) * P], rates_in[:, :], start=True, stop=True)
            last.then_inc(spread, 1)
            for b in range(TS):
                pe.wait_ge(widened, b + 1)
                if b >= 2:
                    pe.wait_ge(summed, b - 1)
                for j in range(2):
                    for g in range(G):
                        last = pe.matmul(psB[:, b % 2, j, g * P:(g + 1) * P], wide[:, G * j + g, :], K["ident"][:, :], start=True, stop=True)
                last.then_inc(bc_made, 1)

        @block.vector
        def _(dve):
            then = Chain(dve, chain)
            dve.tensor_copy(rates_in[:, 0:TS], S["dt"][:, TP:]).then_inc(set_, 1)
            dve.tensor_copy(rates_in[:, TS:], S["decay_s"][:, :]).then_inc(set_, 1)
            dve.wait_ge(spread, 1)
            then(dve.tensor_copy(rates[:, :, :], psS[:, :, :]))
            dve.tensor_tensor(dtx[:, :, :], S["x"][:, 0:KI, TP:], rates[:, :, 0:TS], ALU.mult).then_inc(dtx_made, 1)
            dve.wait_ge(dtx_made, 1)
            groups = lambda ap: ap.rearrange("p (g k) n -> p g k n", g=G)
            for b in range(TS):
                if b:
                    dve.wait_ge(bc_made, b)
                dve.tensor_copy(wide[:, :, :], S["x"][:, XB:XB + 2 * G, TP + b:TP + b + 1].to_broadcast([P, 2 * G, P])).then_inc(widened, 1)
                dve.wait_ge(bc_made, b + 1)
                wide_row = lambda j: psB[:, b % 2, j, :].rearrange("p (g a n) -> p g a n", g=G, a=1)
                for g in range(G):
                    ks = slice(4 * g, 4 * g + 4)
                    last = dve.tensor_tensor(tmp[:, ks, :], psB[:, b % 2, 0, g * P:(g + 1) * P].rearrange("p (a n) -> p a n", a=1).to_broadcast([P, 4, N]),
                                             dtx[:, ks, b:b + 1].to_broadcast([P, 4, N]), ALU.mult)
                then(last)
                dve.wait_ge(decayed, b + 1)
                dve.tensor_tensor(st[:, b % NB], st[:, b % NB], tmp[:, :, :], ALU.add).then_inc(updated, 1)
                dve.wait_ge(updated, b + 1)
                for g in range(G):
                    ks = slice(4 * g, 4 * g + 4)
                    last = dve.tensor_tensor(tmp[:, ks, :], st[:, b % NB, ks, :],
                                             psB[:, b % 2, 1, g * P:(g + 1) * P].rearrange("p (a n) -> p a n", a=1).to_broadcast([P, 4, N]), ALU.mult)
                last.then_inc(summed, 1)
                dve.wait_ge(summed, b + 1)
                then(dve.tensor_reduce(y[:, :, b:b + 1], tmp[:, :, :], X, ALU.add))
            then(dve.tensor_tensor(dtx[:, :, :], S["x"][:, 0:KI, TP:], S["skip"][:, :].rearrange("p (k a) -> p k a", a=1).to_broadcast([P, KI, TS]), ALU.mult))
            dve.tensor_tensor(S["x"][:, 0:KI, TP:], dtx[:, :, :], y[:, :, :], ALU.add)


def skip_gains(nc, A, K, S):
    with ExitStack() as ctx:
        m = Mem(nc, ctx, "skp")
        d, ps = m.sb("d", [SH, 1]), m.ps("ps", [P, KI])
        d_in, made = m.sem("d_in"), m.sem("made")
        block = ctx.enter_context(nc.Block())

        @block.sync
        def _(sp):
            sp.dma_start(d[:, :], A["d_skip"].rearrange("l h -> h l")).then_inc(d_in, 16)
            sp.dma_start(S["g_ssm"][:, :], A["g_ssm"].rearrange("l (k p) -> p (l k)", p=P), allow_slow_non_contiguous=True).then_inc(d_in, 16)

        @block.tensor
        def _(pe):
            pe.wait_ge(d_in, 32)
            for k in range(KI):
                last = pe.matmul(ps[:, k:k + 1], K["spread"][:, k * P:(k + 1) * P], d[:, :], start=True, stop=True)
            last.then_inc(made, 1)

        @block.vector
        def _(dve):
            dve.wait_ge(made, 1)
            dve.tensor_copy(S["skip"][:, :], ps[:, :])


def gated_norm(nc, A, K, S, proj, yT_s):
    with ExitStack() as ctx:
        m = Mem(nc, ctx, "gtn")
        NB = 3
        z, sq = m.sb("z", [P, NB, T]), m.sb("sq", [P, NB, T])
        rstd = m.sb("rstd", [P, 2, HALF])
        ps = m.ps("ps", [P, 2, 512])
        z_in = [m.sem(f"z_in{b}") for b in range(NB)]
        gated, silued, squared, added, rooted, chain = (m.sem(n) for n in ("gated", "silued", "squared", "added", "rooted", "chain"))
        block = ctx.enter_context(nc.Block())

        @block.sync
        def _(sp):
            for k in range(KI):
                if k >= NB:
                    sp.wait_ge(gated, k - NB + 1)
                sp.dma_start(z[:, k % NB, :], proj[C_Z + k]).then_inc(z_in[k % NB], 16)

        @block.scalar
        def _(act):
            for k in range(KI + 1):
                if k < KI:
                    act.wait_ge(z_in[k % NB], 16 * (k // NB + 1))
                    act.activation(z[:, k % NB, :], z[:, k % NB, :], ACT.Silu).then_inc(silued, 1)
                if k:
                    act.wait_ge(gated, k)
                    if k > NB:
                        act.wait_ge(added, k - NB)
                    act.activation(sq[:, (k - 1) % NB, :], S["x"][:, k - 1, :], ACT.Square).then_inc(squared, 1)
            act.wait_ge(added, KI)
            act.activation(rstd[:, :, :], ps[:, :, 0:HALF], ACT.Sqrt, scale=1.0 / DI, bias=K["eps"][:, :]).then_inc(rooted, 1)

        @block.tensor
        def _(pe):
            for k in range(KI):
                pe.wait_ge(squared, k + 1)
                for s in range(2):
                    last = pe.matmul(ps[:, s, 0:HALF], K["ones"][:, :], sq[:, k % NB, s * HALF:(s + 1) * HALF],
                                     start=(k == 0), stop=(k == KI - 1))
                last.then_inc(added, 1)

        @block.vector
        def _(dve):
            then = Chain(dve, chain)
            for k in range(KI):
                dve.wait_ge(silued, k + 1)
                dve.tensor_tensor(S["x"][:, k, :], S["x"][:, k, :], z[:, k % NB, :], ALU.mult).then_inc(gated, 1)
            dve.wait_ge(rooted, 1)
            then(dve.reciprocal(rstd[:, :, :], rstd[:, :, :]))
            for k in range(KI):
                v = S["x"][:, k, :].rearrange("p (s t) -> p s t", s=2)
                last = dve.scalar_tensor_tensor(v, v, S["g_ssm"][:, k:k + 1], rstd[:, :, :], ALU.mult, ALU.mult)
            then(last)
            dve.tensor_copy(yT_s[:, :, :], S["x"][:, 0:KI, TP:])


WQ = 2 * P
BIG = -3.0e38


def merge(nc, A, K, tag, proj, first, W, oT, yT, mT):
    with ExitStack() as ctx:
        m = Mem(nc, ctx, tag)
        wa, wb = m.sb("wa", [P, 2, H, P]), m.sb("wb", [P, 2, KI, P])
        gate, part = m.sb("gate", [P, 2, 2, W]), m.sb("part", [P, 2, W])
        ps = m.ps("ps", [P, 2, 2, 512])
        w_in, gate_in, opened, summed, used = ([m.sem(f"{n}{b}") for b in range(2)]
                                               for n in ("w_in", "gate_in", "opened", "summed", "used"))
        chain = m.sem("chain")
        block = ctx.enter_context(nc.Block())

        def chunks(eng, body):
            with eng.Fori(0, KD // 2) as i:
                for b in range(2):
                    body(i, b, i * 2 + b)

        @block.sync
        def _(sp):
            def load(i, b, d):
                at = bass.ds(d * P, P)
                sp.wait_ge(summed[b], i)
                sp.dma_start(wa[:, b], A["w_br_a"].rearrange("l (k p) n -> p (l k) n", p=P)[:, :, at]).then_inc(w_in[b], 16)
                sp.dma_start(wb[:, b], A["w_br_b"].rearrange("l (k p) n -> p (l k) n", p=P)[:, :, at]).then_inc(w_in[b], 16)
                sp.wait_ge(used[b], i)
                for j, c in enumerate((C_GA, C_GB)):
                    sp.dma_start(gate[:, b, j, :], proj.rearrange("c p t -> p c t")[:, bass.ds(d + c, 1), first:first + W]).then_inc(gate_in[b], 16)
            chunks(sp, load)

        @block.tensor
        def _(pe):
            def product(i, b, d):
                pe.wait_ge(w_in[b], i * 32 + 32)
                pe.wait_ge(used[b], i)
                for j, (w, v, n) in enumerate(((wa, oT, H), (wb, yT, KI))):
                    for k in range(n):
                        last = pe.matmul(ps[:, b, j, 0:W], w[:, b, k, :], v[:, k, :], start=(k == 0), stop=(k == n - 1))
                last.then_inc(summed[b], 1)
            chunks(pe, product)

        @block.scalar
        def _(act):
            def open_(i, b, d):
                act.wait_ge(gate_in[b], i * 32 + 32)
                act.activation(gate[:, b], gate[:, b], ACT.Sigmoid).then_inc(opened[b], 1)
            chunks(act, open_)

        @block.vector
        def _(dve):
            def sum_(i, b, d):
                then = Steps(dve, chain, 2, d)
                dve.wait_ge(opened[b], i + 1)
                dve.wait_ge(summed[b], i + 1)
                dve.tensor_tensor(part[:, 0, :], ps[:, b, 0, 0:W], gate[:, b, 0, :], ALU.mult)
                then(dve.tensor_tensor(part[:, 1, :], ps[:, b, 1, 0:W], gate[:, b, 1, :], ALU.mult))
                then(dve.tensor_tensor(mT[:, bass.ds(d, 1), :].rearrange("p a t -> p (a t)"), part[:, 0, :], part[:, 1, :], ALU.add))
                dve.sem_inc(used[b], 1)
                then.full()
            chunks(dve, sum_)


def residual(nc, A, K, tag, tiles, gate_at, mT, x_src, x1):
    n = tiles[0]
    prompt = n == P
    with ExitStack() as ctx:
        m = Mem(nc, ctx, tag)
        w = m.sb("w", [P, KD, D])
        gate = m.sb("gate", [P, D])
        ps, psG = m.ps("ps", [P, 2, 2, 512]), m.ps("psG", [P, 2, 512])
        w_in, x_in, spread, summed, used, chain = (m.sem(k) for k in ("w_in", "x_in", "spread", "summed", "used", "chain"))
        scaled = m.sem("scaled")
        block = ctx.enter_context(nc.Block())

        @block.sync
        def _(sp):
            sp.dma_start(w[:, :, :], A["w_out"].rearrange("l (k p) n -> p (l k) n", p=P)).then_inc(w_in, 16)
            sp.dma_start(x1[0:n], x_src).then_inc(x_in, 16)

        @block.tensor
        def _(pe):
            if prompt:
                for c in range(2):
                    last = pe.matmul(psG[:, c, :], K["last"][:, :], K["ada"][:, gate_at + c * 512:gate_at + (c + 1) * 512], start=True, stop=True)
                last.then_inc(spread, 1)
            pe.wait_ge(w_in, 16)
            for t in range(len(tiles)):
                if t >= 2:
                    pe.wait_ge(used, t - 1)
                for c in range(2):
                    for k in range(KD):
                        last = pe.matmul(ps[0:n, t % 2, c, :], mT[:, k, t * P:t * P + n], w[:, k, c * 512:(c + 1) * 512], start=(k == 0), stop=(k == KD - 1))
                last.then_inc(summed, 1)

        @block.vector
        def _(dve):
            then = Chain(dve, chain)
            if not prompt:
                g = K["ada"][0:n, gate_at:gate_at + D]
            else:
                dve.wait_ge(spread, 1)
                then(dve.tensor_copy(gate[:, :], psG[:, :, :].rearrange("p c n -> p (c n)")))
                g = gate[:, :]
            dve.wait_ge(x_in, 16)
            for t in range(len(tiles)):
                dve.wait_ge(summed, t + 1)
                flat = ps[0:n, t % 2].rearrange("p c n -> p (c n)")
                then(dve.tensor_tensor(flat, flat, g, ALU.mult))
                dve.tensor_tensor(x1[0:n, t, :], x1[0:n, t, :], flat, ALU.add).then_inc(used, 1)


def choose(nc, A, K, tag, n, NTI, W, h2T, ids_out, gate_out):
    with ExitStack() as ctx:
        m = Mem(nc, ctx, tag)
        wq, keys, keysT = m.sb("wq", [P, KD, WQ]), m.sb("keys", [P, 2, P]), m.sb("keysT", [P, 2, P])
        qT = m.sb("qT", [P, 2, W])
        s, s2 = m.sb("s", [P, NTI, 2, NK]), m.sb("s2", [P, NTI, 2, NK])
        v, at = m.sb("v", [P, NTI, 2, TK]), m.sb("at", [P, NTI, 2, TK], U32)
        at_f = m.sb("at_f", [P, 2, NTI, TK])
        cand, cand2 = m.sb("cand", [P, NTI, TK, TK]), m.sb("cand2", [P, NTI, TK, TK])
        best, j = m.sb("best", [P, NTI, TK]), m.sb("j", [P, NTI, TK], U32)
        part, part_f = m.sb("part", [P, 2, NTI, TK], U32), m.sb("part_f", [P, 2, NTI, TK])
        one = m.sb("one", [P, NTI, TK, TK])
        picked = m.sb("picked", [P, 2, NTI, TK])
        total = m.sb("total", [P, NTI])
        count_i, count = m.sb("count_i", [P, TK], I32), m.sb("count", [P, TK])
        psK, psQ, psS = m.ps("psK", [P, 2, P]), m.ps("psQ", [P, 2, 512]), m.ps("psS", [P, NTI, 2, NK])
        (w_in, keys_in, turned, keys_copied, summed, q_copied, scored, s_copied, shifted, exped, chain, counted, count_made) = (
            m.sem(k) for k in ("w_in", "keys_in", "turned", "keys_copied", "summed", "q_copied", "scored", "s_copied",
                               "shifted", "exped", "chain", "counted", "count_made"))
        block = ctx.enter_context(nc.Block())
        bc = lambda ap, axis, shape: ap.unsqueeze(axis).to_broadcast(shape)

        @block.sync
        def _(sp):
            with sp.Fori(0, PH) as h:
                sp.wait_ge(summed, h)
                sp.dma_start(wq[:, :, :], A["peer_wq"].rearrange("l (k p) n -> p (l k) n", p=P)[:, :, bass.ds(h * WQ, WQ)]).then_inc(w_in, 16)
                sp.wait_ge(turned, h)
                for k, name in enumerate(("peer_keys1", "peer_keys2")):
                    sp.dma_start(keys[:, k, :], A[name].rearrange("l h n d -> n (l h) d")[:, bass.ds(h, 1), :]).then_inc(keys_in, 16)

        @block.gpsimd
        def _(pool):
            pool.iota(count_i[:, :], pattern=[[1, TK]], base=0, channel_multiplier=0).then_inc(counted, 1)

        @block.tensor
        def _(pe):
            with pe.Fori(0, PH) as h:
                pe.wait_ge(keys_in, h * 32 + 32)
                pe.wait_ge(keys_copied, h)
                for k in range(2):
                    last = pe.transpose(psK[:, k, :], keys[:, k, :], K["ident"][:, :])
                last.then_inc(turned, 1)
                pe.wait_ge(w_in, h * 16 + 16)
                pe.wait_ge(q_copied, h)
                for side in range(2):
                    for k in range(KD):
                        last = pe.matmul(psQ[:, side, 0:W], wq[:, k, side * P:(side + 1) * P], h2T[:, k, :], start=(k == 0), stop=(k == KD - 1))
                last.then_inc(summed, 1)
                pe.wait_ge(keys_copied, h + 1)
                pe.wait_ge(q_copied, h + 1)
                pe.wait_ge(s_copied, h)
                for t in range(NTI):
                    for side in range(2):
                        last = pe.matmul(psS[0:n, t, side, :], qT[:, side, t * P:t * P + n], keysT[:, side, :], start=True, stop=True)
                last.then_inc(scored, 1)

        @block.scalar
        def _(act):
            with act.Fori(0, PH) as h:
                act.wait_ge(turned, h + 1)
                act.wait_ge(scored, h)
                act.activation(keysT[:, :, :], psK[:, :, :], ACT.Copy).then_inc(keys_copied, 1)
                act.wait_ge(summed, h + 1)
                act.activation(qT[:, :, :], psQ[:, :, 0:W], ACT.Copy).then_inc(q_copied, 1)
                act.wait_ge(shifted, h + 1)
                act.activation(best[0:n], best[0:n], ACT.Exp).then_inc(exped, 1)

        @block.vector
        def _(dve):
            dve.wait_ge(counted, 1)
            dve.tensor_copy(count[:, :], count_i[:, :]).then_inc(count_made, 1)
            dve.wait_ge(count_made, 1)
            then = Chain(dve, chain)
            for h in range(PH):
                dve.wait_ge(scored, h + 1)
                then(dve.tensor_copy(s[0:n], psS[0:n]))
                dve.sem_inc(s_copied, 1)

                def top(src, src2, vals, ids):
                    then(dve.max(vals[:, 0:8], src))
                    dve.max_index(ids[:, 0:8], vals[:, 0:8], src)
                    then(dve.match_replace(src2, vals[:, 0:8], src, BIG))
                    then(dve.max(vals[:, 8:16], src2))
                    then(dve.max_index(ids[:, 8:16], vals[:, 8:16], src2))

                for t in range(NTI):
                    for side in range(2):
                        top(s[0:n, t, side, :], s2[0:n, t, side, :], v[0:n, t, side, :], at[0:n, t, side, :])
                shape = [n, NTI, TK, TK]
                for side in range(2):
                    dve.tensor_copy(at_f[0:n, side], at[0:n, :, side, :])
                then(dve.tensor_tensor(cand[0:n], bc(v[0:n, :, 0, :], 3, shape), bc(v[0:n, :, 1, :], 2, shape), ALU.add))
                for t in range(NTI):
                    flat = lambda tile: tile[0:n, t].rearrange("p a b -> p (a b)")
                    top(flat(cand), flat(cand2), best[0:n, t, :], j[0:n, t, :])
                dve.tensor_scalar(part[0:n, 0], j[0:n], 4, None, ALU.logical_shift_right)
                then(dve.tensor_scalar(part[0:n, 1], j[0:n], TK - 1, None, ALU.bitwise_and))
                then(dve.tensor_copy(part_f[0:n], part[0:n]))
                then(dve.tensor_copy(total[0:n, :], best[0:n, :, 0]))
                dve.tensor_tensor(best[0:n], best[0:n], bc(total[0:n, :], 2, [n, NTI, TK]), ALU.subtract).then_inc(shifted, 1)
                every = count[0:n, :].unsqueeze(1).unsqueeze(1).to_broadcast(shape)
                for side in range(2):
                    then(dve.tensor_tensor(one[0:n], bc(part_f[0:n, side], 3, shape), every, ALU.is_equal))
                    then(dve.tensor_tensor(one[0:n], one[0:n], bc(at_f[0:n, side], 2, shape), ALU.mult))
                    then(dve.tensor_reduce(picked[0:n, side], one[0:n], X, ALU.add))
                then(dve.scalar_tensor_tensor(ids_out(h), picked[0:n, 0], float(NK), picked[0:n, 1], ALU.mult, ALU.add))
                dve.wait_ge(exped, h + 1)
                then(dve.tensor_reduce(total[0:n, :], best[0:n], X, ALU.add))
                then(dve.reciprocal(total[0:n, :], total[0:n, :]))
                then(dve.tensor_tensor(gate_out(h), best[0:n], bc(total[0:n, :], 2, [n, NTI, TK]), ALU.mult))


UR, VR = 4, 8
GS = 4
SLOTS_SEQ = SL // 2
PE_PLACES = (5,)


def sample_queries(nc, A, K, M, L):
    with ExitStack() as ctx:
        m = Mem(nc, ctx, "sqr")
        gk_n, gk_r = m.sb("gk_n", [P, 1]), m.sb("gk_r", [ROPE, 1])
        q_n = m.sb("q_n", [P, H * TS])
        w_ukT = m.sb("w_ukT", [P, 2, LAT])
        keys, sq = m.sb("keys", [TS, H, NOPE]), m.sb("sq", [TS, H, NOPE])
        kpe, kpe_sq = m.sb("kpe", [TS, ROPE]), m.sb("kpe_sq", [TS, ROPE])
        ss, kss, rstd = m.sb("ss", [TS, H]), m.sb("kss", [TS, 1]), m.sb("rstd", [TS, H])
        mask = m.sb("mask", [TS, TS, H])
        psT, psQ = m.ps("psT", [P, 2, LAT]), m.ps("psQ", [P, KL, TS, H])
        psK, psR, psE = m.ps("psK", [TS, 2, 512]), m.ps("psR", [TS, TS * H]), m.ps("psE", [TS, ROPE])
        loaded, scaled, turned, copied, q_head, q_copied = (m.sem(k) for k in ("loaded", "scaled", "turned", "copied", "q_head", "q_copied"))
        keyed, squared, rooted, scored, chain, masked, zeroed = (m.sem(k) for k in ("keyed", "squared", "rooted", "scored", "chain", "masked", "zeroed"))
        meaned = m.sem("meaned")
        block = ctx.enter_context(nc.Block())

        @block.sync
        def _(sp):
            sp.dma_start(L["w_uk"][:, :, :], A["w_uk"].rearrange("l (k p) h d -> p (l k) (h d)", p=P)).then_inc(loaded, 16)
            sp.dma_start(gk_n[:, :], A["g_k"][0, 0:NOPE].rearrange("(p a) -> p a", a=1)).then_inc(loaded, 16)
            sp.dma_start(gk_r[:, :], A["g_k"][0, NOPE:DQK].rearrange("(p a) -> p a", a=1)).then_inc(loaded, 16)

        @block.gpsimd
        def _(pool):
            pool.memset(mask[:, :, :], 0.0).then_inc(zeroed, 1)
            pool.wait_ge(zeroed, 1)
            pool.affine_select(out=mask[:, :, :], in_=mask[:, :, :], compare_op=ALU.is_equal, fill=NEG, base=0,
                               pattern=[[-1, TS], [0, H]], channel_multiplier=1).then_inc(masked, 1)

        @block.tensor
        def _(pe):
            pe.wait_ge(loaded, 48)
            pe.wait_ge(scaled, 2)
            for h in range(H):
                if h >= 2:
                    pe.wait_ge(copied, h - 1)
                for k in range(KL):
                    last = pe.transpose(psT[:, h % 2, k * P:(k + 1) * P], L["w_uk"][:, k, h * NOPE:(h + 1) * NOPE], K["ident"][:, :])
                last.then_inc(turned, 1)
                pe.wait_ge(copied, h + 1)
                for k in range(KL):
                    last = pe.matmul(psQ[:, k, :, h], w_ukT[:, h % 2, k * P:(k + 1) * P], q_n[:, h * TS:(h + 1) * TS], start=True, stop=True)
                last.then_inc(q_head, 1)
            for c in range(2):
                for k in range(KL):
                    last = pe.matmul(psK[:, c, :], M["ckvT"][:, k, TP:T], L["w_uk"][:, k, c * 512:(c + 1) * 512], start=(k == 0), stop=(k == KL - 1))
            pe.transpose(psE[:, :], M["kpeT"][:, TP:T], K["ident"][0:ROPE, 0:ROPE]).then_inc(keyed, 1)
            pe.wait_ge(q_copied, 1)
            for k in range(KL):
                pe.matmul(psR[:, :], M["ckvT"][:, k, TP:T], L["q_lat"][:, k].rearrange("p b h -> p (b h)"), start=(k == 0), stop=False)
            pe.matmul(psR[:, :], M["kpeT"][:, TP:T], L["q_rope"][:, :, :].rearrange("p b h -> p (b h)"), start=False, stop=True).then_inc(scored, 1)

        @block.scalar
        def _(act):
            for h in range(H):
                act.wait_ge(turned, h + 1)
                if h >= 2:
                    act.wait_ge(q_head, h - 1)
                act.activation(w_ukT[:, h % 2, :], psT[:, h % 2, :], ACT.Copy).then_inc(copied, 1)
            act.wait_ge(keyed, 1)
            act.activation(sq[:, :, :].rearrange("p h d -> p (h d)"), psK[:, :, :].rearrange("p c n -> p (c n)"), ACT.Square).then_inc(squared, 1)
            act.activation(kpe_sq[:, :], psE[:, :], ACT.Square, accum_out=kss[:, :]).then_inc(squared, 1)
            act.wait_ge(meaned, 1)
            act.activation(rstd[:, :], ss[:, :], ACT.Sqrt, scale=1.0 / DQK, bias=K["eps"][0:TS, :]).then_inc(rooted, 1)

        @block.vector
        def _(dve):
            then = Chain(dve, chain)
            dve.wait_ge(loaded, 48)
            dve.tensor_scalar(q_n[:, :], M["qs_n"][:, :], gk_n[:, :], None, ALU.mult).then_inc(scaled, 1)
            dve.tensor_scalar(L["q_rope"][:, :, :].rearrange("p b h -> p h b"), M["qs_r"][:, :].rearrange("p (h b) -> p h b", h=H),
                              gk_r[:, :], None, ALU.mult).then_inc(scaled, 1)
            dve.wait_ge(q_head, H)
            dve.tensor_copy(L["q_lat"][:, :, :, :], psQ[:, :, :, :]).then_inc(q_copied, 1)
            dve.wait_ge(squared, 2)
            then(dve.tensor_reduce(ss[:, :], sq[:, :, :], X, ALU.add))
            dve.tensor_scalar(ss[:, :], ss[:, :], kss[:, :], None, ALU.add).then_inc(meaned, 1)
            dve.wait_ge(rooted, 1)
            then(dve.reciprocal(rstd[:, :], rstd[:, :]))
            dve.wait_ge(scored, 1)
            dve.wait_ge(masked, 1)
            then(dve.tensor_tensor(L["new"][:, :, :], psR[:, :].rearrange("p (b h) -> p b h", h=H),
                                   rstd[:, :].unsqueeze(1).to_broadcast([TS, TS, H]), ALU.mult))
            dve.tensor_tensor(L["new"][:, :, :], L["new"][:, :, :], mask[:, :, :], ALU.add)


def attend_and_mix(nc, A, K, L, D_, outs):
    with ExitStack() as ctx:
        m = Mem(nc, ctx, "mix")
        ckv, kpe = m.sb("ckv", [P, 2, NT, LAT]), m.sb("kpe", [P, 2, NT, ROPE])
        ckvT, kpeT = m.sb("ckvT", [P, 2, KL, P]), m.sb("kpeT", [ROPE, 2, P])
        sq = m.sb("sq", [P, H, NOPE])
        q_lat, q_rope = m.sb("q_lat", [P, 2, KL, H]), m.sb("q_rope", [ROPE, 2, H])
        ss, kss, rstd = m.sb("ss", [P, NT, H]), m.sb("kss", [P, NT]), m.sb("rstd", [P, NT, H])
        s = m.sb("s", [P, NT + 1, H])
        top, top_row, diag8, part_sum, share = m.sb("top", [P, H]), m.sb("top_row", [H, 1]), m.sb("diag8", [H, H]), m.sb("part_sum", [P, H]), m.sb("share", [H, 1])
        o_lat = m.sb("o_lat", [H, LAT])
        table = m.sb("table", [1, TS * NT], I32)
        u, v = m.sb("u", [P, UR, D]), m.sb("v", [P, VR, D])
        h2, x1, acc = m.sb("h2", [P, D]), m.sb("x1", [P, D]), m.sb("acc", [P, D])
        ids, gate, gate2 = m.sb("ids", [P, SL], I32), m.sb("gate", [P, SL]), m.sb("gate2", [P, D])
        dots, coef = m.sb("dots", [P, SL]), m.sb("coef", [P, SL])
        diag = m.sb("diag", [P, len(PE_PLACES), P])
        psT, psE, psN, psR, psO, psA = (m.ps("psT", [P, 512]), m.ps("psE", [P, 512]), m.ps("psN", [P, 2, 512]),
                                        m.ps("psR", [P, 512]), m.ps("psO", [H, 512]), m.ps("psA", [P, 2, 512]))
        psK, psTop, psBc, psSum, psOT = psE[0:ROPE, 0:P], psE[0:H, P:2 * P], psE[:, 256:264], psE[0:H, 272:273], psE[:, 288:320]
        pages_in = [m.sem(f"pages_in{b}") for b in range(2)]
        pages_used = [m.sem(f"pages_used{b}") for b in range(2)]
        (table_in, table_read, q_set, turned, copied, keyed, squared, reduced, kpe_squared, meaned, rooted, topped, top_turned,
         diag_made, top_spread, shifted, exped, summed, sums_made, weighed, scaled, o_turned, o_kept, chain) = (m.sem(k) for k in (
             "table_in", "table_read", "q_set", "turned", "copied", "keyed", "squared", "reduced", "kpe_squared", "meaned", "rooted", "topped",
             "top_turned", "diag_made", "top_spread", "shifted", "exped", "summed", "sums_made", "weighed", "scaled",
             "o_turned", "o_kept", "chain"))
        u_in, u_used = [m.sem(f"u_in{k}") for k in range(UR)], [m.sem(f"u_used{k}") for k in range(UR)]
        v_in, v_used = [m.sem(f"v_in{k}") for k in range(VR)], [m.sem(f"v_used{k}") for k in range(VR)]
        (ids_in, tile_in, tile_used, dotted, gelued, weighted, added, diagonal, mixed, y_made, y_stored, gate2_made,
         gate2_spread, held) = (
            m.sem(k) for k in ("ids_in", "tile_in", "tile_used", "dotted", "gelued", "weighted", "added", "diagonal",
                               "mixed", "y_made", "y_stored", "gate2_made", "gate2_spread", "held"))
        block = ctx.enter_context(nc.Block())
        TURNS = TT
        NG = SL // GS
        NPE = len(PE_PLACES) * SL // VR
        u_rows, v_rows = A["peer_u"].rearrange("l e d -> (l e) d"), A["peer_v"].rearrange("l e d -> (l e) d")

        TILE_SLOT = {3 * t: t for t in range(NT)}
        END = 3 * NT

        def by_pe(slot):
            return slot >= 0 and slot % VR in PE_PLACES

        def pe_before(slot):
            return sum(by_pe(x) for x in range(slot))

        def hold(eng, sem, value):
            eng.wait_ge(sem, value)
            eng.sem_inc(held, 1)

        def dve_before(slot):
            return slot - pe_before(slot)

        def pe_add(pe, i, slot, j):
            pe.wait_ge(diagonal, i * NPE + (j + 1))
            if j == 0:
                pe.wait_ge(gate2_made, 1)
                pe.wait_ge(mixed, i)
            place = slot % VR
            pe.wait_ge(v_in[place], i * (16 * SL // VR) + 16 * (slot // VR + 1))
            for c in range(2):
                last = pe.matmul(psA[:, c, :], diag[:, PE_PLACES.index(place), :], v[:, place, c * 512:(c + 1) * 512],
                                 start=(j == 0), stop=(j == NPE - 1))
            last.then_inc(v_used[place], 1)

        @block.sync
        def _(sp):
            sp.dma_start(table[:, :], A["page_table"].rearrange("b n -> (b n)").unsqueeze(0)).then_inc(table_in, 16)
            sp.wait_ge(table_in, 16)
            with sp.Fori(0, TURNS) as i:
                for b in range(2):
                    sp.wait_ge(pages_used[b], i)
                    for t in range(NT):
                        page = sp.value_load(table[0:1, bass.ds(i * (2 * NT) + (b * NT + t), 1)], min_val=0, max_val=A["cache_ckv"].shape[1] - 1)
                        sp.dma_start(ckv[:, b, t, :], A["cache_ckv"][0, bass.ds(page, 1)].rearrange("a p c -> (a p) c")).then_inc(pages_in[b], 16)
                        sp.dma_start(kpe[:, b, t, :], A["cache_kpe"][0, bass.ds(page, 1)].rearrange("a p c -> (a p) c")).then_inc(pages_in[b], 16)

        @block.gpsimd
        def _(pool):
            with pool.Fori(0, TURNS) as i:
                pool.dma_start(ids[:, :], D_["ids"][bass.ds(i, 1)].rearrange("a p s -> (a p) s")).then_inc(ids_in, 16)
                hold(pool, ids_in, i * 16 + 16)
                for slot in range(SL):
                    for ring, n, used, landed, table_rows in ((u, UR, u_used, u_in, u_rows), (v, VR, v_used, v_in, v_rows)):
                        hold(pool, used[slot % n], i * (SL // n) + slot // n)
                        pool.indirect_dma_start(ring[:, slot % n, :], None, table_rows,
                                                bass.IndirectOffsetOnAxis(ids[:, slot:slot + 1], 0)).then_inc(landed[slot % n], 16)
                for n, landed in ((UR, u_in), (VR, v_in)):
                    for k in range(n):
                        hold(pool, landed[k], (i + 1) * (16 * SL // n))

        @block.tensor
        def _(pe):
            for c in range(2):
                last = pe.matmul(psA[:, c, :], K["last"][:, :], K["ada"][:, 5 * D + c * 512:5 * D + (c + 1) * 512], start=True, stop=True)
            last.then_inc(gate2_spread, 1)
            with pe.Fori(0, TURNS) as i:
                for slot in range(SL):
                    b, r = slot // SLOTS_SEQ, slot % SLOTS_SEQ
                    n = i * 2 + b
                    def turn(t):
                        if t == 0:
                            pe.wait_ge(pages_in[b], (i + 1) * (NT * 32))
                            pe.wait_ge(o_kept, n)
                        pe.wait_ge(copied, (n * NT + t) * 2)
                        for k in range(KL):
                            pe.transpose(psT[:, k * P:(k + 1) * P], ckv[:, b, t, k * P:(k + 1) * P], K["ident"][:, :])
                        pe.transpose(psK, kpe[:, b, t, :], K["ident"][:, :]).then_inc(turned, 1)
                    if r == 0:
                        turn(0)
                    if r in TILE_SLOT:
                        t = TILE_SLOT[r]
                        if t == 0:
                            pe.wait_ge(q_set, (n + 1) * 2)
                            pe.wait_ge(topped, n)
                        pe.wait_ge(squared, n * NT + t)
                        pe.wait_ge(copied, (n * NT + (t + 1)) * 2)
                        for c in range(2):
                            for k in range(KL):
                                last = pe.matmul(psN[:, c, :], ckvT[:, t % 2, k, :], L["w_uk"][:, k, c * 512:(c + 1) * 512], start=(k == 0), stop=(k == KL - 1))
                        last.then_inc(keyed, 1)
                        for k in range(KL):
                            pe.matmul(psR[:, t * H:(t + 1) * H], ckvT[:, t % 2, k, :], q_lat[:, b, k, :], start=(k == 0), stop=False)
                        pe.matmul(psR[:, t * H:(t + 1) * H], kpeT[:, t % 2, :], q_rope[:, b, :], start=False, stop=True).then_inc(summed, 1)
                        if t + 1 < NT:
                            turn(t + 1)
                    if r == END + 3:
                        pe.wait_ge(topped, n + 1)
                        pe.transpose(psTop, top[:, :], K["ident"][:, :]).then_inc(top_turned, 1)
                    if r == END + 5:
                        pe.wait_ge(diag_made, n + 1)
                        pe.matmul(psBc, K["ones"][0:H, :], diag8[:, :], start=True, stop=True).then_inc(top_spread, 1)
                    if r == END + 8:
                        pe.wait_ge(exped, n + 1)
                        for t in range(NT):
                            pe.matmul(psO[:, :], s[:, t, :], ckv[:, b, t, :], start=(t == 0), stop=False)
                        pe.matmul(psO[:, :], s[0:TS, NT, :], L["ckv_new"][:, :], start=False, stop=True).then_inc(weighed, 1)
                    if r == END + 9:
                        pe.wait_ge(sums_made, n + 1)
                        pe.matmul(psSum, part_sum[:, :], K["ones"][:, 0:1], start=True, stop=True).then_inc(o_turned, 1)
                    if r == END + 12:
                        hold(pe, scaled, n + 1)
                        for k in range(KL):
                            last = pe.transpose(psOT[:, k * H:(k + 1) * H], o_lat[:, k * P:(k + 1) * P], K["ident"][0:H, 0:H])
                        last.then_inc(o_turned, 1)
                    if by_pe(slot - GS):
                        j = pe_before(slot - GS)
                        pe_add(pe, i, slot - GS, j)
                for slot in range(SL - GS, SL):
                    if by_pe(slot):
                        pe_add(pe, i, slot, pe_before(slot))

        @block.scalar
        def _(act):
            with act.Fori(0, TURNS) as i:
                act.wait_ge(tile_used, i)
                for tile, name in ((h2, "h2"), (gate, "gate")):
                    act.dma_start(tile[:, :], D_[name][bass.ds(i, 1)].rearrange("a p s -> (a p) s")).then_inc(tile_in, 16)
                act.wait_ge(y_stored, i * 16)
                act.dma_start(x1[:, :], D_["x1"][bass.ds(i, 1)].rearrange("a p s -> (a p) s")).then_inc(tile_in, 16)
                for slot in range(SL):
                    b, r = slot // SLOTS_SEQ, slot % SLOTS_SEQ
                    n = i * 2 + b

                    def copy(t):
                        act.wait_ge(turned, n * NT + (t + 1))
                        if t >= 1:
                            act.wait_ge(summed, n * NT + (t - 1))
                        else:
                            act.wait_ge(summed, n * NT)
                        act.activation(ckvT[:, t % 2].rearrange("p k n -> p (k n)"), psT[:, :], ACT.Copy).then_inc(copied, 1)
                        act.activation(kpeT[:, t % 2, :], psK, ACT.Copy).then_inc(copied, 1)
                    if r == 0:
                        copy(0)
                    if r in TILE_SLOT:
                        t = TILE_SLOT[r]
                        act.wait_ge(keyed, n * NT + (t + 1))
                        act.wait_ge(reduced, n * NT + t)
                        act.activation(sq[:, :, :].rearrange("p h d -> p (h d)"), psN[:, :, :].rearrange("p c n -> p (c n)"), ACT.Square).then_inc(squared, 1)
                        if t + 1 < NT:
                            copy(t + 1)
                    if r == END:
                        act.wait_ge(reduced, n * NT + NT)
                        act.activation(sq[:, :, :].rearrange("p h d -> p (h d)"), kpe[:, b].rearrange("p t c -> p (t c)"), ACT.Square).then_inc(kpe_squared, 1)
                    if r == END + 1:
                        act.wait_ge(meaned, n + 1)
                        act.activation(rstd[:, :, :], ss[:, :, :], ACT.Sqrt, scale=1.0 / DQK, bias=K["eps"][:, :]).then_inc(rooted, 1)
                    if r == END + 7:
                        act.wait_ge(shifted, n + 1)
                        act.activation(s[:, :, :], s[:, :, :], ACT.Exp, scale=SCALE).then_inc(exped, 1)
                    if slot % GS == GS - 1:
                        g = slot // GS
                        act.wait_ge(dotted, i * NG + (g + 1))
                        act.activation(coef[:, g * GS:(g + 1) * GS], dots[:, g * GS:(g + 1) * GS], ACT.Gelu).then_inc(gelued, 1)
                act.wait_ge(y_made, i + 1)
                act.dma_start(outs["y_p"][0, bass.ds(i * P, P), :], x1[:, :]).then_inc(y_stored, 16)
            act.wait_ge(y_stored, TURNS * 16)

        @block.vector
        def _(dve):
            dve.wait_ge(gate2_spread, 1)
            dve.tensor_copy(gate2[:, :], psA[:, :, :].rearrange("p c n -> p (c n)")).then_inc(gate2_made, 1)
            dve.wait_ge(gate2_made, 1)
            with dve.Fori(0, TURNS) as i:
                then = Steps(dve, chain, 2 * 8 + 2, i)

                def weigh(g):
                    dve.wait_ge(gelued, i * NG + (g + 1))
                    dve.tensor_tensor(coef[:, g * GS:(g + 1) * GS], coef[:, g * GS:(g + 1) * GS], gate[:, g * GS:(g + 1) * GS], ALU.mult).then_inc(weighted, 1)
                    dve.wait_ge(weighted, i * NG + (g + 1))

                def add(slot):
                    c = coef[:, slot:slot + 1]
                    if by_pe(slot):
                        place = slot % VR
                        dve.wait_ge(v_used[place], i * (SL // VR) + slot // VR)
                        dve.tensor_scalar(diag[:, PE_PLACES.index(place), :], K["ident"][:, :], c, None, ALU.mult).then_inc(diagonal, 1)
                        return
                    j = dve_before(slot)
                    dve.wait_ge(v_in[slot % VR], i * (16 * SL // VR) + 16 * (slot // VR + 1))
                    if j == 0:
                        last = dve.tensor_scalar(acc[:, :], v[:, slot % VR, :], c, None, ALU.mult)
                    else:
                        dve.wait_ge(added, i * (SL - NPE) + j)
                        last = dve.scalar_tensor_tensor(acc[:, :], v[:, slot % VR, :], c, acc[:, :], ALU.mult, ALU.add)
                    last.then_inc(added, 1)
                    dve.wait_ge(added, i * (SL - NPE) + (j + 1))
                    dve.sem_inc(v_used[slot % VR], 1)

                for slot in range(SL):
                    b, r = slot // SLOTS_SEQ, slot % SLOTS_SEQ
                    n = i * 2 + b
                    if r == 0:
                        dve.tensor_scalar(q_lat[:, b], L["q_lat"][:, :, bass.ds(n, 1), :].rearrange("p k a h -> p k (a h)"), 1.0, None, ALU.mult).then_inc(q_set, 1)
                        dve.tensor_scalar(q_rope[:, b], L["q_rope"][:, bass.ds(n, 1), :].rearrange("p a h -> p (a h)"), 1.0, None, ALU.mult).then_inc(q_set, 1)
                    if r - 1 in TILE_SLOT:
                        t = TILE_SLOT[r - 1]
                        dve.wait_ge(squared, n * NT + (t + 1))
                        dve.tensor_reduce(ss[:, t, :], sq[:, :, :], X, ALU.add).then_inc(reduced, 1)
                    if r == END + 1:
                        dve.wait_ge(kpe_squared, n + 1)
                        then(dve.tensor_reduce(kss[:, :], sq[:, :, :].rearrange("p h d -> p (h d)").rearrange("p (t c) -> p t c", t=NT), X, ALU.add))
                        dve.tensor_tensor(ss[:, :, :], ss[:, :, :], kss[:, :].unsqueeze(2).to_broadcast([P, NT, H]), ALU.add).then_inc(meaned, 1)
                    if r == END + 3:
                        dve.wait_ge(rooted, n + 1)
                        then(dve.reciprocal(rstd[:, :, :], rstd[:, :, :]))
                        dve.wait_ge(summed, n * NT + NT)
                        dve.tensor_tensor(s[:, 0:NT, :], psR[:, 0:NT * H].rearrange("p (t h) -> p t h", h=H), rstd[:, :, :], ALU.mult)
                        then(dve.memset(s[:, NT, :], NEG))
                        then(dve.tensor_scalar(s[0:TS, NT, :], L["new"][:, bass.ds(n, 1), :].rearrange("p a h -> p (a h)"), 1.0, None, ALU.mult))
                        dve.tensor_reduce(top[:, :], s[:, :, :].rearrange("p t h -> p h t"), X, ALU.max).then_inc(topped, 1)
                    if r == END + 5:
                        dve.wait_ge(top_turned, n + 1)
                        then(dve.tensor_reduce(top_row[:, :], psTop, X, ALU.max))
                        dve.tensor_scalar(diag8[:, :], K["ident"][0:H, 0:H], top_row[:, :], None, ALU.mult).then_inc(diag_made, 1)
                    if r == END + 7:
                        dve.wait_ge(top_spread, n + 1)
                        dve.tensor_tensor(s[:, :, :], s[:, :, :], psBc.unsqueeze(1).to_broadcast([P, NT + 1, H]), ALU.subtract).then_inc(shifted, 1)
                    if r == END + 9:
                        dve.wait_ge(exped, n + 1)
                        dve.tensor_reduce(part_sum[:, :], s[:, :, :].rearrange("p t h -> p h t"), X, ALU.add).then_inc(sums_made, 1)
                    if r == END + 11:
                        dve.wait_ge(o_turned, n * 2 + 1)
                        then(dve.reciprocal(share[:, :], psSum))
                        dve.wait_ge(weighed, n + 1)
                        then(dve.tensor_scalar(o_lat[:, :], psO[:, :], share[:, :], None, ALU.mult))
                        dve.sem_inc(scaled, 1)
                        dve.sem_inc(pages_used[b], 1)
                    if r == END + 13:
                        dve.wait_ge(o_turned, n * 2 + 2)
                        then(dve.tensor_scalar(L["o_lat"][:, bass.ds(n, 1), :].rearrange("p a k -> p (a k)"), psOT, 1.0, None, ALU.mult))
                        dve.sem_inc(o_kept, 1)
                    if slot == 0:
                        dve.wait_ge(tile_in, i * 48 + 48)
                    k = slot % UR
                    dve.wait_ge(u_in[k], i * (16 * SL // UR) + 16 * (slot // UR + 1))
                    dve.tensor_tensor_reduce(u[:, k, :], u[:, k, :], h2[:, :], 1.0, 0.0, ALU.mult, ALU.add, dots[:, slot:slot + 1]).then_inc(u_used[k], 1)
                    if slot % GS == GS - 1:
                        dve.wait_ge(u_used[k], i * (SL // UR) + (slot // UR + 1))
                        dve.sem_inc(dotted, 1)
                    if slot >= GS:
                        if slot % GS == 0:
                            weigh(slot // GS - 1)
                        add(slot - GS)
                weigh(NG - 1)
                for slot in range(SL - GS, SL):
                    add(slot)
                dve.sem_inc(tile_used, 1)
                for place in PE_PLACES:
                    dve.wait_ge(v_used[place], (i + 1) * (SL // VR))
                then(dve.tensor_tensor(acc[:, :], acc[:, :], psA[:, :, :].rearrange("p c n -> p (c n)"), ALU.add))
                dve.sem_inc(mixed, 1)
                then(dve.tensor_tensor(acc[:, :], acc[:, :], gate2[:, :], ALU.mult))
                dve.tensor_tensor(x1[:, :], x1[:, :], acc[:, :], ALU.add).then_inc(y_made, 1)
                dve.wait_ge(y_made, i + 1)
                then.full()


def sample_values(nc, A, K, L, oT):
    with ExitStack() as ctx:
        m = Mem(nc, ctx, "val")
        w = m.sb("w", [P, KL, H * DV])
        ps = m.ps("ps", [P, H, TS])
        w_in, made = m.sem("w_in"), m.sem("made")
        block = ctx.enter_context(nc.Block())

        @block.sync
        def _(sp):
            sp.dma_start(w[:, :, :], A["w_uv"].rearrange("l (k p) h d -> p (l k) (h d)", p=P)).then_inc(w_in, 16)

        @block.tensor
        def _(pe):
            pe.wait_ge(w_in, 16)
            for h in range(H):
                for k in range(KL):
                    last = pe.matmul(ps[:, h, :], w[:, k, h * DV:(h + 1) * DV], L["o_lat"][:, :, k * H + h], start=(k == 0), stop=(k == KL - 1))
            last.then_inc(made, 1)

        @block.vector
        def _(dve):
            dve.wait_ge(made, 1)
            dve.tensor_copy(oT[:, :, :], ps[:, :, :])


def sample_experts(nc, A, K, h2, x1, ids_f, gate, outs):
    with ExitStack() as ctx:
        m = Mem(nc, ctx, "sex")
        NB = 4
        u, v = m.sb("u", [P, NB, D]), m.sb("v", [P, NB, D])
        idsT, gateT, coef = m.sb("idsT", [P, TS], I32), m.sb("gateT", [P, TS]), m.sb("coef", [P, TS])
        coefs = m.sb("coefs", [P, TS, TS])
        same = m.sb("same", [P, TS, TS])
        row = m.sb("row", [TS, TS, P])
        y = m.sb("y", [TS, D])
        psT, psH, psY = m.ps("psT", [P, 2, TS]), m.ps("psH", [P, 2, 512]), m.ps("psY", [TS, 2, 512])
        filled, made, turned, set_, h_spread, dotted, gelued, weighted, mixed, y_done, chain, stored = (m.sem(k) for k in (
            "filled", "made", "turned", "set", "h_spread", "dotted", "gelued", "weighted", "mixed", "y_done", "chain", "stored"))
        u_in, v_in = [m.sem(f"u_in{k}") for k in range(NB)], [m.sem(f"v_in{k}") for k in range(NB)]
        block = ctx.enter_context(nc.Block())
        u_rows, v_rows = A["peer_u"].rearrange("l e d -> (l e) d"), A["peer_v"].rearrange("l e d -> (l e) d")

        @block.gpsimd
        def _(pool):
            pool.memset(same[:, :, :], 0.0).then_inc(filled, 1)
            pool.memset(row[:, :, :], 1.0).then_inc(filled, 1)
            pool.wait_ge(filled, 2)
            pool.affine_select(out=same[:, :, :], in_=same[:, :, :], compare_op=ALU.not_equal, fill=1.0, base=0,
                               pattern=[[1, TS], [-1, TS]], channel_multiplier=0).then_inc(made, 1)
            pool.affine_select(out=row[:, :, :], in_=row[:, :, :], compare_op=ALU.is_equal, fill=0.0, base=0,
                               pattern=[[-1, TS], [0, P]], channel_multiplier=1).then_inc(made, 1)
            pool.wait_ge(set_, 2)
            for b in range(TS):
                if b >= NB:
                    pool.wait_ge(dotted, b - NB + 1)
                pool.indirect_dma_start(u[:, b % NB, :], None, u_rows, bass.IndirectOffsetOnAxis(idsT[:, b:b + 1], 0)).then_inc(u_in[b % NB], 16)
                if b >= NB:
                    pool.wait_ge(mixed, b - NB + 1)
                pool.indirect_dma_start(v[:, b % NB, :], None, v_rows, bass.IndirectOffsetOnAxis(idsT[:, b:b + 1], 0)).then_inc(v_in[b % NB], 16)

        @block.tensor
        def _(pe):
            pe.transpose(psT[:, 0, :], ids_f[:, :], K["ident"][0:TS, 0:TS])
            pe.transpose(psT[:, 1, :], gate[:, :], K["ident"][0:TS, 0:TS]).then_inc(turned, 1)
            pe.wait_ge(made, 2)
            for b in range(TS + 1):
                if b < TS:
                    if b:
                        pe.wait_ge(dotted, b)
                    for c in range(2):
                        last = pe.matmul(psH[:, c, :], row[:, b, :], h2[:, c * 512:(c + 1) * 512], start=True, stop=True)
                    last.then_inc(h_spread, 1)
                if b:
                    pe.wait_ge(weighted, b)
                    pe.wait_ge(v_in[(b - 1) % NB], 16 * ((b - 1) // NB + 1))
                    for c in range(2):
                        last = pe.matmul(psY[:, c, :], coefs[:, b - 1, :], v[:, (b - 1) % NB, c * 512:(c + 1) * 512], start=(b == 1), stop=(b == TS), skip_group_check=True)
                    last.then_inc(mixed, 1)

        @block.scalar
        def _(act):
            for b in range(TS):
                act.wait_ge(dotted, b + 1)
                act.activation(coef[:, b:b + 1], coef[:, b:b + 1], ACT.Gelu).then_inc(gelued, 1)
            act.wait_ge(y_done, 1)
            act.dma_start(outs["y_s"].rearrange("b t d -> (b t) d"), y[:, :]).then_inc(stored, 16)
            act.wait_ge(stored, 16)

        @block.vector
        def _(dve):
            then = Chain(dve, chain)
            dve.wait_ge(turned, 1)
            dve.tensor_copy(idsT[:, :], psT[:, 0, :]).then_inc(set_, 1)
            dve.tensor_copy(gateT[:, :], psT[:, 1, :]).then_inc(set_, 1)
            dve.wait_ge(set_, 2)
            dve.wait_ge(made, 2)
            for b in range(TS):
                dve.wait_ge(h_spread, b + 1)
                dve.wait_ge(u_in[b % NB], 16 * (b // NB + 1))
                dve.tensor_tensor_reduce(u[:, b % NB, :], u[:, b % NB, :], psH[:, :, :].rearrange("p c n -> p (c n)"), 1.0, 0.0,
                                         ALU.mult, ALU.add, coef[:, b:b + 1]).then_inc(dotted, 1)
                dve.wait_ge(gelued, b + 1)
                then(dve.tensor_tensor(coef[:, b:b + 1], coef[:, b:b + 1], gateT[:, b:b + 1], ALU.mult))
                dve.tensor_scalar(coefs[:, b, :], same[:, b, :], coef[:, b:b + 1], None, ALU.mult).then_inc(weighted, 1)
            dve.wait_ge(mixed, TS)
            then(dve.tensor_tensor(y[:, :], psY[:, :, :].rearrange("p c n -> p (c n)"), K["ada"][0:TS, 5 * D:6 * D], ALU.mult))
            dve.tensor_tensor(y[:, :], y[:, :], x1, ALU.add).then_inc(y_done, 1)


def step(nc, A, outs, D_):
    with ExitStack() as whole:
        m = Mem(nc, whole, "all")
        K = {name: m.sb(name, shape) for name, shape in (
            ("ident", [P, P]), ("ones", [P, P]), ("bias", [P, P]), ("keep", [P, P]), ("swap", [ROPE, ROPE]),
            ("last", [TS + 1, P]), ("eps", [P, 1]), ("ada", [TS + 1, 6 * D]))}
        L = {"q_lat": m.sb("q_lat", [P, KL, TS, H]), "q_rope": m.sb("q_rope", [ROPE, TS, H]), "new": m.sb("new", [TS, TS, H]),
             "ckv_new": m.sb("ckv_new", [TS, LAT]), "o_lat": m.sb("o_lat", [P, TS, KL * H])}
        yT_s = m.sb("yT_s", [P, KI, TS])
        by_tile = lambda ap: ap.rearrange("t p d -> p t d")
        with ExitStack() as front:
            m = Mem(nc, front, "frt")
            constants(nc, K)
            conditioning(nc, A, K)
            with ExitStack() as part:
                part.enter_context(own_semaphores(nc))
                n = Mem(nc, part, "inp")
                x, hT = n.sb("x", [P, TT + 1, D]), n.sb("hT", [P, KD, T])
                modulated(nc, K, "mod1", [(x[:, 0:TT, :], A["x_prompt"].rearrange("b (t p) d -> p (b t) d", p=P)),
                                          (x[0:TS, TT, :], A["x_sample"].rearrange("b t d -> (b t) d"))],
                          x, A["g_mix"], 0, D, x, hT)
                projection(nc, A, hT, D_["proj"])
            oT = m.sb("oT", [P, H * T])
            with ExitStack() as part:
                part.enter_context(own_semaphores(nc))
                n = Mem(nc, part, "mla")
                M = {"ckvT": n.sb("ckvT", [P, KL, T]), "kpeT": n.sb("kpeT", [ROPE, T]), "kpe_sq": n.sb("kpe_sq", [ROPE, T]),
                     "ckv_s": L["ckv_new"], "cos": n.sb("cos", [ROPE, T]), "sin": n.sb("sin", [ROPE, T]),
                     "qs_n": n.sb("qs_n", [P, H * TS]), "qs_r": n.sb("qs_r", [ROPE, H * TS])}
                latents(nc, A, K, M, D_["proj"], outs)
                prompt_attention(nc, A, K, M, D_["proj"], oT)
                L["w_uk"] = n.sb("w_uk", [P, KL, H * NOPE])
                sample_queries(nc, A, K, M, L)
            S = {"x": m.sb("x", [P, KC, T]), "skip": m.sb("skip", [P, KI]), "g_ssm": m.sb("g_ssm", [P, KI])}
            with ExitStack() as part:
                part.enter_context(own_semaphores(nc))
                n = Mem(nc, part, "ssm")
                K["spread"] = n.sb("spread", [SH, DI])
                S.update({"dt": n.sb("dt", [SH, T]), "acs": n.sb("acs", [SH, T]), "a": n.sb("a", [SH, 1]), "decay_s": n.sb("decay_s", [SH, TS]),
                          "dt_tok": n.sb("dt_tok", [P, TT, SH]), "acs_tok": n.sb("acs_tok", [P, TT, SH])})
                head_channels(nc, K)
                skip_gains(nc, A, K, S)
                convolution(nc, A, K, S, D_["proj"], outs)
                time_steps(nc, A, K, S, D_["proj"], D_["acs"])
                prompt_scan(nc, A, K, S, D_["acs"], outs)
                sample_scan(nc, A, K, S, outs)
            gated_norm(nc, A, K, S, D_["proj"], yT_s)
            mT = m.sb("mT", [P, KD, TP])
            merge(nc, A, K, "mrg", D_["proj"], 0, TP, oT[:, :].rearrange("p (h t) -> p h t", h=H)[:, :, 0:TP], S["x"][:, 0:KI, 0:TP], mT)
            x1 = m.sb("x1", [P, TT, D])
            residual(nc, A, K, "res", [P] * TT, 2 * D, mT, A["x_prompt"].rearrange("b (t p) d -> p (b t) d", p=P), x1)
            store(nc, "sx1", [(by_tile(D_["x1"]), x1)])
        with ExitStack() as part:
            part.enter_context(own_semaphores(nc))
            m = Mem(nc, part, "exp")
            h2, h2T = m.sb("h2", [P, TT, D]), m.sb("h2T", [P, KD, TP])
            modulated(nc, K, "mod2", [(h2[:, :, :], by_tile(D_["x1"]))], h2, A["g_ffn"], 3 * D, 4 * D, h2, h2T, samples=False)
            ids, gate = m.sb("ids", [P, TT, SL], I32), m.sb("gate", [P, TT, SL])
            head = lambda tile: (lambda h: tile[:, :, h * TK:(h + 1) * TK])
            choose(nc, A, K, "chs", P, TT, TP, h2T, head(ids), head(gate))
            store(nc, "sh2", [(by_tile(D_["h2"]), h2), (by_tile(D_["ids"]), ids), (by_tile(D_["gate"]), gate)])
        with ExitStack() as part:
            part.enter_context(own_semaphores(nc))
            L["w_uk"] = Mem(nc, part, "mix0").sb("w_uk", [P, KL, H * NOPE])
            load(nc, "ldw", [(L["w_uk"], A["w_uk"].rearrange("l (k p) h d -> p (l k) (h d)", p=P))])
            attend_and_mix(nc, A, K, L, D_, outs)
        with ExitStack() as part:
            part.enter_context(own_semaphores(nc))
            m = Mem(nc, part, "smp")
            oT = m.sb("oT", [P, H, TS])
            sample_values(nc, A, K, L, oT)
            mT, x1, h2, h2T = m.sb("mT", [P, KD, TS]), m.sb("x1", [TS, 1, D]), m.sb("h2", [TS, 1, D]), m.sb("h2T", [P, KD, TS])
            merge(nc, A, K, "mgs", D_["proj"], TP, TS, oT, yT_s, mT)
            residual(nc, A, K, "rss", [TS], 2 * D, mT, A["x_sample"].rearrange("b (t a) d -> b (t a) d", a=1), x1)
            modulated(nc, K, "mod3", [], x1, A["g_ffn"], 3 * D, 4 * D, h2, h2T, prompt=False)
            ids, gate = m.sb("ids", [TS, SL]), m.sb("gate", [TS, SL])
            head = lambda tile: (lambda h: tile[:, h * TK:(h + 1) * TK].unsqueeze(1))
            choose(nc, A, K, "chz", TS, 1, TS, h2T, head(ids), head(gate))
            sample_experts(nc, A, K, h2[:, 0, :], x1[:, 0, :], ids, gate, outs)


def copies(nc, tag, pairs, name):
    with ExitStack() as ctx:
        done = Mem(nc, ctx, tag).sem(name)
        block = ctx.enter_context(nc.Block())

        @block.sync
        def _(sp):
            for to, of in pairs:
                sp.dma_start(to, of).then_inc(done, 16)
            sp.wait_ge(done, 16 * len(pairs))


def store(nc, tag, pairs):
    copies(nc, tag, [(to, of[:]) for to, of in pairs], "stored")


def load(nc, tag, pairs):
    copies(nc, tag, [(to[:], of) for to, of in pairs], "loaded")


_INS = ['x_prompt', 'x_sample', 'c_prompt', 'c_sample', 'cache_ckv', 'cache_kpe', 'page_table', 'state_conv', 'state_ssm',
        'w_ada', 'b_ada', 'g_mix', 'w_in', 'g_q', 'g_ckv', 'w_uk', 'w_uv', 'g_k', 'conv_w', 'conv_b', 'dt_bias', 'a_log',
        'd_skip', 'g_ssm', 'w_br_a', 'w_br_b', 'w_out', 'g_ffn', 'peer_wq', 'peer_keys1', 'peer_keys2', 'peer_u', 'peer_v']
_OUTS = [('y_p', (1, TP, D)), ('y_s', (TS, 1, D)), ('ckv_p', (1, 1, TP, LAT)), ('kpe_p', (1, 1, TP, ROPE)),
         ('conv_p', (1, 1, CW - 1, CD)), ('ssm_p', (1, 1, SH, HD, N)), ('ckv_s', (1, TS, 1, LAT)), ('kpe_s', (1, TS, 1, ROPE)),
         ('conv_s', (1, TS, CW - 1, CD)), ('ssm_s', (1, TS, SH, HD, N))]


def rope_tables():
    half = ROPE // 2
    pos = np.concatenate([np.arange(TP), np.full(TS, PAST)]).astype(np.float32)
    inv = (10000.0 ** (-np.arange(half) / half)).astype(np.float32)
    angle = np.tile(inv[:, None] * pos[None, :], (2, 1))
    return np.cos(angle).astype(np.float32), np.sin(angle).astype(np.float32)


def kernel(**inputs):
    import numpy as _np
    import concourse.bacc as _bacc
    from concourse import mybir as _mybir
    from concourse.bass_utils import run_bass_kernel_spmd as _run

    nc = _bacc.Bacc("TRN2", target_bir_lowering=False, num_devices=1)
    arrays, A = {}, {}

    def give(name, a):
        arrays[f"in_{name}"] = a
        A[name] = nc.dram_tensor(f"in_{name}", a.shape, _mybir.dt.from_np(a.dtype), kind="ExternalInput").ap()

    for name in _INS:
        give(name, _np.ascontiguousarray(inputs[name]))
    cos, sin = rope_tables()
    give("rope_cos", cos)
    give("rope_sin", sin)
    outs = {name: nc.dram_tensor(f"out_{name}", shape, F32, kind="ExternalOutput").ap() for name, shape in _OUTS}
    D_ = {name: nc.dram_tensor(f"keep_{name}", shape, dt, kind="Internal").ap() for name, shape, dt in (
        ("proj", (2 * PAIRS, P, T), F32), ("acs", (SH, TP), F32), ("x1", (TT, P, D), F32), ("h2", (TT, P, D), F32),
        ("ids", (TT, P, SL), I32), ("gate", (TT, P, SL), F32))}
    step(nc, A, outs, D_)
    r = _run(nc, [arrays], core_ids=[0])
    return tuple(r.results[0][f"out_{name}"] for name, _ in _OUTS)
```

```python
from contextlib import ExitStack, contextmanager

import numpy as np

import concourse.bass as bass
from concourse import mybir

F32 = mybir.dt.float32
I32 = mybir.dt.int32
F32R = mybir.dt.float32r
U32 = mybir.dt.uint32
ALU = mybir.AluOpType
ACT = mybir.ActivationFunctionType
X = mybir.AxisListType.X

P = 128
D = 1024
KD = D // P
TP = 512
TS = 8
T = TP + TS
TT = TP // P
H = 8
NOPE, ROPE, DV, LAT = 128, 64, 128, 512
DQK = NOPE + ROPE
KL = LAT // P
PAST, PAGE = 2048, 128
NT = PAST // PAGE
DI, HD, SH, G, N = 2048, 64, 32, 4, 128
KI = DI // P
CD = DI + 2 * G * N
KC = CD // P
CW = 4
PH, NK, DK, TK = 8, 128, 256, 16
SL = PH * TK
IN = H * DQK + LAT + ROPE + DI + CD + SH + 2 * D
EPS = 1e-6
HALF = T // 2
NEG = -1e30

C_Q, C_CKV, C_KPE, C_Z, C_XBC, C_DT, C_GA, C_GB = 0, 12, 16, 17, 33, 57, 58, 66


class Chain:

    def __init__(self, eng, sem):
        self.eng, self.sem, self.n = eng, sem, 0

    def __call__(self, ins):
        self.n += 1
        ins.then_inc(self.sem, 1)
        self.eng.wait_ge(self.sem, self.n)


class Mem:

    def __init__(self, nc, ctx, tag):
        self.nc, self.ctx, self.tag = nc, ctx, tag

    def sb(self, name, shape, dt=F32):
        return self.ctx.enter_context(self.nc.sbuf_tensor(f"{self.tag}_{name}", shape, dt))

    def ps(self, name, shape, dt=F32):
        return self.ctx.enter_context(self.nc.psum_tensor(f"{self.tag}_{name}", shape, dt))

    def sem(self, name):
        return self.nc.alloc_semaphore(f"{self.tag}_{name}")


@contextmanager
def own_semaphores(nc):
    before = nc.snapshot_sems()
    yield
    nc.clear_and_free_semaphores(nc.allocated_since(before))
    nc.all_engine_barrier()


def rows(t):
    return P if t < TT else TS


def constants(nc, K):
    with ExitStack() as ctx:
        m = Mem(nc, ctx, "cst")
        filled, made = m.sem("filled"), m.sem("made")
        block = ctx.enter_context(nc.Block())

        @block.gpsimd
        def _(pool):
            for tile, value in ((K["ident"], 0.0), (K["ones"], 1.0), (K["bias"], 0.0), (K["keep"], 1.0),
                                (K["swap"], 0.0), (K["last"], 0.0), (K["eps"], EPS)):
                pool.memset(tile[:], value).then_inc(filled, 1)
            pool.wait_ge(filled, 7)
            pool.affine_select(out=K["ident"][:, :], in_=K["ident"][:, :], compare_op=ALU.not_equal, fill=1.0,
                               base=0, pattern=[[-1, P]], channel_multiplier=1).then_inc(made, 1)
            pool.affine_select(out=K["bias"][:, :], in_=K["bias"][:, :], compare_op=ALU.is_ge, fill=NEG,
                               base=0, pattern=[[-1, P]], channel_multiplier=1).then_inc(made, 1)
            pool.affine_select(out=K["keep"][:, :], in_=K["keep"][:, :], compare_op=ALU.is_ge, fill=0.0,
                               base=0, pattern=[[1, P]], channel_multiplier=-1).then_inc(made, 1)
            pool.affine_select(out=K["swap"][:, :], in_=K["swap"][:, :], compare_op=ALU.not_equal, fill=-1.0,
                               base=-ROPE // 2, pattern=[[-1, ROPE]], channel_multiplier=1).then_inc(made, 1)
            pool.affine_select(out=K["last"][:, :], in_=K["last"][:, :], compare_op=ALU.not_equal, fill=1.0,
                               base=-TS, pattern=[[0, P]], channel_multiplier=1).then_inc(made, 1)
            pool.wait_ge(made, 5)
            pool.affine_select(out=K["swap"][:, :], in_=K["swap"][:, :], compare_op=ALU.not_equal, fill=1.0,
                               base=ROPE // 2, pattern=[[-1, ROPE]], channel_multiplier=1).then_inc(made, 1)
            pool.wait_ge(made, 6)


def head_channels(nc, K):
    with ExitStack() as ctx:
        m = Mem(nc, ctx, "hch")
        made = m.sem("made")
        block = ctx.enter_context(nc.Block())

        @block.gpsimd
        def _(pool):
            pool.memset(K["spread"][:, :], 1.0).then_inc(made, 1)
            pool.wait_ge(made, 1)
            pool.affine_select(out=K["spread"][:, :], in_=K["spread"][:, :], compare_op=ALU.is_ge, fill=0.0,
                               base=0, pattern=[[1, DI]], channel_multiplier=-HD).then_inc(made, 1)
            pool.wait_ge(made, 2)
            pool.affine_select(out=K["spread"][:, :], in_=K["spread"][:, :], compare_op=ALU.is_ge, fill=0.0,
                               base=HD - 1, pattern=[[-1, DI]], channel_multiplier=HD)


def conditioning(nc, A, K):
    NG = 6 * D // 512
    with ExitStack() as ctx:
        m = Mem(nc, ctx, "ada")
        c_rows, cT = m.sb("c_rows", [TS + 1, D]), m.sb("cT", [P, KD, TS + 1])
        bias = m.sb("bias", [TS + 1, 6 * D])
        w = m.sb("w", [P, 2, KD, 512])
        psT, psA = m.ps("psT", [P, KD, TS + 1]), m.ps("psA", [TS + 1, 2, 512])
        c_in, bias_in = m.sem("c_in"), m.sem("bias_in")
        w_in = [m.sem(f"w_in{b}") for b in range(2)]
        turned, cT_ready = m.sem("turned"), m.sem("cT_ready")
        summed = [m.sem(f"summed{b}") for b in range(2)]
        added = [m.sem(f"added{b}") for b in range(2)]
        block = ctx.enter_context(nc.Block())
        w_view = A["w_ada"].rearrange("l (k p) n -> p (l k) n", p=P)

        @block.sync
        def _(sp):
            sp.dma_start(c_rows[0:TS, :], A["c_sample"]).then_inc(c_in, 16)
            sp.dma_start(c_rows[TS:TS + 1, :], A["c_prompt"]).then_inc(c_in, 16)
            sp.dma_start(bias[:, :], A["b_ada"].to_broadcast([TS + 1, 6 * D])).then_inc(bias_in, 16)
            with sp.Fori(0, NG // 2) as i:
                for b in range(2):
                    sp.wait_ge(summed[b], i)
                    sp.dma_start(w[:, b], w_view[:, :, bass.ds(i * 1024 + b * 512, 512)]).then_inc(w_in[b], 16)

        @block.tensor
        def _(pe):
            pe.wait_ge(c_in, 32)
            for k in range(KD):
                last = pe.transpose(psT[:, k, :], c_rows[:, k * P:(k + 1) * P], K["ident"][0:TS + 1, 0:TS + 1])
            last.then_inc(turned, 1)
            pe.wait_ge(cT_ready, 1)
            with pe.Fori(0, NG // 2) as i:
                for b in range(2):
                    pe.wait_ge(w_in[b], i * 16 + 16)
                    pe.wait_ge(added[b], i)
                    for k in range(KD):
                        last = pe.matmul(psA[:, b, :], cT[:, k, :], w[:, b, k, :], start=(k == 0), stop=(k == KD - 1))
                    last.then_inc(summed[b], 1)

        @block.vector
        def _(dve):
            dve.wait_ge(turned, 1)
            dve.tensor_copy(cT[:, :, :], psT[:, :, :]).then_inc(cT_ready, 1)
            dve.wait_ge(bias_in, 16)
            with dve.Fori(0, NG // 2) as i:
                for b in range(2):
                    dve.wait_ge(summed[b], i + 1)
                    at = bass.ds(i * 1024 + b * 512, 512)
                    dve.tensor_tensor(K["ada"][:, at], psA[:, b, :], bias[:, at], ALU.add).then_inc(added[b], 1)


def modulated(nc, K, tag, load, x, gain, shift_at, scale_at, out, outT, prompt=True, samples=True):
    NP = TT if prompt else 0
    tiles = [P] * NP + [TS] * samples
    NA = len(tiles)
    halves = isinstance(outT, tuple)
    with ExitStack() as ctx:
        m = Mem(nc, ctx, tag)
        gain_bc = m.sb("gain", [P, D])
        mul_p, add_p, mul_s = m.sb("mul_p", [P, D]), m.sb("add_p", [P, D]), m.sb("mul_s", [TS, D])
        squares = m.sb("squares", [P, D])
        ss, ms, rms, rstd = (m.sb(n, [P, NA]) for n in ("ss", "ms", "rms", "rstd"))
        psB = m.ps("psB", [P, 4, 512])
        psT = m.ps("psT", [P, 2, 4, P])
        x_in, gain_in, spread = m.sem("x_in"), m.sem("gain_in"), m.sem("spread")
        summed, meaned, rooted = m.sem("summed"), m.sem("meaned"), m.sem("rooted")
        rounded = m.sem("rounded")
        normed, turned, copied, chain = m.sem("normed"), m.sem("turned"), m.sem("copied"), m.sem("chain")
        stats = [(P, slice(0, NP))] * prompt + [(TS, slice(NP, NA))] * samples
        block = ctx.enter_context(nc.Block())

        @block.sync
        def _(sp):
            sp.dma_start(gain_bc[:, :], gain.to_broadcast([P, D])).then_inc(gain_in, 16)
            for dst, src in load:
                sp.dma_start(dst, src).then_inc(x_in, 16)

        @block.scalar
        def _(act):
            act.wait_ge(x_in, 16 * len(load)) if load else None
            for t, n in enumerate(tiles):
                if t:
                    act.wait_ge(summed, t)
                act.activation(squares[0:n, :], x[0:n, t, :], ACT.Square, accum_out=ss[0:n, t:t + 1]).then_inc(summed, 1)
            act.wait_ge(meaned, len(stats))
            for n, cols in stats:
                act.activation(rms[0:n, cols], ms[0:n, cols], ACT.Sqrt).then_inc(rooted, 1)
            for j in range(2 * NA if halves else 0):
                t, c = j // 2, j % 2
                act.wait_ge(turned, j + 1)
                act.activation(outT[0][:, 4 * c:4 * c + 4, t * P:t * P + tiles[t]], psT[:, j % 2, :, 0:tiles[t]], ACT.Copy).then_inc(rounded, 1)

        @block.tensor
        def _(pe):
            for j, at in enumerate((shift_at, scale_at)):
                for c in range(2):
                    last = pe.matmul(psB[:, 2 * j + c, :], K["last"][:, :], K["ada"][:, at + c * 512:at + (c + 1) * 512],
                                     start=True, stop=True)
            last.then_inc(spread, 1)
            for t, n in enumerate(tiles):
                pe.wait_ge(normed, t + 1)
                for c in range(2):
                    j = 2 * t + c
                    if j >= 2:
                        pe.wait_ge(copied, j - 1)
                    for k in range(4):
                        last = pe.transpose(psT[:, j % 2, k, 0:n], out[0:n, t, (4 * c + k) * P:(4 * c + k + 1) * P],
                                            K["ident"][0:n, 0:n])
                    last.then_inc(turned, 1)

        @block.vector
        def _(dve):
            then = Chain(dve, chain)
            dve.wait_ge(gain_in, 16)
            dve.wait_ge(spread, 1)
            dve.tensor_copy(add_p[:, :].rearrange("p (c n) -> p c n", c=2), psB[:, 0:2, :])
            dve.scalar_tensor_tensor(mul_p[:, :].rearrange("p (c n) -> p c n", c=2), psB[:, 2:4, :], 1.0,
                                     gain_bc[:, :].rearrange("p (c n) -> p c n", c=2), ALU.add, ALU.mult)
            dve.scalar_tensor_tensor(mul_s[:, :], K["ada"][0:TS, scale_at:scale_at + D], 1.0, gain_bc[0:TS, :],
                                     ALU.add, ALU.mult)
            dve.wait_ge(summed, NA)
            for n, cols in stats:
                dve.tensor_scalar(ms[0:n, cols], ss[0:n, cols], 1.0 / D, EPS, ALU.mult, ALU.add).then_inc(meaned, 1)
            dve.wait_ge(rooted, len(stats))
            for n, cols in stats:
                then(dve.reciprocal(rstd[0:n, cols], rms[0:n, cols]))

            def copy(j):
                t, c = j // 2, j % 2
                n = tiles[t]
                place = (slice(None), slice(4 * c, 4 * c + 4), slice(t * P, t * P + n))
                if halves:
                    lower(dve, outT[0][place], outT[1][place], psT[:, j % 2, :, 0:n], rounded, copied, j + 1)
                else:
                    dve.wait_ge(turned, j + 1)
                    dve.tensor_copy(outT[place], psT[:, j % 2, :, 0:n]).then_inc(copied, 1)

            for t, n in enumerate(tiles):
                mul, add = (mul_p, add_p[:, :]) if t < NP else (mul_s, K["ada"][0:TS, shift_at:shift_at + D])
                then(dve.scalar_tensor_tensor(out[0:n, t, :], x[0:n, t, :], rstd[0:n, t:t + 1], mul[0:n, :],
                                              ALU.mult, ALU.mult))
                dve.tensor_tensor(out[0:n, t, :], out[0:n, t, :], add, ALU.add).then_inc(normed, 1)
                if t:
                    copy(2 * t - 2)
                    copy(2 * t - 1)
            copy(2 * NA - 2)
            copy(2 * NA - 1)


def lower(dve, hi, lo, x, hi_made, lo_made, value):
    dve.wait_ge(hi_made, value)
    dve.tensor_tensor(lo, x, hi.bitcast(F32), ALU.subtract).then_inc(lo_made, 1)


def products(pe, out, w_parts, x_parts, first, last):
    (w_hi, w_lo), (x_hi, x_lo) = w_parts, x_parts
    pe.matmul(out, w_hi, x_hi, start=first, stop=False)
    pe.matmul(out, w_hi, x_lo, start=False, stop=False)
    return pe.matmul(out, w_lo, x_hi, start=False, stop=last)


def weights_in(sp, w, w_view, w_in, lowered, columns):
    for c, at in enumerate(columns):
        if c >= 2:
            sp.wait_ge(lowered, c - 1)
        sp.dma_start(w[:, c % 2], w_view[:, :, at:at + P]).then_inc(w_in[c % 2], 16)


def round_weights(pool, w, w_hi, w_in, multiplied, rounded, c):
    pool.wait_ge(w_in[c % 2], 16 * (c // 2 + 1))
    if c >= 4:
        pool.wait_ge(multiplied, c - 3)
    pool.tensor_copy(w_hi[:, c % 4], w[:, c % 2]).then_inc(rounded, 1)


def chunk_product(pe, out, c, w_hi, w_lo, h_hi, h_lo):
    for k in range(KD):
        for s in range(2):
            cols = slice(s * HALF, (s + 1) * HALF)
            last = products(pe, out[:, s, 0:HALF], (w_hi[:, c % 4, k, :], w_lo[:, c % 4, k, :]),
                            (h_hi[:, k, cols], h_lo[:, k, cols]), k == 0, k == KD - 1)
    return last


def chunks_from(first, n):
    return [first + P * j for j in range(n)]


def projection(nc, A, h_hi, h_lo, proj):
    GATES = 2 * D // P
    with ExitStack() as ctx:
        m = Mem(nc, ctx, "prj")
        w, w_hi, w_lo = m.sb("w", [P, 2, KD, P]), m.sb("w_hi", [P, 4, KD, P], F32R), m.sb("w_lo", [P, 4, KD, P], F32R)
        out = m.sb("out", [P, 2, T])
        ps = m.ps("ps", [P, 2, 2, 512])
        w_in, stored = ([m.sem(f"{n}{b}") for b in range(2)] for n in ("w_in", "stored"))
        rounded, lowered, multiplied, drained = (m.sem(n) for n in ("rounded", "lowered", "multiplied", "drained"))
        block = ctx.enter_context(nc.Block())
        w_view = A["w_in"].rearrange("l (k p) n -> p (l k) n", p=P)
        columns = chunks_from(IN - 2 * D, GATES)

        @block.sync
        def _(sp):
            weights_in(sp, w, w_view, w_in, lowered, columns)

        @block.gpsimd
        def _(pool):
            for c in range(GATES):
                round_weights(pool, w, w_hi, w_in, multiplied, rounded, c)

        @block.vector
        def _(dve):
            for c in range(GATES):
                lower(dve, w_hi[:, c % 4], w_lo[:, c % 4], w[:, c % 2], rounded, lowered, c + 1)

        @block.tensor
        def _(pe):
            for c in range(GATES):
                pe.wait_ge(lowered, c + 1)
                if c >= 2:
                    pe.wait_ge(drained, c - 1)
                chunk_product(pe, ps[:, c % 2], c, w_hi, w_lo, h_hi, h_lo).then_inc(multiplied, 1)

        @block.scalar
        def _(act):
            for c in range(GATES):
                act.wait_ge(multiplied, c + 1)
                if c >= 2:
                    act.wait_ge(stored[c % 2], 16 * (c // 2))
                act.activation(out[:, c % 2].rearrange("p (s t) -> p s t", s=2), ps[:, c % 2, :, 0:HALF], ACT.Copy).then_inc(drained, 1)
                act.wait_ge(drained, c + 1)
                act.dma_start(proj[C_GA + c], out[:, c % 2]).then_inc(stored[c % 2], 16)
            for b in range(2):
                act.wait_ge(stored[b], 16 * (GATES // 2))


SCALE = float(DQK) ** -0.5


class Steps:

    def __init__(self, eng, sem, n, turn):
        self.eng, self.sem, self.size, self.base, self.n = eng, sem, n, turn * n, 0

    def __call__(self, ins):
        self.n += 1
        ins.then_inc(self.sem, 1)
        self.eng.wait_ge(self.sem, self.base + self.n)

    def full(self):
        assert self.n == self.size, self.n


def latents(nc, A, K, M, proj, outs):
    with ExitStack() as ctx:
        m = Mem(nc, ctx, "lat")
        raw, sq = m.sb("raw", [P, KL, T]), m.sb("sq", [P, KL, T])
        rstd, turned = m.sb("rstd", [P, 2, HALF]), m.sb("turned", [ROPE, 2, HALF])
        gain = m.sb("gain", [P, KL])
        by_token, kpe_by_token = m.sb("by_token", [P, 2, LAT]), m.sb("kpe_by_token", [P, 2, ROPE])
        psN, psR = m.ps("psN", [P, 2, 512]), m.ps("psR", [ROPE, 2, 512])
        psT, psK = m.ps("psT", [P, 2, 512]), m.ps("psK", [P, 2, 512])
        raw_in, squared, summed, swapped = m.sem("raw_in"), m.sem("squared"), m.sem("summed"), m.sem("swapped")
        rooted, ready, chain = m.sem("rooted"), m.sem("ready"), m.sem("chain")
        moved, copied = m.sem("moved"), m.sem("copied")
        stored = [m.sem(f"stored{b}") for b in range(2)]
        block = ctx.enter_context(nc.Block())
        flat = proj.rearrange("c p t -> (c p) t")
        halves = lambda ap: ap.rearrange("p (s t) -> p s t", s=2)

        @block.sync
        def _(sp):
            sp.dma_start(raw[:, :, :], proj[C_CKV:C_CKV + KL].rearrange("c p t -> p c t")).then_inc(raw_in, 16)
            sp.dma_start(M["kpeT"][:, :], proj[C_KPE, 0:ROPE, :]).then_inc(raw_in, 16)
            sp.dma_start(gain[:, :], A["g_ckv"].rearrange("l (k p) -> p (l k)", p=P), allow_slow_non_contiguous=True).then_inc(raw_in, 16)
            sp.dma_start(M["cos"][:, :], A["rope_cos"]).then_inc(raw_in, 16)
            sp.dma_start(M["sin"][:, :], A["rope_sin"]).then_inc(raw_in, 16)
            for t in range(TT + 1):
                n, b = rows(t), t % 2
                sp.wait_ge(copied, 2 * t + 2)
                where = (outs["ckv_p"][0, 0, t * P:t * P + n, :], outs["kpe_p"][0, 0, t * P:t * P + n, :]) if t < TT else \
                    (outs["ckv_s"][0, :, 0, :], outs["kpe_s"][0, :, 0, :])
                sp.dma_start(where[0], by_token[0:n, b, :]).then_inc(stored[b], 16)
                sp.dma_start(where[1], kpe_by_token[0:n, b, :]).then_inc(stored[b], 16)
            sp.wait_ge(stored[0], 96)
            sp.wait_ge(stored[1], 64)

        @block.scalar
        def _(act):
            act.wait_ge(raw_in, 80)
            act.activation(sq[:, :, :], raw[:, :, :], ACT.Square).then_inc(squared, 1)
            act.wait_ge(summed, 1)
            act.activation(rstd[:, :, :], psN[:, :, 0:HALF], ACT.Sqrt, scale=1.0 / LAT, bias=K["eps"][:, :]).then_inc(rooted, 1)
            act.wait_ge(ready, 1)
            act.activation(M["kpe_sq"][:, :], M["kpeT"][:, :], ACT.Square).then_inc(rooted, 1)

        @block.tensor
        def _(pe):
            pe.wait_ge(raw_in, 80)
            for s in range(2):
                last = pe.matmul(psR[:, s, 0:HALF], K["swap"][:, :], M["kpeT"][:, s * HALF:(s + 1) * HALF], start=True, stop=True)
            last.then_inc(swapped, 1)
            pe.wait_ge(squared, 1)
            for s in range(2):
                for k in range(KL):
                    last = pe.matmul(psN[:, s, 0:HALF], K["ones"][:, :], sq[:, k, s * HALF:(s + 1) * HALF],
                                     start=(k == 0), stop=(k == KL - 1))
            last.then_inc(summed, 1)
            pe.wait_ge(ready, 2)
            for t in range(TT + 1):
                n, b = rows(t), t % 2
                if t >= 2:
                    pe.wait_ge(copied, 2 * t - 2)
                for k in range(KL):
                    pe.transpose(psT[0:n, b, k * P:(k + 1) * P], M["ckvT"][:, k, t * P:t * P + n], K["ident"][:, :])
                pe.transpose(psK[0:n, b, 0:ROPE], M["kpeT"][:, t * P:t * P + n], K["ident"][0:ROPE, 0:ROPE]).then_inc(moved, 1)

        @block.vector
        def _(dve):
            then = Chain(dve, chain)
            dve.wait_ge(raw_in, 80)
            dve.wait_ge(swapped, 1)
            dve.tensor_tensor(turned[:, :, :], psR[:, :, 0:HALF], halves(M["sin"][:, :]), ALU.mult)
            then(dve.tensor_tensor(M["kpeT"][:, :], M["kpeT"][:, :], M["cos"][:, :], ALU.mult))
            dve.tensor_tensor(halves(M["kpeT"][:, :]), halves(M["kpeT"][:, :]), turned[:, :, :], ALU.add).then_inc(ready, 1)
            dve.wait_ge(rooted, 1)
            then(dve.reciprocal(rstd[:, :, :], rstd[:, :, :]))
            for k in range(KL):
                last = dve.scalar_tensor_tensor(halves(M["ckvT"][:, k, :]), halves(raw[:, k, :]), gain[:, k:k + 1],
                                                rstd[:, :, :], ALU.mult, ALU.mult)
            last.then_inc(ready, 1)
            for t in range(TT + 1):
                n, b = rows(t), t % 2
                dve.wait_ge(moved, t + 1)
                if t >= 2:
                    dve.wait_ge(stored[b], 32 * (t // 2))
                dve.tensor_copy(by_token[0:n, b, :], psT[0:n, b, :]).then_inc(copied, 1)
                dve.tensor_copy(kpe_by_token[0:n, b, :], psK[0:n, b, 0:ROPE]).then_inc(copied, 1)
                if t == TT:
                    dve.wait_ge(copied, 2 * t + 2)
                    dve.tensor_copy(M["ckv_s"][:, :], by_token[0:n, b, :])


def prompt_attention(nc, A, K, M, proj, oT):
    with ExitStack() as ctx:
        m = Mem(nc, ctx, "att")
        q_n, q_r = m.sb("q_n", [P, 2, T]), m.sb("q_r", [ROPE, 2, T])
        w_uk, w_uv = m.sb("w_uk", [P, 2, KL, NOPE]), m.sb("w_uv", [P, 2, KL, DV])
        turned, sq_n, sq_r = m.sb("turned", [ROPE, T]), m.sb("sq_n", [P, T]), m.sb("sq_r", [ROPE, T])
        sq_k = m.sb("sq_k", [P, TP])
        root_q, root_k = m.sb("root_q", [P, T]), m.sb("root_k", [P, TP])
        k_n, k_r, v = m.sb("k_n", [P, TP]), m.sb("k_r", [ROPE, TP]), m.sb("v", [P, TT, DV])
        probs, probsT = m.sb("probs", [P, TT, TP]), m.sb("probsT", [P, 2, TT, P])
        top, shift, total, share = (m.sb(n, [P, TT]) for n in ("top", "shift", "total", "share"))
        bank = [m.ps(f"bank{b}", [P, 512]) for b in range(8)]
        psV, psT, psO = bank[4], bank[5:7], bank[7]
        gq_n, gq_r, gk_n, gk_r = m.sb("gq_n", [P, 1]), m.sb("gq_r", [ROPE, 1]), m.sb("gk_n", [P, 1]), m.sb("gk_r", [ROPE, 1])
        gains_in, chain = m.sem("gains_in"), m.sem("chain")
        head_in = [m.sem(f"head_in{b}") for b in range(2)]
        head_done = [m.sem(f"head_done{b}") for b in range(2)]
        (swapped, keyed, valued, q_sq, r_roped, r_sq, k_sq, q_summed, k_summed, q_rooted, k_rooted, prepared, v_copied,
         scored, shifted, exped, shared, turned_p, copied_p, weighed) = (m.sem(n) for n in (
             "swapped", "keyed", "valued", "q_sq", "r_roped", "r_sq", "k_sq", "q_summed", "k_summed", "q_rooted",
             "k_rooted", "prepared", "v_copied", "scored", "shifted", "exped", "shared", "turned_p", "copied_p", "weighed"))
        block = ctx.enter_context(nc.Block())
        q_view = proj.rearrange("c p t -> (c p) t")

        def heads(eng, body):
            with eng.Fori(0, H // 2) as i:
                for b in range(2):
                    body(i, b, i * 2 + b)

        @block.sync
        def _(sp):
            for tile, src in ((gq_n, A["g_q"][0, 0:NOPE]), (gq_r, A["g_q"][0, NOPE:DQK]),
                              (gk_n, A["g_k"][0, 0:NOPE]), (gk_r, A["g_k"][0, NOPE:DQK])):
                sp.dma_start(tile[:, :], src.rearrange("(p a) -> p a", a=1)).then_inc(gains_in, 16)

            def load(i, b, h):
                sp.wait_ge(head_done[b], i)
                sp.dma_start(q_n[:, b, :], q_view[bass.ds(h * DQK, NOPE), :]).then_inc(head_in[b], 16)
                sp.dma_start(q_r[:, b, :], q_view[bass.ds(h * DQK + NOPE, ROPE), :]).then_inc(head_in[b], 16)
                sp.dma_start(w_uk[:, b], A["w_uk"].rearrange("l (k p) h d -> p (l k) (h d)", p=P)[:, :, bass.ds(h * NOPE, NOPE)]).then_inc(head_in[b], 16)
                sp.dma_start(w_uv[:, b], A["w_uv"].rearrange("l (k p) h d -> p (l k) (h d)", p=P)[:, :, bass.ds(h * DV, DV)]).then_inc(head_in[b], 16)
            heads(sp, load)

        @block.tensor
        def _(pe):
            def head(i, b, h):
                pe.wait_ge(head_in[b], i * 64 + 64)
                pe.wait_ge(exped, h * TT)
                for k in range(KL):
                    last = pe.matmul(bank[2][:, :], w_uk[:, b, k, :], M["ckvT"][:, k, 0:TP], start=(k == 0), stop=(k == KL - 1))
                last.then_inc(keyed, 1)
                for s in range(2):
                    last = pe.matmul(bank[s][0:ROPE, 0:HALF], K["swap"][:, :], q_r[:, b, s * HALF:(s + 1) * HALF], start=True, stop=True)
                last.then_inc(swapped, 1)
                pe.wait_ge(v_copied, h)
                for t in range(TT):
                    for k in range(KL):
                        last = pe.matmul(psV[:, t * DV:(t + 1) * DV], M["ckvT"][:, k, t * P:(t + 1) * P], w_uv[:, b, k, :],
                                         start=(k == 0), stop=(k == KL - 1))
                last.then_inc(valued, 1)
                pe.wait_ge(k_sq, h + 1)
                pe.matmul(bank[3][:, :], K["ones"][:, :], sq_k[:, :], start=True, stop=False)
                pe.matmul(bank[3][:, :], K["ones"][0:ROPE, :], M["kpe_sq"][:, 0:TP], start=False, stop=True).then_inc(k_summed, 1)
                pe.wait_ge(q_sq, h + 1)
                pe.wait_ge(r_sq, h + 1)
                for s in range(2):
                    pe.matmul(bank[s][:, 0:HALF], K["ones"][:, :], sq_n[:, s * HALF:(s + 1) * HALF], start=True, stop=False)
                    last = pe.matmul(bank[s][:, 0:HALF], K["ones"][0:ROPE, :], sq_r[:, s * HALF:(s + 1) * HALF], start=False, stop=True)
                last.then_inc(q_summed, 1)
                pe.wait_ge(prepared, h + 1)
                for q in range(TT):
                    w = (q + 1) * P
                    pe.matmul(bank[q][:, 0:w], q_n[:, b, q * P:w], k_n[:, 0:w], start=True, stop=False)
                    pe.matmul(bank[q][:, 0:w], q_r[:, b, q * P:w], k_r[:, 0:w], start=False, stop=True).then_inc(scored, 1)

                def turn(q):
                    pe.wait_ge(shared, h * TT + (q + 1))
                    if q >= 2:
                        pe.wait_ge(copied_p, h * TT + (q - 1))
                    for k in range(q + 1):
                        last = pe.transpose(psT[q % 2][:, k * P:(k + 1) * P], probs[:, q, k * P:(k + 1) * P], K["ident"][:, :])
                    last.then_inc(turned_p, 1)

                def weigh(q):
                    pe.wait_ge(copied_p, h * TT + (q + 1))
                    if q == 0:
                        pe.wait_ge(v_copied, h + 1)
                        pe.wait_ge(head_done[1 - b], i + b)
                    for k in range(q + 1):
                        last = pe.matmul(psO[:, q * P:(q + 1) * P], v[:, k, :], probsT[:, q % 2, k, :], start=(k == 0), stop=(k == q))
                    last.then_inc(weighed, 1)

                turn(0)
                turn(1)
                weigh(0)
                turn(2)
                weigh(1)
                turn(3)
                weigh(2)
                weigh(3)
            heads(pe, head)

        @block.scalar
        def _(act):
            def head(i, b, h):
                act.wait_ge(head_in[b], i * 64 + 64)
                act.activation(sq_n[:, :], q_n[:, b, :], ACT.Square).then_inc(q_sq, 1)
                act.wait_ge(keyed, h + 1)
                act.activation(sq_k[:, :], bank[2][:, :], ACT.Square).then_inc(k_sq, 1)
                act.wait_ge(r_roped, h + 1)
                act.activation(sq_r[:, :], q_r[:, b, :], ACT.Square).then_inc(r_sq, 1)
                act.wait_ge(k_summed, h + 1)
                act.activation(root_k[:, :], bank[3][:, :], ACT.Sqrt, scale=1.0 / DQK, bias=K["eps"][:, :]).then_inc(k_rooted, 1)
                act.wait_ge(q_summed, h + 1)
                for s in range(2):
                    act.activation(root_q[:, s * HALF:(s + 1) * HALF], bank[s][:, 0:HALF], ACT.Sqrt, scale=1.0 / DQK,
                                   bias=K["eps"][:, :]).then_inc(q_rooted, 1)
                act.wait_ge(valued, h + 1)
                act.activation(v[:, :, :].rearrange("p t d -> p (t d)"), psV[:, :], ACT.Copy).then_inc(v_copied, 1)
                for q in range(TT):
                    w = (q + 1) * P
                    act.wait_ge(shifted, h * TT + (q + 1))
                    act.activation(probs[:, q, 0:w], bank[q][:, 0:w], ACT.Exp, bias=shift[:, q:q + 1], scale=SCALE,
                                   accum_out=total[:, q:q + 1]).then_inc(exped, 1)
                for q in range(TT):
                    w = (q + 1) * P
                    act.wait_ge(turned_p, h * TT + (q + 1))
                    if q >= 2:
                        act.wait_ge(weighed, h * TT + (q - 1))
                    act.activation(probsT[:, q % 2, 0:q + 1, :].rearrange("p k q -> p (k q)"), psT[q % 2][:, 0:w], ACT.Copy).then_inc(copied_p, 1)
            heads(act, head)

        @block.vector
        def _(dve):
            dve.wait_ge(gains_in, 64)

            def head(i, b, h):
                then = Steps(dve, chain, 15, h)
                dve.wait_ge(head_in[b], i * 64 + 64)
                dve.wait_ge(swapped, h + 1)
                for s in range(2):
                    dve.tensor_tensor(turned[:, s * HALF:(s + 1) * HALF], bank[s][0:ROPE, 0:HALF], M["sin"][:, s * HALF:(s + 1) * HALF], ALU.mult)
                then(dve.tensor_tensor(q_r[:, b, :], q_r[:, b, :], M["cos"][:, :], ALU.mult))
                then(dve.tensor_tensor(q_r[:, b, :], q_r[:, b, :], turned[:, :], ALU.add))
                dve.sem_inc(r_roped, 1)
                dve.wait_ge(k_rooted, h + 1)
                then(dve.reciprocal(root_k[:, :], root_k[:, :]))
                dve.scalar_tensor_tensor(k_n[:, :], bank[2][:, :], gk_n[:, :], root_k[:, :], ALU.mult, ALU.mult)
                dve.scalar_tensor_tensor(k_r[:, :], M["kpeT"][:, 0:TP], gk_r[:, :], root_k[0:ROPE, :], ALU.mult, ALU.mult)
                dve.wait_ge(q_rooted, h * 2 + 2)
                then(dve.reciprocal(root_q[:, :], root_q[:, :]))
                dve.scalar_tensor_tensor(q_n[:, b, :], q_n[:, b, :], gq_n[:, :], root_q[:, :], ALU.mult, ALU.mult)
                then(dve.scalar_tensor_tensor(q_r[:, b, :], q_r[:, b, :], gq_r[:, :], root_q[0:ROPE, :], ALU.mult, ALU.mult))
                dve.sem_inc(prepared, 1)
                dve.tensor_copy(M["qs_n"][:, bass.ds(h * TS, TS)], q_n[:, b, TP:T])
                dve.tensor_copy(M["qs_r"][:, bass.ds(h * TS, TS)], q_r[:, b, TP:T])
                for q in range(TT):
                    w = (q + 1) * P
                    dve.wait_ge(scored, h * TT + (q + 1))
                    then(dve.tensor_tensor(bank[q][:, w - P:w], bank[q][:, w - P:w], K["bias"][:, :], ALU.add))
                    then(dve.tensor_reduce(top[:, q:q + 1], bank[q][:, 0:w], X, ALU.max))
                    dve.tensor_scalar(shift[:, q:q + 1], top[:, q:q + 1], -SCALE, None, ALU.mult).then_inc(shifted, 1)
                dve.wait_ge(exped, h * TT + TT)
                then(dve.reciprocal(share[:, :], total[:, :]))
                for q in range(TT):
                    w = (q + 1) * P
                    dve.tensor_scalar(probs[:, q, 0:w], probs[:, q, 0:w], share[:, q:q + 1], None, ALU.mult).then_inc(shared, 1)
                dve.wait_ge(weighed, h * TT + TT)
                then(dve.tensor_copy(oT[:, bass.ds(h * T, TP)], psO[:, :]))
                dve.sem_inc(head_done[b], 1)
                then.full()
            heads(dve, head)


XB, XC_ = KI, KI + G
NR = TS * (CW - 1)
LAST = CW - 1 + TS


def convolution(nc, A, K, S, h_hi, h_lo, proj, outs):
    with ExitStack() as ctx:
        m = Mem(nc, ctx, "cnv")
        NB = 3
        NP = NR + CW + 1
        w, w_hi, w_lo = m.sb("w", [P, 2, KD, P]), m.sb("w_hi", [P, 4, KD, P], F32R), m.sb("w_lo", [P, 4, KD, P], F32R)
        held = m.sb("held", [NP, CD])
        params = m.sb("params", [P, KC, NP])
        raw, y = m.sb("raw", [P, NB, CW - 1 + T]), m.sb("y", [P, NB, T])
        rows_out = m.sb("rows_out", [LAST, 2, 512])
        ps, psP, psR = m.ps("ps", [P, 2, 2, 512]), m.ps("psP", [P, 2, 512]), m.ps("psR", [LAST, 2, 512])
        w_in = [m.sem(f"w_in{b}") for b in range(2)]
        rounded, lowered, multiplied, drained = (m.sem(n) for n in ("rounded", "lowered", "multiplied", "drained"))
        held_in, padded, turned, placed = m.sem("held_in"), m.sem("padded"), m.sem("turned"), m.sem("placed")
        began, summed, done, chain = m.sem("began"), m.sem("summed"), m.sem("done"), m.sem("chain")
        rows_stored = [m.sem(f"rows_stored{b}") for b in range(2)]
        rows_turned, rows_copied, stored = m.sem("rows_turned"), m.sem("rows_copied"), m.sem("stored")
        block = ctx.enter_context(nc.Block())
        PC = KC // 2
        w_view = A["w_in"].rearrange("l (k p) n -> p (l k) n", p=P)
        AT_KPE, AT_XBC, AT_DT = H * DQK + LAT, IN - 2 * D - SH - CD, IN - 2 * D - SH
        columns = chunks_from(AT_XBC, KC) + [AT_DT, AT_KPE]

        @block.sync
        def _(sp):
            sp.dma_start(held[0:NR, :], A["state_conv"].rearrange("l b w c -> (l b w) c")).then_inc(held_in, 16)
            sp.dma_start(held[NR:NR + CW, :], A["conv_w"].rearrange("l w c -> (l w) c")).then_inc(held_in, 16)
            sp.dma_start(held[NR + CW:NP, :], A["conv_b"]).then_inc(held_in, 16)
            weights_in(sp, w, w_view, w_in, lowered, columns)
            sp.dma_start(outs["conv_s"][0, :, 0:CW - 2, :], A["state_conv"][0, :, 1:CW - 1, :]).then_inc(stored, 16)
            sp.wait_ge(drained, KC + 2)
            sp.dma_start(proj[C_KPE], y[:, 0, :]).then_inc(stored, 16)
            sp.wait_ge(stored, 32)

        @block.gpsimd
        def _(pool):
            pool.memset(raw[:, :, 0:CW - 1], 0.0).then_inc(padded, 1)
            for c in range(KC + 2):
                round_weights(pool, w, w_hi, w_in, multiplied, rounded, c)

        @block.tensor
        def _(pe):
            pe.wait_ge(held_in, 48)
            for c in range(KC):
                last = pe.transpose(psP[:, c // PC, (c % PC) * NP:(c % PC) * NP + NP], held[:, c * P:(c + 1) * P], K["ident"][0:NP, 0:NP])
            last.then_inc(turned, 1)

            def turn_rows(c):
                pe.wait_ge(drained, c + 1)
                if c >= 8:
                    pe.wait_ge(rows_copied, c // 4 - 1)
                pe.transpose(psR[:, c // 4 % 2, (c % 4) * P:(c % 4 + 1) * P], raw[:, c % NB, TP:], K["ident"][:, :]).then_inc(rows_turned, 1)

            for c in range(KC + 2):
                pe.wait_ge(lowered, c + 1)
                if c >= 2:
                    pe.wait_ge(drained, c - 1)
                chunk_product(pe, ps[:, c % 2], c, w_hi, w_lo, h_hi, h_lo).then_inc(multiplied, 1)
                if 1 <= c <= KC:
                    turn_rows(c - 1)

        @block.scalar
        def _(act):
            act.wait_ge(placed, 1)
            act.wait_ge(padded, 1)
            b0 = NR + CW
            for c in range(KC + 1):
                if c < KC:
                    s = c % NB
                    act.wait_ge(multiplied, c + 1)
                    if c >= NB:
                        act.wait_ge(summed, c - NB + 1)
                        act.wait_ge(rows_turned, c - NB + 1)
                        act.wait_ge(done, c - NB + 1)
                    act.activation(raw[:, s, CW - 1:].rearrange("p (s t) -> p s t", s=2), ps[:, c % 2, :, 0:HALF], ACT.Copy).then_inc(drained, 1)
                    act.wait_ge(drained, c + 1)
                    act.activation(y[:, s, 0:TP], raw[:, s, 0:TP], ACT.Identity, scale=params[:, c, NR:NR + 1],
                                   bias=params[:, c, b0:b0 + 1])
                    act.activation(y[:, s, TP:], params[:, c, 0:NR:CW - 1], ACT.Identity, scale=params[:, c, NR:NR + 1],
                                   bias=params[:, c, b0:b0 + 1]).then_inc(began, 1)
                if c:
                    act.wait_ge(summed, c)
                    act.activation(S["x"][:, c - 1, :], y[:, (c - 1) % NB, :], ACT.Silu).then_inc(done, 1)
                if c and c % 4 == 0:
                    g = c // 4 - 1
                    cols = slice(g * 512, (g + 1) * 512)
                    act.wait_ge(rows_copied, g + 1)
                    act.dma_start(outs["conv_p"][0, 0, :, cols], rows_out[0:CW - 1, g % 2, :]).then_inc(rows_stored[g % 2], 16)
                    act.dma_start(outs["conv_s"][0, :, CW - 2, cols], rows_out[CW - 1:LAST, g % 2, :]).then_inc(rows_stored[g % 2], 16)
            act.wait_ge(done, KC)
            act.wait_ge(multiplied, KC + 1)
            act.activation(S["dt_raw"][:, :].rearrange("p (s t) -> p s t", s=2), ps[0:SH, KC % 2, :, 0:HALF], ACT.Copy).then_inc(drained, 1)
            act.wait_ge(multiplied, KC + 2)
            act.activation(y[:, 0, :].rearrange("p (s t) -> p s t", s=2), ps[:, (KC + 1) % 2, :, 0:HALF], ACT.Copy).then_inc(drained, 1)
            for b in range(2):
                act.wait_ge(rows_stored[b], 32 * (KC // 8))

        @block.vector
        def _(dve):
            then = Chain(dve, chain)
            dve.wait_ge(turned, 1)
            dve.tensor_copy(params[:, :, :].rearrange("p (h c) n -> p h (c n)", h=2), psP[:, :, 0:PC * NP]).then_inc(placed, 1)
            dve.wait_ge(placed, 1)
            dve.wait_ge(padded, 1)
            AHEAD = 3
            for c in range(-AHEAD, KC):
                if c + AHEAD < KC + 2:
                    n = c + AHEAD
                    lower(dve, w_hi[:, n % 4], w_lo[:, n % 4], w[:, n % 2], rounded, lowered, n + 1)
                if c < 0:
                    continue
                s = c % NB
                dve.wait_ge(began, c + 1)
                for t in range(1, CW):
                    tap = params[:, c, NR + t:NR + t + 1]
                    dve.scalar_tensor_tensor(y[:, s, 0:TP], raw[:, s, t:t + TP], tap, y[:, s, 0:TP], ALU.mult, ALU.add)
                    held_t = params[:, c, t:NR:CW - 1] if t < CW - 1 else raw[:, s, CW - 1 + TP:]
                    last = dve.scalar_tensor_tensor(y[:, s, TP:], held_t, tap, y[:, s, TP:], ALU.mult, ALU.add)
                    if t < CW - 1:
                        then(last)
                last.then_inc(summed, 1)
                if c % 4 == 3:
                    g = c // 4
                    dve.wait_ge(rows_turned, c + 1)
                    if g >= 2:
                        dve.wait_ge(rows_stored[g % 2], 32 * (g // 2))
                    dve.tensor_copy(rows_out[:, g % 2, :], psR[:, g % 2, :]).then_inc(rows_copied, 1)


def prompt_scan(nc, A, K, S, acs_dram, outs):
    HP = SH // G
    with ExitStack() as ctx:
        m = Mem(nc, ctx, "scn")
        seg, ce = m.sb("seg", [P, SH, P]), m.sb("ce", [P, SH, P])
        x_tok, b_tok, xw = m.sb("x_tok", [P, DI]), m.sb("b_tok", [P, G * N]), m.sb("xw", [P, DI])
        cb = m.sb("cb", [P, G, P])
        state, state_out = m.sb("state", [P, DI]), m.sb("state_out", [P, 2, 512])
        to_end, end = m.sb("to_end", [P, SH]), m.sb("end", [P, SH])
        bank = [m.ps(f"bank{b}", [P, 512]) for b in range(8)]
        read_in, turned, copied, cb_made = m.sem("read_in"), m.sem("turned"), m.sem("copied"), m.sem("cb_made")
        cb_masked, seg_made, decayed, exped, weighted = (m.sem(n) for n in ("cb_masked", "seg_made", "decayed", "exped", "weighted"))
        ce_made, x_weighted, summed, y_done, grown, state_done = (m.sem(n) for n in ("ce_made", "x_weighted", "summed", "y_done", "grown", "state_done"))
        end_exped, end_in, chain = m.sem("end_exped"), m.sem("end_in"), m.sem("chain")
        out_turned, out_copied = m.sem("out_turned"), m.sem("out_copied")
        stored = [m.sem(f"stored{b}") for b in range(2)]
        block = ctx.enter_context(nc.Block())
        acs_all = acs_dram.rearrange("(a h) t -> a h t", a=1)
        heads_of = lambda ap, g: ap[:, g * HP:(g + 1) * HP, :]

        @block.sync
        def _(sp):
            for c in range(TT):
                if c:
                    sp.wait_ge(summed, 4 * c)
                    sp.wait_ge(exped, c)
                sp.dma_start(ce[:, :, :], acs_all[:, :, c * P:(c + 1) * P].to_broadcast([P, SH, P])).then_inc(read_in, 16)
            for q in range(4):
                sp.wait_ge(out_copied, q + 1)
                sp.dma_start(outs["ssm_p"][0, 0].rearrange("(k a) p n -> (a p) k n", a=2)[:, 4 * q:4 * q + 4, :],
                             state_out[:, q % 2, :].rearrange("p (k n) -> p k n", k=4)).then_inc(stored[q % 2], 16)
            sp.wait_ge(stored[0], 32)
            sp.wait_ge(stored[1], 32)

        @block.tensor
        def _(pe):
            for c in range(TT):
                at = slice(c * P, (c + 1) * P)
                for q in range(5):
                    if c:
                        pe.wait_ge(y_done if q < 4 else state_done, 4 * c if q < 4 else c)
                    for k in range(4):
                        last = pe.transpose(bank[q][:, k * P:(k + 1) * P], S["x"][:, 4 * q + k, at], K["ident"][:, :])
                    last.then_inc(turned, 1)
                if c:
                    pe.wait_ge(cb_masked, c)
                for g in range(G):
                    last = pe.matmul(bank[5][:, g * P:(g + 1) * P], S["x"][:, XB + g, at], S["x"][:, XC_ + g, at], start=True, stop=True)
                last.then_inc(cb_made, 1)
                pe.wait_ge(copied, 5 * c + 5)
                for q in range(4):
                    pe.wait_ge(weighted, 4 * c + q + 1)
                    if c:
                        pe.wait_ge(ce_made, 4 * c + q + 1)
                        pe.wait_ge(state_done, c)
                    for h in range(8 * q, 8 * q + 8):
                        out = bank[q][HD * (h % 2):HD * (h % 2) + HD, (h // 2 % 4) * P:(h // 2 % 4 + 1) * P]
                        last = pe.matmul(out, x_tok[:, h * HD:(h + 1) * HD], seg[:, h, :], start=True, stop=(c == 0))
                        if c:
                            last = pe.matmul(out, state[:, h * HD:(h + 1) * HD], ce[:, h, :], start=False, stop=True)
                    last.then_inc(summed, 1)
                pe.wait_ge(x_weighted, c + 1)
                for g in range(G):
                    if g == 0 and c:
                        pe.wait_ge(state_done, c)
                    dst = bank[4 if g == 0 else 5 + (g - 1)]
                    if g == 1:
                        pe.wait_ge(cb_masked, c + 1)
                    last = pe.matmul(dst[:, :], b_tok[:, g * N:(g + 1) * N], xw[:, g * 512:(g + 1) * 512], start=True, stop=True)
                last.then_inc(grown, 1)
            pe.wait_ge(state_done, TT)
            for q in range(4):
                if q >= 2:
                    pe.wait_ge(out_copied, q - 1)
                if q == 0:
                    pe.wait_ge(y_done, 4 * TT)
                for k in range(4):
                    last = pe.transpose(bank[q % 2][:, k * P:(k + 1) * P], state[:, (4 * q + k) * P:(4 * q + k + 1) * P], K["ident"][:, :])
                last.then_inc(out_turned, 1)

        @block.scalar
        def _(act):
            for c in range(TT):
                for q in range(5):
                    act.wait_ge(turned, 5 * c + q + 1)
                    if c and q == 0:
                        act.wait_ge(summed, 4 * c)
                        act.wait_ge(x_weighted, c)
                        act.wait_ge(grown, c)
                    act.activation(x_tok[:, q * 512:(q + 1) * 512] if q < 4 else b_tok[:, :], bank[q][:, :], ACT.Copy).then_inc(copied, 1)
                act.wait_ge(seg_made, c + 1)
                act.activation(seg[:, :, :], seg[:, :, :], ACT.Exp).then_inc(decayed, 1)
                act.wait_ge(end_in, c + 1)
                act.activation(to_end[:, :], to_end[:, :], ACT.Exp).then_inc(end_exped, 1)
                act.activation(end[:, :], ce[:, :, P - 1], ACT.Exp).then_inc(end_exped, 1)
                act.wait_ge(end_exped, 2 * c + 2)
                act.activation(ce[:, :, :], ce[:, :, :], ACT.Exp).then_inc(exped, 1)

        @block.vector
        def _(dve):
            then = Chain(dve, chain)
            for c in range(TT):
                at = slice(c * P, (c + 1) * P)
                dve.wait_ge(read_in, 16 * c + 16)
                for h in range(SH):
                    last = dve.tensor_scalar(seg[:, h, :], ce[:, h, :], S["acs_tok"][:, c, h:h + 1], 0.0, ALU.subtract, ALU.min)
                last.then_inc(seg_made, 1)
                dve.tensor_tensor(to_end[:, :], ce[:, :, P - 1], S["acs_tok"][:, c, :], ALU.subtract).then_inc(end_in, 1)
                dve.wait_ge(cb_made, c + 1)
                if c:
                    dve.wait_ge(weighted, 4 * c)
                dve.tensor_tensor(cb[:, :, :], bank[5][:, :].rearrange("p (g i) -> p g i", g=G),
                                  K["keep"][:, :].rearrange("p (a i) -> p a i", a=1).to_broadcast([P, G, P]), ALU.mult).then_inc(cb_masked, 1)
                dve.wait_ge(cb_masked, c + 1)
                dve.wait_ge(decayed, c + 1)
                for q in range(4):
                    for h in range(8 * q, 8 * q + 8):
                        last = dve.scalar_tensor_tensor(seg[:, h, :], seg[:, h, :], S["dt_tok"][:, c, h:h + 1], cb[:, h // HP, :], ALU.mult, ALU.mult)
                    last.then_inc(weighted, 1)
                if c:
                    dve.wait_ge(exped, c + 1)
                    for g in range(G):
                        dve.tensor_tensor(heads_of(ce, g), heads_of(ce, g),
                                          S["x"][:, XC_ + g:XC_ + g + 1, at].to_broadcast([P, HP, P]), ALU.mult).then_inc(ce_made, 1)
                else:
                    dve.sem_inc(ce_made, G)
                dve.wait_ge(end_exped, 2 * c + 2)
                then(dve.tensor_tensor(to_end[:, :], to_end[:, :], S["dt_tok"][:, c, :], ALU.mult))
                dve.wait_ge(copied, 5 * c + 4)
                dve.tensor_tensor(xw[:, :].rearrange("p (h d) -> p h d", h=SH), x_tok[:, :].rearrange("p (h d) -> p h d", h=SH),
                                  to_end[:, :].rearrange("p (h a) -> p h a", a=1).to_broadcast([P, SH, HD]), ALU.mult).then_inc(x_weighted, 1)
                for q in range(4):
                    dve.wait_ge(summed, 4 * c + q + 1)
                    for k in range(4 * q, 4 * q + 4):
                        last = dve.scalar_tensor_tensor(S["x"][:, k, at], S["x"][:, k, at], S["skip"][:, k:k + 1],
                                                        bank[q][:, (k % 4) * P:(k % 4 + 1) * P], ALU.mult, ALU.add)
                    last.then_inc(y_done, 1)
                dve.wait_ge(grown, c + 1)
                view = lambda ap: ap.rearrange("p (h d) -> p h d", d=HD)
                if c:
                    then(dve.tensor_tensor(view(state[:, :]), view(state[:, :]),
                                           end[:, :].rearrange("p (h a) -> p h a", a=1).to_broadcast([P, SH, HD]), ALU.mult))
                for g in range(G):
                    part, new = state[:, g * 512:(g + 1) * 512], bank[4 + g][:, :]
                    last = dve.tensor_tensor(part, part, new, ALU.add) if c else dve.tensor_copy(part, new)
                last.then_inc(state_done, 1)
            for q in range(4):
                dve.wait_ge(out_turned, q + 1)
                if q >= 2:
                    dve.wait_ge(stored[q % 2], 16)
                dve.tensor_copy(state_out[:, q % 2, :], bank[q % 2][:, :]).then_inc(out_copied, 1)


def sample_scan(nc, A, K, S, h_hi, h_lo, proj, acs_dram, outs):
    ORDER = 9
    with ExitStack() as ctx:
        m = Mem(nc, ctx, "stp")
        w, w_hi, w_lo = m.sb("w", [P, 2, KD, P]), m.sb("w_hi", [P, 4, KD, P], F32R), m.sb("w_lo", [P, 4, KD, P], F32R)
        out = m.sb("out", [P, 2, T])
        ps = m.ps("ps", [P, 2, 2, 512])
        w_in = [m.sem(f"w_in{b}") for b in range(2)]
        out_stored = [m.sem(f"out_stored{b}") for b in range(2)]
        rounded, lowered, multiplied, drained = (m.sem(n) for n in ("rounded", "lowered", "multiplied", "drained"))
        w_view = A["w_in"].rearrange("l (k p) n -> p (l k) n", p=P)
        CHUNKS = list(range(C_Q, C_KPE)) + list(range(C_Z, C_XBC))
        columns = chunks_from(0, C_KPE) + chunks_from(H * DQK + LAT + ROPE, KI)
        bias, a_log = m.sb("bias", [SH, 1]), m.sb("a_log", [SH, 1])
        psT = m.ps("psT", [P, 2, TT, SH])
        loaded, biased, magnitude, exped, a_made, ready = (m.sem(n) for n in ("loaded", "biased", "magnitude", "exped", "a_made", "ready"))
        turned, acs_stored, chain = m.sem("turned"), m.sem("acs_stored"), m.sem("chain")
        NB = 2
        st, tmp = m.sb("st", [P, NB, KI, N]), m.sb("tmp", [P, KI, N])
        NR_ = 2 * TS + 1
        rates_in, rates, dtx = m.sb("rates_in", [SH, NR_]), m.sb("rates", [P, KI, NR_]), m.sb("dtx", [P, KI, TS])
        y = m.sb("y", [P, KI, TS])
        psS, psB = m.ps("psS", [P, KI, NR_]), m.ps("psB", [P, 2, 512])
        wide = m.sb("wide", [P, 2 * G, P])
        x = S["dt_raw"]
        s, s2, p_ = (tmp[0:SH].rearrange("p k n -> p (k n)")[:, j * T:(j + 1) * T] for j in range(3))
        e = wide[0:SH].rearrange("p g n -> p (g n)")[:, 0:T]
        st_in = [m.sem(f"st_in{b}") for b in range(NB)]
        stored = [m.sem(f"stored{b}") for b in range(NB)]
        set_, spread, widened, bc_made, decayed, updated, summed, dtx_made = (m.sem(n) for n in (
            "set", "spread", "widened", "bc_made", "decayed", "updated", "summed", "dtx_made"))
        block = ctx.enter_context(nc.Block())
        view_in = A["state_ssm"][0].rearrange("b (k a) p n -> b (a p) k n", a=2)
        view_out = outs["ssm_s"][0].rearrange("b (k a) p n -> b (a p) k n", a=2)
        TURN, SPREAD = 5, 6
        sequence_at = {8 + 3 * b: b for b in range(TS)}

        @block.sync
        def _(sp):
            sp.dma_start(bias[:, :], A["dt_bias"].rearrange("l h -> h l")).then_inc(loaded, 16)
            sp.dma_start(a_log[:, :], A["a_log"].rearrange("l h -> h l")).then_inc(loaded, 16)
            sp.dma_start(rates_in[:, 2 * TS:], A["d_skip"].rearrange("l h -> h l")).then_inc(loaded, 16)
            weights_in(sp, w, w_view, w_in, lowered, columns)

        @block.scalar
        def _(act):
            act.wait_ge(loaded, 48)
            act.activation(S["a"][:, :], a_log[:, :], ACT.Exp).then_inc(a_made, 1)
            act.wait_ge(biased, 1)
            act.activation(e[:, :], x[:, :], ACT.Abs).then_inc(magnitude, 1)
            act.wait_ge(magnitude, 1)
            act.activation(e[:, :], e[:, :], ACT.Exp, scale=-1.0).then_inc(exped, 1)
            for c, chunk in enumerate(CHUNKS):
                act.wait_ge(multiplied, c + 1)
                if c >= 2:
                    act.wait_ge(out_stored[c % 2], 16 * (c // 2))
                act.activation(out[:, c % 2].rearrange("p (s t) -> p s t", s=2), ps[:, c % 2, :, 0:HALF], ACT.Copy).then_inc(drained, 1)
                act.wait_ge(drained, c + 1)
                act.dma_start(proj[chunk], out[:, c % 2]).then_inc(out_stored[c % 2], 16)
                if c == TURN - 1:
                    act.wait_ge(ready, 1)
                    act.activation(S["decay_s"][:, :], S["acs"][:, TP:], ACT.Exp).then_inc(exped, 1)
            for b in range(2):
                act.wait_ge(out_stored[b], 16 * (len(CHUNKS) // 2))

        @block.gpsimd
        def _(pool):
            for c in range(len(CHUNKS)):
                round_weights(pool, w, w_hi, w_in, multiplied, rounded, c)
                if c + 1 in sequence_at:
                    b = sequence_at[c + 1]
                    if b >= NB:
                        pool.wait_ge(updated, b - NB + 1)
                        pool.dma_start(view_out[b - NB], st[:, b % NB]).then_inc(stored[b % NB], 16)
                        pool.wait_ge(stored[b % NB], 16 * (b // NB))
                        pool.wait_ge(summed, b - NB + 1)
                    pool.dma_start(st[:, b % NB], view_in[b]).then_inc(st_in[b % NB], 16)
            for b in range(TS - NB, TS):
                pool.wait_ge(updated, b + 1)
                pool.dma_start(view_out[b], st[:, b % NB]).then_inc(stored[b % NB], 16)
            pool.wait_ge(ready, 1)
            pool.dma_start(acs_dram, S["acs"][:, 0:TP]).then_inc(acs_stored, 16)
            pool.wait_ge(acs_stored, 16)
            for b in range(NB):
                pool.wait_ge(stored[b], 16 * (TS // NB))

        @block.tensor
        def _(pe):
            for c in range(len(CHUNKS)):
                pe.wait_ge(lowered, c + 1)
                if c >= 2:
                    pe.wait_ge(drained, c - 1)
                chunk_product(pe, ps[:, c % 2], c, w_hi, w_lo, h_hi, h_lo).then_inc(multiplied, 1)
                if c == TURN:
                    pe.wait_ge(ready, 1)
                    for t in range(TT):
                        pe.transpose(psT[:, 0, t, :], S["dt"][:, t * P:(t + 1) * P], K["ident"][0:SH, 0:SH])
                        last = pe.transpose(psT[:, 1, t, :], S["acs"][:, t * P:(t + 1) * P], K["ident"][0:SH, 0:SH])
                    last.then_inc(turned, 1)
                if c == SPREAD:
                    pe.wait_ge(set_, 2)
                    for k in range(KI):
                        last = pe.matmul(psS[:, k, :], K["spread"][:, k * P:(k + 1) * P], rates_in[:, :], start=True, stop=True)
                    last.then_inc(spread, 1)
                if c in sequence_at:
                    b = sequence_at[c]
                    pe.wait_ge(widened, b + 1)
                    if b:
                        pe.wait_ge(summed, b)
                    for j in range(2):
                        for g in range(G):
                            last = pe.matmul(psB[:, j, g * P:(g + 1) * P], wide[:, G * j + g, :], K["ident"][:, :], start=True, stop=True)
                    last.then_inc(bc_made, 1)

        @block.vector
        def _(dve):
            then = Chain(dve, chain)

            def lower_to(end):
                while lower_to.c < min(end, len(CHUNKS)):
                    c = lower_to.c
                    lower(dve, w_hi[:, c % 4], w_lo[:, c % 4], w[:, c % 2], rounded, lowered, c + 1)
                    lower_to.c += 1
            lower_to.c = 0

            dve.wait_ge(loaded, 48)
            dve.tensor_scalar(x[:, :], S["dt_raw"][:, :], bias[:, :], None, ALU.add).then_inc(biased, 1)
            lower_to(2)
            dve.wait_ge(exped, 1)
            then(dve.tensor_scalar(s[:, :], e[:, :], 2.0, None, ALU.add))
            then(dve.reciprocal(s[:, :], s[:, :]))
            lower_to(4)
            then(dve.tensor_tensor(s[:, :], s[:, :], e[:, :], ALU.mult))
            then(dve.tensor_tensor(s2[:, :], s[:, :], s[:, :], ALU.mult))
            then(dve.tensor_scalar(p_[:, :], s2[:, :], 2.0 / (2 * ORDER + 1), None, ALU.mult))
            for k in range(ORDER - 1, 0, -1):
                then(dve.scalar_tensor_tensor(p_[:, :], p_[:, :], 2.0 / (2 * k + 1), s2[:, :], ALU.add, ALU.mult))
            lower_to(5)
            then(dve.scalar_tensor_tensor(p_[:, :], p_[:, :], 2.0, s[:, :], ALU.add, ALU.mult))
            then(dve.scalar_tensor_tensor(S["dt"][:, :], x[:, :], 0.0, p_[:, :], ALU.max, ALU.add))
            dve.wait_ge(a_made, 1)
            then(dve.tensor_scalar(S["a"][:, :], S["a"][:, :], -1.0, None, ALU.mult))
            then(dve.tensor_scalar(p_[:, :], S["dt"][:, :], S["a"][:, :], None, ALU.mult))
            for c in range(TT):
                dve.tensor_tensor_scan(S["acs"][:, c * P:(c + 1) * P], K["ones"][0:SH, :], p_[:, c * P:(c + 1) * P], 0.0, ALU.mult, ALU.add)
            dve.tensor_copy(S["acs"][:, TP:], p_[:, TP:]).then_inc(ready, 1)
            lower_to(6)
            dve.tensor_copy(rates_in[:, 0:TS], S["dt"][:, TP:]).then_inc(set_, 1)
            dve.wait_ge(exped, 2)
            dve.tensor_copy(rates_in[:, TS:2 * TS], S["decay_s"][:, :]).then_inc(set_, 1)
            lower_to(8)
            dve.wait_ge(turned, 1)
            dve.tensor_copy(S["dt_tok"][:, :, :], psT[:, 0, :, :])
            dve.tensor_copy(S["acs_tok"][:, :, :], psT[:, 1, :, :])
            dve.wait_ge(spread, 1)
            then(dve.tensor_copy(rates[:, :, :], psS[:, :, :]))
            dve.tensor_copy(S["skip"][:, :], rates[:, :, 2 * TS])
            then(dve.tensor_tensor(dtx[:, :, :], S["x"][:, 0:KI, TP:], rates[:, :, 0:TS], ALU.mult))
            for b in range(TS):
                at = {seq: c for c, seq in sequence_at.items()}[b]
                dve.tensor_copy(wide[:, :, :], S["x"][:, XB:XB + 2 * G, TP + b:TP + b + 1].to_broadcast([P, 2 * G, P])).then_inc(widened, 1)
                lower_to(at + 2)
                dve.wait_ge(st_in[b % NB], 16 * (b // NB + 1))
                then(dve.tensor_tensor(st[:, b % NB], st[:, b % NB], rates[:, :, TS + b:TS + b + 1].to_broadcast([P, KI, N]), ALU.mult))
                dve.wait_ge(bc_made, b + 1)
                for g in range(G):
                    ks = slice(4 * g, 4 * g + 4)
                    last = dve.tensor_tensor(tmp[:, ks, :], psB[:, 0, g * P:(g + 1) * P].rearrange("p (a n) -> p a n", a=1).to_broadcast([P, 4, N]),
                                             dtx[:, ks, b:b + 1].to_broadcast([P, 4, N]), ALU.mult)
                then(last)
                dve.tensor_tensor(st[:, b % NB], st[:, b % NB], tmp[:, :, :], ALU.add).then_inc(updated, 1)
                dve.wait_ge(updated, b + 1)
                lower_to(at + 4)
                for g in range(G):
                    ks = slice(4 * g, 4 * g + 4)
                    last = dve.tensor_tensor(tmp[:, ks, :], st[:, b % NB, ks, :],
                                             psB[:, 1, g * P:(g + 1) * P].rearrange("p (a n) -> p a n", a=1).to_broadcast([P, 4, N]), ALU.mult)
                last.then_inc(summed, 1)
                dve.wait_ge(summed, b + 1)
                then(dve.tensor_reduce(y[:, :, b:b + 1], tmp[:, :, :], X, ALU.add))
            lower_to(len(CHUNKS))
            then(dve.tensor_tensor(dtx[:, :, :], S["x"][:, 0:KI, TP:], S["skip"][:, :].rearrange("p (k a) -> p k a", a=1).to_broadcast([P, KI, TS]), ALU.mult))
            dve.tensor_tensor(S["x"][:, 0:KI, TP:], dtx[:, :, :], y[:, :, :], ALU.add)


def gated_norm(nc, A, K, S, proj, yT_s):
    with ExitStack() as ctx:
        m = Mem(nc, ctx, "gtn")
        NB = 3
        z, sq = m.sb("z", [P, NB, T]), m.sb("sq", [P, NB, T])
        rstd = m.sb("rstd", [P, 2, HALF])
        ps = m.ps("ps", [P, 2, 512])
        z_in = [m.sem(f"z_in{b}") for b in range(NB)]
        gated, silued, squared, added, rooted, chain = (m.sem(n) for n in ("gated", "silued", "squared", "added", "rooted", "chain"))
        gain_in = m.sem("gain_in")
        block = ctx.enter_context(nc.Block())

        @block.sync
        def _(sp):
            sp.dma_start(S["g_ssm"][:, :], A["g_ssm"].rearrange("l (k p) -> p (l k)", p=P), allow_slow_non_contiguous=True).then_inc(gain_in, 16)
            for k in range(KI):
                if k >= NB:
                    sp.wait_ge(gated, k - NB + 1)
                sp.dma_start(z[:, k % NB, :], proj[C_Z + k]).then_inc(z_in[k % NB], 16)

        @block.scalar
        def _(act):
            for k in range(KI + 1):
                if k < KI:
                    act.wait_ge(z_in[k % NB], 16 * (k // NB + 1))
                    act.activation(z[:, k % NB, :], z[:, k % NB, :], ACT.Silu).then_inc(silued, 1)
                if k:
                    act.wait_ge(gated, k)
                    if k > NB:
                        act.wait_ge(added, k - NB)
                    act.activation(sq[:, (k - 1) % NB, :], S["x"][:, k - 1, :], ACT.Square).then_inc(squared, 1)
            act.wait_ge(added, KI)
            act.activation(rstd[:, :, :], ps[:, :, 0:HALF], ACT.Sqrt, scale=1.0 / DI, bias=K["eps"][:, :]).then_inc(rooted, 1)

        @block.tensor
        def _(pe):
            for k in range(KI):
                pe.wait_ge(squared, k + 1)
                for s in range(2):
                    last = pe.matmul(ps[:, s, 0:HALF], K["ones"][:, :], sq[:, k % NB, s * HALF:(s + 1) * HALF],
                                     start=(k == 0), stop=(k == KI - 1))
                last.then_inc(added, 1)

        @block.vector
        def _(dve):
            then = Chain(dve, chain)
            for k in range(KI):
                dve.wait_ge(silued, k + 1)
                dve.tensor_tensor(S["x"][:, k, :], S["x"][:, k, :], z[:, k % NB, :], ALU.mult).then_inc(gated, 1)
            dve.wait_ge(rooted, 1)
            then(dve.reciprocal(rstd[:, :, :], rstd[:, :, :]))
            dve.wait_ge(gain_in, 16)
            for k in range(KI):
                v = S["x"][:, k, :].rearrange("p (s t) -> p s t", s=2)
                last = dve.scalar_tensor_tensor(v, v, S["g_ssm"][:, k:k + 1], rstd[:, :, :], ALU.mult, ALU.mult)
            then(last)
            dve.tensor_copy(yT_s[:, :, :], S["x"][:, 0:KI, TP:])


WQ = 2 * P
BIG = -3.0e38


def merge(nc, A, K, tag, proj, first, W, oT, yT, mT):
    with ExitStack() as ctx:
        m = Mem(nc, ctx, tag)
        wa, wb = m.sb("wa", [P, 2, H, P]), m.sb("wb", [P, 2, KI, P])
        gate, part = m.sb("gate", [P, 2, 2, W]), m.sb("part", [P, 2, W])
        ps = m.ps("ps", [P, 2, 2, 512])
        w_in, gate_in, opened, summed, used = ([m.sem(f"{n}{b}") for b in range(2)]
                                               for n in ("w_in", "gate_in", "opened", "summed", "used"))
        chain = m.sem("chain")
        block = ctx.enter_context(nc.Block())

        def chunks(eng, body):
            with eng.Fori(0, KD // 2) as i:
                for b in range(2):
                    body(i, b, i * 2 + b)

        @block.sync
        def _(sp):
            def load(i, b, d):
                at = bass.ds(d * P, P)
                sp.wait_ge(summed[b], i)
                sp.dma_start(wa[:, b], A["w_br_a"].rearrange("l (k p) n -> p (l k) n", p=P)[:, :, at]).then_inc(w_in[b], 16)
                sp.dma_start(wb[:, b], A["w_br_b"].rearrange("l (k p) n -> p (l k) n", p=P)[:, :, at]).then_inc(w_in[b], 16)
                sp.wait_ge(used[b], i)
                for j, c in enumerate((C_GA, C_GB)):
                    sp.dma_start(gate[:, b, j, :], proj.rearrange("c p t -> p c t")[:, bass.ds(d + c, 1), first:first + W]).then_inc(gate_in[b], 16)
            chunks(sp, load)

        @block.tensor
        def _(pe):
            def product(i, b, d):
                pe.wait_ge(w_in[b], i * 32 + 32)
                pe.wait_ge(used[b], i)
                for j, (w, v, n) in enumerate(((wa, oT, H), (wb, yT, KI))):
                    for k in range(n):
                        last = pe.matmul(ps[:, b, j, 0:W], w[:, b, k, :], v[:, k, :], start=(k == 0), stop=(k == n - 1))
                last.then_inc(summed[b], 1)
            chunks(pe, product)

        @block.scalar
        def _(act):
            def open_(i, b, d):
                act.wait_ge(gate_in[b], i * 32 + 32)
                act.activation(gate[:, b], gate[:, b], ACT.Sigmoid).then_inc(opened[b], 1)
            chunks(act, open_)

        @block.vector
        def _(dve):
            def sum_(i, b, d):
                then = Steps(dve, chain, 2, d)
                dve.wait_ge(opened[b], i + 1)
                dve.wait_ge(summed[b], i + 1)
                dve.tensor_tensor(part[:, 0, :], ps[:, b, 0, 0:W], gate[:, b, 0, :], ALU.mult)
                then(dve.tensor_tensor(part[:, 1, :], ps[:, b, 1, 0:W], gate[:, b, 1, :], ALU.mult))
                then(dve.tensor_tensor(mT[:, bass.ds(d, 1), :].rearrange("p a t -> p (a t)"), part[:, 0, :], part[:, 1, :], ALU.add))
                dve.sem_inc(used[b], 1)
                then.full()
            chunks(dve, sum_)


def residual(nc, A, K, tag, tiles, gate_at, mT, x_src, x1):
    n = tiles[0]
    prompt = n == P
    with ExitStack() as ctx:
        m = Mem(nc, ctx, tag)
        w = m.sb("w", [P, KD, D])
        gate = m.sb("gate", [P, D])
        ps, psG = m.ps("ps", [P, 2, 2, 512]), m.ps("psG", [P, 2, 512])
        w_in, x_in, spread, summed, used, chain = (m.sem(k) for k in ("w_in", "x_in", "spread", "summed", "used", "chain"))
        scaled = m.sem("scaled")
        block = ctx.enter_context(nc.Block())

        @block.sync
        def _(sp):
            sp.dma_start(w[:, :, :], A["w_out"].rearrange("l (k p) n -> p (l k) n", p=P)).then_inc(w_in, 16)
            sp.dma_start(x1[0:n], x_src).then_inc(x_in, 16)

        @block.tensor
        def _(pe):
            if prompt:
                for c in range(2):
                    last = pe.matmul(psG[:, c, :], K["last"][:, :], K["ada"][:, gate_at + c * 512:gate_at + (c + 1) * 512], start=True, stop=True)
                last.then_inc(spread, 1)
            pe.wait_ge(w_in, 16)
            for t in range(len(tiles)):
                if t >= 2:
                    pe.wait_ge(used, t - 1)
                for c in range(2):
                    for k in range(KD):
                        last = pe.matmul(ps[0:n, t % 2, c, :], mT[:, k, t * P:t * P + n], w[:, k, c * 512:(c + 1) * 512], start=(k == 0), stop=(k == KD - 1))
                last.then_inc(summed, 1)

        @block.vector
        def _(dve):
            then = Chain(dve, chain)
            if not prompt:
                g = K["ada"][0:n, gate_at:gate_at + D]
            else:
                dve.wait_ge(spread, 1)
                then(dve.tensor_copy(gate[:, :], psG[:, :, :].rearrange("p c n -> p (c n)")))
                g = gate[:, :]
            dve.wait_ge(x_in, 16)
            for t in range(len(tiles)):
                dve.wait_ge(summed, t + 1)
                flat = ps[0:n, t % 2].rearrange("p c n -> p (c n)")
                then(dve.tensor_tensor(flat, flat, g, ALU.mult))
                dve.tensor_tensor(x1[0:n, t, :], x1[0:n, t, :], flat, ALU.add).then_inc(used, 1)


def choose(nc, A, K, tag, n, NTI, W, h2T, ids_out, gate_out):
    with ExitStack() as ctx:
        m = Mem(nc, ctx, tag)
        wq, keys, keysT = m.sb("wq", [P, KD, WQ]), m.sb("keys", [P, 2, P]), m.sb("keysT", [P, 2, P])
        qT = m.sb("qT", [P, 2, W])
        s, s2 = m.sb("s", [P, NTI, 2, NK]), m.sb("s2", [P, NTI, 2, NK])
        v, at = m.sb("v", [P, NTI, 2, TK]), m.sb("at", [P, NTI, 2, TK], U32)
        at_f = m.sb("at_f", [P, 2, NTI, TK])
        cand, cand2 = m.sb("cand", [P, NTI, TK, TK]), m.sb("cand2", [P, NTI, TK, TK])
        best, j = m.sb("best", [P, NTI, TK]), m.sb("j", [P, NTI, TK], U32)
        part, part_f = m.sb("part", [P, 2, NTI, TK], U32), m.sb("part_f", [P, 2, NTI, TK])
        one = m.sb("one", [P, NTI, TK, TK])
        picked = m.sb("picked", [P, 2, NTI, TK])
        total = m.sb("total", [P, NTI])
        count_i, count = m.sb("count_i", [P, TK], I32), m.sb("count", [P, TK])
        psK, psQ, psS = m.ps("psK", [P, 2, P]), m.ps("psQ", [P, 2, 512]), m.ps("psS", [P, NTI, 2, NK])
        (w_in, keys_in, turned, keys_copied, summed, q_copied, scored, s_copied, shifted, exped, chain, counted, count_made) = (
            m.sem(k) for k in ("w_in", "keys_in", "turned", "keys_copied", "summed", "q_copied", "scored", "s_copied",
                               "shifted", "exped", "chain", "counted", "count_made"))
        block = ctx.enter_context(nc.Block())
        bc = lambda ap, axis, shape: ap.unsqueeze(axis).to_broadcast(shape)

        @block.sync
        def _(sp):
            with sp.Fori(0, PH) as h:
                sp.wait_ge(summed, h)
                sp.dma_start(wq[:, :, :], A["peer_wq"].rearrange("l (k p) n -> p (l k) n", p=P)[:, :, bass.ds(h * WQ, WQ)]).then_inc(w_in, 16)
                sp.wait_ge(turned, h)
                for k, name in enumerate(("peer_keys1", "peer_keys2")):
                    sp.dma_start(keys[:, k, :], A[name].rearrange("l h n d -> n (l h) d")[:, bass.ds(h, 1), :]).then_inc(keys_in, 16)

        @block.gpsimd
        def _(pool):
            pool.iota(count_i[:, :], pattern=[[1, TK]], base=0, channel_multiplier=0).then_inc(counted, 1)

        @block.tensor
        def _(pe):
            with pe.Fori(0, PH) as h:
                pe.wait_ge(keys_in, h * 32 + 32)
                pe.wait_ge(keys_copied, h)
                for k in range(2):
                    last = pe.transpose(psK[:, k, :], keys[:, k, :], K["ident"][:, :])
                last.then_inc(turned, 1)
                pe.wait_ge(w_in, h * 16 + 16)
                pe.wait_ge(q_copied, h)
                for side in range(2):
                    for k in range(KD):
                        last = pe.matmul(psQ[:, side, 0:W], wq[:, k, side * P:(side + 1) * P], h2T[:, k, :], start=(k == 0), stop=(k == KD - 1))
                last.then_inc(summed, 1)
                pe.wait_ge(keys_copied, h + 1)
                pe.wait_ge(q_copied, h + 1)
                pe.wait_ge(s_copied, h)
                for t in range(NTI):
                    for side in range(2):
                        last = pe.matmul(psS[0:n, t, side, :], qT[:, side, t * P:t * P + n], keysT[:, side, :], start=True, stop=True)
                last.then_inc(scored, 1)

        @block.scalar
        def _(act):
            with act.Fori(0, PH) as h:
                act.wait_ge(turned, h + 1)
                act.wait_ge(scored, h)
                act.activation(keysT[:, :, :], psK[:, :, :], ACT.Copy).then_inc(keys_copied, 1)
                act.wait_ge(summed, h + 1)
                act.activation(qT[:, :, :], psQ[:, :, 0:W], ACT.Copy).then_inc(q_copied, 1)
                act.wait_ge(shifted, h + 1)
                act.activation(best[0:n], best[0:n], ACT.Exp).then_inc(exped, 1)

        @block.vector
        def _(dve):
            dve.wait_ge(counted, 1)
            dve.tensor_copy(count[:, :], count_i[:, :]).then_inc(count_made, 1)
            dve.wait_ge(count_made, 1)
            then = Chain(dve, chain)
            for h in range(PH):
                dve.wait_ge(scored, h + 1)
                then(dve.tensor_copy(s[0:n], psS[0:n]))
                dve.sem_inc(s_copied, 1)

                def top(src, src2, vals, ids):
                    then(dve.max(vals[:, 0:8], src))
                    dve.max_index(ids[:, 0:8], vals[:, 0:8], src)
                    then(dve.match_replace(src2, vals[:, 0:8], src, BIG))
                    then(dve.max(vals[:, 8:16], src2))
                    then(dve.max_index(ids[:, 8:16], vals[:, 8:16], src2))

                for t in range(NTI):
                    for side in range(2):
                        top(s[0:n, t, side, :], s2[0:n, t, side, :], v[0:n, t, side, :], at[0:n, t, side, :])
                shape = [n, NTI, TK, TK]
                for side in range(2):
                    dve.tensor_copy(at_f[0:n, side], at[0:n, :, side, :])
                then(dve.tensor_tensor(cand[0:n], bc(v[0:n, :, 0, :], 3, shape), bc(v[0:n, :, 1, :], 2, shape), ALU.add))
                for t in range(NTI):
                    flat = lambda tile: tile[0:n, t].rearrange("p a b -> p (a b)")
                    top(flat(cand), flat(cand2), best[0:n, t, :], j[0:n, t, :])
                dve.tensor_scalar(part[0:n, 0], j[0:n], 4, None, ALU.logical_shift_right)
                then(dve.tensor_scalar(part[0:n, 1], j[0:n], TK - 1, None, ALU.bitwise_and))
                then(dve.tensor_copy(part_f[0:n], part[0:n]))
                then(dve.tensor_copy(total[0:n, :], best[0:n, :, 0]))
                dve.tensor_tensor(best[0:n], best[0:n], bc(total[0:n, :], 2, [n, NTI, TK]), ALU.subtract).then_inc(shifted, 1)
                every = count[0:n, :].unsqueeze(1).unsqueeze(1).to_broadcast(shape)
                for side in range(2):
                    then(dve.tensor_tensor(one[0:n], bc(part_f[0:n, side], 3, shape), every, ALU.is_equal))
                    then(dve.tensor_tensor(one[0:n], one[0:n], bc(at_f[0:n, side], 2, shape), ALU.mult))
                    then(dve.tensor_reduce(picked[0:n, side], one[0:n], X, ALU.add))
                then(dve.scalar_tensor_tensor(ids_out(h), picked[0:n, 0], float(NK), picked[0:n, 1], ALU.mult, ALU.add))
                dve.wait_ge(exped, h + 1)
                then(dve.tensor_reduce(total[0:n, :], best[0:n], X, ALU.add))
                then(dve.reciprocal(total[0:n, :], total[0:n, :]))
                then(dve.tensor_tensor(gate_out(h), best[0:n], bc(total[0:n, :], 2, [n, NTI, TK]), ALU.mult))


GS = 4
UR, VR = GS, 8
SQUARES = 3
PAGE_LAG = 5


def sample_queries(nc, A, K, M, L):
    with ExitStack() as ctx:
        m = Mem(nc, ctx, "sqr")
        gk_n, gk_r = m.sb("gk_n", [P, 1]), m.sb("gk_r", [ROPE, 1])
        q_n = m.sb("q_n", [P, H * TS])
        w_ukT = m.sb("w_ukT", [P, 2, LAT])
        keys, sq = m.sb("keys", [TS, H, NOPE]), m.sb("sq", [TS, H, NOPE])
        kpe, kpe_sq = m.sb("kpe", [TS, ROPE]), m.sb("kpe_sq", [TS, ROPE])
        ss, kss, rstd = m.sb("ss", [TS, H]), m.sb("kss", [TS, 1]), m.sb("rstd", [TS, H])
        mask = m.sb("mask", [TS, TS, H])
        psT, psQ = m.ps("psT", [P, 2, LAT]), m.ps("psQ", [P, KL, TS, H])
        psK, psR, psE = m.ps("psK", [TS, 2, 512]), m.ps("psR", [TS, TS * H]), m.ps("psE", [TS, ROPE])
        loaded, scaled, turned, copied, q_head, q_copied = (m.sem(k) for k in ("loaded", "scaled", "turned", "copied", "q_head", "q_copied"))
        keyed, squared, rooted, scored, chain, masked, zeroed = (m.sem(k) for k in ("keyed", "squared", "rooted", "scored", "chain", "masked", "zeroed"))
        meaned = m.sem("meaned")
        block = ctx.enter_context(nc.Block())

        @block.sync
        def _(sp):
            sp.dma_start(L["w_uk"][:, :, :], A["w_uk"].rearrange("l (k p) h d -> p (l k) (h d)", p=P)).then_inc(loaded, 16)
            sp.dma_start(gk_n[:, :], A["g_k"][0, 0:NOPE].rearrange("(p a) -> p a", a=1)).then_inc(loaded, 16)
            sp.dma_start(gk_r[:, :], A["g_k"][0, NOPE:DQK].rearrange("(p a) -> p a", a=1)).then_inc(loaded, 16)

        @block.gpsimd
        def _(pool):
            pool.memset(mask[:, :, :], 0.0).then_inc(zeroed, 1)
            pool.wait_ge(zeroed, 1)
            pool.affine_select(out=mask[:, :, :], in_=mask[:, :, :], compare_op=ALU.is_equal, fill=NEG, base=0,
                               pattern=[[-1, TS], [0, H]], channel_multiplier=1).then_inc(masked, 1)

        @block.tensor
        def _(pe):
            pe.wait_ge(loaded, 48)
            pe.wait_ge(scaled, 2)
            for h in range(H):
                if h >= 2:
                    pe.wait_ge(copied, h - 1)
                for k in range(KL):
                    last = pe.transpose(psT[:, h % 2, k * P:(k + 1) * P], L["w_uk"][:, k, h * NOPE:(h + 1) * NOPE], K["ident"][:, :])
                last.then_inc(turned, 1)
                pe.wait_ge(copied, h + 1)
                for k in range(KL):
                    last = pe.matmul(psQ[:, k, :, h], w_ukT[:, h % 2, k * P:(k + 1) * P], q_n[:, h * TS:(h + 1) * TS], start=True, stop=True)
                last.then_inc(q_head, 1)
            for c in range(2):
                for k in range(KL):
                    last = pe.matmul(psK[:, c, :], M["ckvT"][:, k, TP:T], L["w_uk"][:, k, c * 512:(c + 1) * 512], start=(k == 0), stop=(k == KL - 1))
            pe.transpose(psE[:, :], M["kpeT"][:, TP:T], K["ident"][0:ROPE, 0:ROPE]).then_inc(keyed, 1)
            pe.wait_ge(q_copied, 1)
            for k in range(KL):
                pe.matmul(psR[:, :], M["ckvT"][:, k, TP:T], L["q_lat"][:, k].rearrange("p b h -> p (b h)"), start=(k == 0), stop=False)
            pe.matmul(psR[:, :], M["kpeT"][:, TP:T], L["q_rope"][:, :, :].rearrange("p b h -> p (b h)"), start=False, stop=True).then_inc(scored, 1)

        @block.scalar
        def _(act):
            for h in range(H):
                act.wait_ge(turned, h + 1)
                if h >= 2:
                    act.wait_ge(q_head, h - 1)
                act.activation(w_ukT[:, h % 2, :], psT[:, h % 2, :], ACT.Copy).then_inc(copied, 1)
            act.wait_ge(keyed, 1)
            act.activation(sq[:, :, :].rearrange("p h d -> p (h d)"), psK[:, :, :].rearrange("p c n -> p (c n)"), ACT.Square).then_inc(squared, 1)
            act.activation(kpe_sq[:, :], psE[:, :], ACT.Square, accum_out=kss[:, :]).then_inc(squared, 1)
            act.wait_ge(meaned, 1)
            act.activation(rstd[:, :], ss[:, :], ACT.Sqrt, scale=1.0 / DQK, bias=K["eps"][0:TS, :]).then_inc(rooted, 1)

        @block.vector
        def _(dve):
            then = Chain(dve, chain)
            dve.wait_ge(loaded, 48)
            dve.tensor_scalar(q_n[:, :], M["qs_n"][:, :], gk_n[:, :], None, ALU.mult).then_inc(scaled, 1)
            dve.tensor_scalar(L["q_rope"][:, :, :].rearrange("p b h -> p h b"), M["qs_r"][:, :].rearrange("p (h b) -> p h b", h=H),
                              gk_r[:, :], None, ALU.mult).then_inc(scaled, 1)
            dve.wait_ge(q_head, H)
            dve.tensor_copy(L["q_lat"][:, :, :, :], psQ[:, :, :, :]).then_inc(q_copied, 1)
            dve.wait_ge(squared, 2)
            then(dve.tensor_reduce(ss[:, :], sq[:, :, :], X, ALU.add))
            dve.tensor_scalar(ss[:, :], ss[:, :], kss[:, :], None, ALU.add).then_inc(meaned, 1)
            dve.wait_ge(rooted, 1)
            then(dve.reciprocal(rstd[:, :], rstd[:, :]))
            dve.wait_ge(scored, 1)
            dve.wait_ge(masked, 1)
            then(dve.tensor_tensor(L["new"][:, :, :], psR[:, :].rearrange("p (b h) -> p b h", h=H),
                                   rstd[:, :].unsqueeze(1).to_broadcast([TS, TS, H]), ALU.mult))
            dve.tensor_tensor(L["new"][:, :, :], L["new"][:, :, :], mask[:, :, :], ALU.add)


def attend_and_mix(nc, A, K, L, D_, outs):
    with ExitStack() as ctx:
        m = Mem(nc, ctx, "mix")
        ckv, kpe = m.sb("ckv", [P, 2, NT, LAT]), m.sb("kpe", [P, 2, NT, ROPE])
        ckvT, kpeT = m.sb("ckvT", [P, 2, KL, P]), m.sb("kpeT", [ROPE, 2, P])
        sq, kpe_sq = m.sb("sq", [P, H, NOPE]), m.sb("kpe_sq", [P, ROPE])
        q_lat, q_rope = m.sb("q_lat", [P, 2, KL, H]), m.sb("q_rope", [ROPE, 2, H])
        ss, kss, rstd = m.sb("ss", [P, 2, NT, H]), m.sb("kss", [P, 2, NT]), m.sb("rstd", [P, NT, H])
        s = m.sb("s", [P, NT + 1, H])
        top, top_row, diag8, part_sum, share = m.sb("top", [P, H]), m.sb("top_row", [H, 1]), m.sb("diag8", [H, H]), m.sb("part_sum", [P, H]), m.sb("share", [H, 1])
        o_lat = m.sb("o_lat", [H, LAT])
        table = m.sb("table", [1, TS * NT], I32)
        u, v = m.sb("u", [P, UR, D]), m.sb("v", [P, VR, D])
        h2, x1, acc = m.sb("h2", [P, 2, D]), m.sb("x1", [P, D]), m.sb("acc", [P, D])
        ids, gate, gate2 = m.sb("ids", [P, 2, SL], I32), m.sb("gate", [P, 2, SL]), m.sb("gate2", [P, D])
        dots, coef = m.sb("dots", [P, 2, SL]), m.sb("coef", [P, 2, SL])
        psT, psK, psN, psR, psO, psS = (m.ps("psT", [P, 512]), m.ps("psK", [ROPE, P]), m.ps("psN", [P, 2, 512]),
                                        m.ps("psR", [P, 512]), m.ps("psO", [H, 512]), m.ps("psS", [P, 512]))
        psTop, psBc, psSum, psOT = psS[0:H, 0:P], psS[:, 256:264], psS[0:H, 272:273], psS[:, 288:320]
        pages_in = [m.sem(f"pages_in{b}") for b in range(2)]
        pages_used = [m.sem(f"pages_used{b}") for b in range(2)]
        (table_in, q_set, turned, copied, keyed, squared, meaned, rooted, topped, top_turned,
         diag_made, top_spread, shifted, exped, summed, sums_made, sums_turned, weighed, scaled, o_turned, o_kept, chain) = (m.sem(k) for k in (
             "table_in", "q_set", "turned", "copied", "keyed", "squared", "meaned", "rooted", "topped",
             "top_turned", "diag_made", "top_spread", "shifted", "exped", "summed", "sums_made", "sums_turned", "weighed", "scaled",
             "o_turned", "o_kept", "chain"))
        u_in, u_used = [m.sem(f"u_in{k}") for k in range(UR)], [m.sem(f"u_used{k}") for k in range(UR)]
        v_in, v_used = [m.sem(f"v_in{k}") for k in range(VR)], [m.sem(f"v_used{k}") for k in range(VR)]
        tile_in, tile_used = [m.sem(f"tile_in{k}") for k in range(2)], [m.sem(f"tile_used{k}") for k in range(2)]
        gelued, weighted, x1_in, y_made, y_stored, gate2_made, gate2_spread, held = (
            m.sem(k) for k in ("gelued", "weighted", "x1_in", "y_made", "y_stored", "gate2_made", "gate2_spread", "held"))
        block = ctx.enter_context(nc.Block())
        TURNS = TT // 2
        SLOTS = 2 * SL
        SEQS = TS // TURNS
        PAGES = SEQS * NT
        UROUNDS, VROUNDS, GROUPS = SLOTS // UR, SLOTS // VR, SLOTS // GS
        u_rows, v_rows = A["peer_u"].rearrange("l e d -> (l e) d"), A["peer_v"].rearrange("l e d -> (l e) d")

        page_slot = [g * (SLOTS - 14) // (PAGES - 1) for g in range(PAGES)]
        page_at = {x: g for g, x in enumerate(page_slot)}
        square_at = {x + SQUARES: g for g, x in enumerate(page_slot)}
        end = [page_slot[(q + 1) * NT - 1] + PAGE_LAG for q in range(SEQS)]
        ending = lambda x, behind: [q for q in range(SEQS) if end[q] + behind == x]
        LAST_SLOT = end[-1] + 16

        def hold(eng, sem, value):
            eng.wait_ge(sem, value)
            eng.sem_inc(held, 1)

        @block.sync
        def _(sp):
            sp.dma_start(table[:, :], A["page_table"].rearrange("b n -> (b n)").unsqueeze(0)).then_inc(table_in, 16)
            sp.wait_ge(table_in, 16)
            with sp.Fori(0, TURNS) as i:
                for q in range(SEQS):
                    b = q % 2
                    if q % 2 == 0:
                        half = q // 2
                        sp.wait_ge(tile_used[half], i)
                        for tile, name in ((ids, "ids"), (h2, "h2"), (gate, "gate")):
                            sp.dma_start(tile[:, half, :], D_[name][bass.ds(i * 2 + half, 1)].rearrange("a p s -> (a p) s")).then_inc(tile_in[half], 16)
                    sp.wait_ge(pages_used[b], i * (SEQS // 2) + q // 2)
                    for t in range(NT):
                        page = sp.value_load(table[0:1, bass.ds(i * PAGES + (q * NT + t), 1)], min_val=0, max_val=A["cache_ckv"].shape[1] - 1)
                        sp.dma_start(ckv[:, b, t, :], A["cache_ckv"][0, bass.ds(page, 1)].rearrange("a p c -> (a p) c")).then_inc(pages_in[b], 16)
                        sp.dma_start(kpe[:, b, t, :], A["cache_kpe"][0, bass.ds(page, 1)].rearrange("a p c -> (a p) c")).then_inc(pages_in[b], 16)

        @block.gpsimd
        def _(pool):
            with pool.Fori(0, TURNS) as i:
                for x in range(SLOTS):
                    half, slot = x // SL, x % SL
                    if slot == 0:
                        hold(pool, tile_in[half], i * 48 + 48)
                    for ring, n, used, landed, table_rows in ((u, UR, u_used, u_in, u_rows), (v, VR, v_used, v_in, v_rows)):
                        hold(pool, used[x % n], i * (SLOTS // n) + x // n)
                        pool.indirect_dma_start(ring[:, x % n, :], None, table_rows,
                                                bass.IndirectOffsetOnAxis(ids[:, half, slot:slot + 1], 0)).then_inc(landed[x % n], 16)

        @block.tensor
        def _(pe):
            for c in range(2):
                last = pe.matmul(psN[:, c, :], K["last"][:, :], K["ada"][:, 5 * D + c * 512:5 * D + (c + 1) * 512], start=True, stop=True)
            last.then_inc(gate2_spread, 1)
            pe.wait_ge(gate2_made, 1)
            with pe.Fori(0, TURNS) as i:

                def turn(g):
                    q, t = g // NT, g % NT
                    if t == 0:
                        pe.wait_ge(pages_in[q % 2], i * (SEQS // 2 * NT * 32) + (q // 2 + 1) * (NT * 32))
                    pe.wait_ge(copied, (i * PAGES + g) * 2)
                    for k in range(KL):
                        pe.transpose(psT[:, k * P:(k + 1) * P], ckv[:, q % 2, t, k * P:(k + 1) * P], K["ident"][:, :])
                    pe.transpose(psK[:, :], kpe[:, q % 2, t, :], K["ident"][:, :]).then_inc(turned, 1)

                turn(0)
                for x in range(LAST_SLOT):
                    if x in page_at:
                        g = page_at[x]
                        q, t = g // NT, g % NT
                        n = i * SEQS + q
                        if g + 1 < PAGES:
                            turn(g + 1)
                        pe.wait_ge(squared, (i * PAGES + g) * 2)
                        pe.wait_ge(copied, (i * PAGES + (g + 1)) * 2)
                        for c in range(2):
                            for k in range(KL):
                                last = pe.matmul(psN[:, c, :], ckvT[:, g % 2, k, :], L["w_uk"][:, k, c * 512:(c + 1) * 512], start=(k == 0), stop=(k == KL - 1))
                            last.then_inc(keyed, 1)
                        if t == 0:
                            pe.wait_ge(q_set, n * 2 + 2)
                            pe.wait_ge(topped, n)
                        for k in range(KL):
                            pe.matmul(psR[:, t * H:(t + 1) * H], ckvT[:, g % 2, k, :], q_lat[:, q % 2, k, :], start=(k == 0), stop=False)
                        pe.matmul(psR[:, t * H:(t + 1) * H], kpeT[:, g % 2, :], q_rope[:, q % 2, :], start=False, stop=True).then_inc(summed, 1)
                    for q in ending(x, 3):
                        pe.wait_ge(topped, i * SEQS + (q + 1))
                        pe.transpose(psTop, top[:, :], K["ident"][:, :]).then_inc(top_turned, 1)
                    for q in ending(x, 5):
                        pe.wait_ge(diag_made, i * SEQS + (q + 1))
                        pe.matmul(psBc, K["ones"][0:H, :], diag8[:, :], start=True, stop=True).then_inc(top_spread, 1)
                    for q in ending(x, 8):
                        pe.wait_ge(exped, i * SEQS + (q + 1))
                        pe.wait_ge(sums_made, i * SEQS + (q + 1))
                        pe.matmul(psSum, part_sum[:, :], K["ones"][:, 0:1], start=True, stop=True).then_inc(sums_turned, 1)
                        for t in range(NT):
                            pe.matmul(psO[:, :], s[:, t, :], ckv[:, q % 2, t, :], start=(t == 0), stop=False)
                        pe.matmul(psO[:, :], s[0:TS, NT, :], L["ckv_new"][:, :], start=False, stop=True).then_inc(weighed, 1)
                    for q in ending(x, 14):
                        hold(pe, scaled, i * SEQS + (q + 1))
                        for k in range(KL):
                            last = pe.transpose(psOT[:, k * H:(k + 1) * H], o_lat[:, k * P:(k + 1) * P], K["ident"][0:H, 0:H])
                        last.then_inc(o_turned, 1)

        @block.scalar
        def _(act):
            with act.Fori(0, TURNS) as i:

                def copy(g):
                    act.wait_ge(turned, i * PAGES + (g + 1))
                    act.wait_ge(summed, i * PAGES + max(g - 1, 0))
                    act.activation(ckvT[:, g % 2].rearrange("p k n -> p (k n)"), psT[:, :], ACT.Copy).then_inc(copied, 1)
                    act.activation(kpeT[:, g % 2, :], psK[:, :], ACT.Copy).then_inc(copied, 1)

                copy(0)
                for x in range(LAST_SLOT):
                    if x in page_at and page_at[x] + 1 < PAGES:
                        copy(page_at[x] + 1)
                    if x in square_at:
                        g = square_at[x]
                        q, t = g // NT, g % NT
                        act.wait_ge(squared, (i * PAGES + g) * 2)
                        act.activation(kpe_sq[:, :], kpe[:, q % 2, t, :], ACT.Square, accum_out=kss[:, q % 2, t:t + 1])
                        for c in range(2):
                            act.wait_ge(keyed, (i * PAGES + g) * 2 + (c + 1))
                            for h in range(H // 2):
                                last = act.activation(sq[:, c * (H // 2) + h, :], psN[:, c, h * NOPE:(h + 1) * NOPE], ACT.Square,
                                                      accum_out=ss[:, q % 2, t, c * (H // 2) + h:c * (H // 2) + h + 1])
                            last.then_inc(squared, 1)
                    for q in ending(x, 1):
                        act.wait_ge(meaned, i * SEQS + (q + 1))
                        act.activation(rstd[:, :, :], rstd[:, :, :], ACT.Sqrt, scale=1.0 / DQK, bias=K["eps"][:, :]).then_inc(rooted, 1)
                    for q in ending(x, 7):
                        act.wait_ge(shifted, i * SEQS + (q + 1))
                        act.activation(s[:, :, :], s[:, :, :], ACT.Exp, scale=SCALE).then_inc(exped, 1)
                    if x < SLOTS and x % GS == GS - 1:
                        half, at = x // SL, x % SL - (GS - 1)
                        act.wait_ge(u_used[x % UR], i * UROUNDS + (x // UR + 1))
                        act.activation(coef[:, half, at:at + GS], dots[:, half, at:at + GS], ACT.Gelu).then_inc(gelued, 1)
                    if x % SL == SL // 2:
                        act.wait_ge(y_stored, (i * 2 + x // SL) * 16)
                        act.dma_start(x1[:, :], D_["x1"][bass.ds(i * 2 + x // SL, 1)].rearrange("a p s -> (a p) s")).then_inc(x1_in, 16)
                    if x >= SL and x % SL == GS + 2:
                        act.wait_ge(y_made, i * 2 + x // SL)
                        act.dma_start(outs["y_p"][0, bass.ds((i * 2 + (x // SL - 1)) * P, P), :], x1[:, :]).then_inc(y_stored, 16)
            act.wait_ge(y_stored, TT * 16)

        @block.vector
        def _(dve):
            dve.wait_ge(gate2_spread, 1)
            dve.tensor_copy(gate2[:, :], psN[:, :, :].rearrange("p c n -> p (c n)")).then_inc(gate2_made, 1)
            dve.wait_ge(gate2_made, 1)
            with dve.Fori(0, TURNS) as i:
                then = Steps(dve, chain, SEQS * 7 + 2, i)

                def add(x):
                    half, slot = x // SL, x % SL
                    c = coef[:, half, slot:slot + 1]
                    dve.wait_ge(v_in[x % VR], (i * VROUNDS + (x // VR + 1)) * 16)
                    if slot == 0:
                        last = dve.tensor_scalar(acc[:, :], v[:, x % VR, :], c, None, ALU.mult)
                    else:
                        dve.wait_ge(v_used[(x - 1) % VR], i * VROUNDS + ((x - 1) // VR + 1))
                        last = dve.scalar_tensor_tensor(acc[:, :], v[:, x % VR, :], c, acc[:, :], ALU.mult, ALU.add)
                    last.then_inc(v_used[x % VR], 1)
                    if slot == SL - 1:
                        dve.wait_ge(v_used[x % VR], i * VROUNDS + (x // VR + 1))
                        dve.sem_inc(tile_used[half], 1)
                        then(dve.tensor_tensor(acc[:, :], acc[:, :], gate2[:, :], ALU.mult))
                        dve.wait_ge(x1_in, (i * 2 + half) * 16 + 16)
                        dve.tensor_tensor(x1[:, :], x1[:, :], acc[:, :], ALU.add).then_inc(y_made, 1)
                        dve.wait_ge(y_made, i * 2 + (half + 1))

                for x in range(LAST_SLOT):
                    if x in page_at and page_at[x] % NT == 0:
                        q = page_at[x] // NT
                        n = i * SEQS + q
                        dve.tensor_scalar(q_lat[:, q % 2], L["q_lat"][:, :, bass.ds(n, 1), :].rearrange("p k a h -> p k (a h)"), 1.0, None, ALU.mult).then_inc(q_set, 1)
                        dve.tensor_scalar(q_rope[:, q % 2], L["q_rope"][:, bass.ds(n, 1), :].rearrange("p a h -> p (a h)"), 1.0, None, ALU.mult).then_inc(q_set, 1)
                    for q in ending(x, 0):
                        dve.wait_ge(squared, (i * PAGES + (q + 1) * NT) * 2)
                        dve.tensor_tensor(rstd[:, :, :], ss[:, q % 2], kss[:, q % 2].unsqueeze(2).to_broadcast([P, NT, H]), ALU.add).then_inc(meaned, 1)
                    for q in ending(x, 2):
                        n = i * SEQS + q
                        dve.wait_ge(rooted, n + 1)
                        then(dve.reciprocal(rstd[:, :, :], rstd[:, :, :]))
                        dve.wait_ge(summed, (i * PAGES + (q + 1) * NT))
                        dve.tensor_tensor(s[:, 0:NT, :], psR[:, 0:NT * H].rearrange("p (t h) -> p t h", h=H), rstd[:, :, :], ALU.mult)
                        then(dve.memset(s[:, NT, :], NEG))
                        then(dve.tensor_scalar(s[0:TS, NT, :], L["new"][:, bass.ds(n, 1), :].rearrange("p a h -> p (a h)"), 1.0, None, ALU.mult))
                        dve.tensor_reduce(top[:, :], s[:, :, :].rearrange("p t h -> p h t"), X, ALU.max).then_inc(topped, 1)
                    for q in ending(x, 4):
                        dve.wait_ge(top_turned, i * SEQS + (q + 1))
                        then(dve.tensor_reduce(top_row[:, :], psTop, X, ALU.max))
                        dve.tensor_scalar(diag8[:, :], K["ident"][0:H, 0:H], top_row[:, :], None, ALU.mult).then_inc(diag_made, 1)
                    for q in ending(x, 6):
                        dve.wait_ge(top_spread, i * SEQS + (q + 1))
                        dve.tensor_tensor(s[:, :, :], s[:, :, :], psBc.unsqueeze(1).to_broadcast([P, NT + 1, H]), ALU.subtract).then_inc(shifted, 1)
                    for q in ending(x, 8):
                        dve.wait_ge(exped, i * SEQS + (q + 1))
                        dve.tensor_reduce(part_sum[:, :], s[:, :, :].rearrange("p t h -> p h t"), X, ALU.add).then_inc(sums_made, 1)
                    for q in ending(x, 13):
                        dve.wait_ge(sums_turned, i * SEQS + (q + 1))
                        then(dve.reciprocal(share[:, :], psSum))
                        dve.wait_ge(weighed, i * SEQS + (q + 1))
                        then(dve.tensor_scalar(o_lat[:, :], psO[:, :], share[:, :], None, ALU.mult))
                        dve.sem_inc(scaled, 1)
                        dve.sem_inc(pages_used[q % 2], 1)
                    for q in ending(x, 15):
                        dve.wait_ge(o_turned, i * SEQS + (q + 1))
                        then(dve.tensor_scalar(L["o_lat"][:, bass.ds(i * SEQS + q, 1), :].rearrange("p a k -> p (a k)"), psOT, 1.0, None, ALU.mult))
                        dve.sem_inc(o_kept, 1)
                    if x < SLOTS:
                        half, slot = x // SL, x % SL
                        if slot == 0:
                            dve.wait_ge(tile_in[half], i * 48 + 48)
                        dve.wait_ge(u_in[x % UR], (i * UROUNDS + (x // UR + 1)) * 16)
                        dve.tensor_tensor_reduce(u[:, x % UR, :], u[:, x % UR, :], h2[:, half, :], 1.0, 0.0, ALU.mult, ALU.add, dots[:, half, slot:slot + 1]).then_inc(u_used[x % UR], 1)
                    if GS <= x < SLOTS + GS:
                        if x % GS == 0:
                            g = x // GS - 1
                            half, at = g * GS // SL, g * GS % SL
                            dve.wait_ge(gelued, i * GROUPS + (g + 1))
                            dve.tensor_tensor(coef[:, half, at:at + GS], coef[:, half, at:at + GS], gate[:, half, at:at + GS], ALU.mult).then_inc(weighted, 1)
                            dve.wait_ge(weighted, i * GROUPS + (g + 1))
                        add(x - GS)
                then.full()


def sample_values(nc, A, K, L, oT):
    with ExitStack() as ctx:
        m = Mem(nc, ctx, "val")
        w = m.sb("w", [P, KL, H * DV])
        ps = m.ps("ps", [P, H, TS])
        w_in, made = m.sem("w_in"), m.sem("made")
        block = ctx.enter_context(nc.Block())

        @block.sync
        def _(sp):
            sp.dma_start(w[:, :, :], A["w_uv"].rearrange("l (k p) h d -> p (l k) (h d)", p=P)).then_inc(w_in, 16)

        @block.tensor
        def _(pe):
            pe.wait_ge(w_in, 16)
            for h in range(H):
                for k in range(KL):
                    last = pe.matmul(ps[:, h, :], w[:, k, h * DV:(h + 1) * DV], L["o_lat"][:, :, k * H + h], start=(k == 0), stop=(k == KL - 1))
            last.then_inc(made, 1)

        @block.vector
        def _(dve):
            dve.wait_ge(made, 1)
            dve.tensor_copy(oT[:, :, :], ps[:, :, :])


def sample_experts(nc, A, K, h2, x1, ids_f, gate, outs):
    with ExitStack() as ctx:
        m = Mem(nc, ctx, "sex")
        NB = 4
        u, v = m.sb("u", [P, NB, D]), m.sb("v", [P, NB, D])
        idsT, gateT, coef = m.sb("idsT", [P, TS], I32), m.sb("gateT", [P, TS]), m.sb("coef", [P, TS])
        coefs = m.sb("coefs", [P, TS, TS])
        same = m.sb("same", [P, TS, TS])
        row = m.sb("row", [TS, TS, P])
        y = m.sb("y", [TS, D])
        psT, psH, psY = m.ps("psT", [P, 2, TS]), m.ps("psH", [P, 2, 512]), m.ps("psY", [TS, 2, 512])
        filled, made, turned, set_, h_spread, dotted, gelued, weighted, mixed, y_done, chain, stored = (m.sem(k) for k in (
            "filled", "made", "turned", "set", "h_spread", "dotted", "gelued", "weighted", "mixed", "y_done", "chain", "stored"))
        u_in, v_in = [m.sem(f"u_in{k}") for k in range(NB)], [m.sem(f"v_in{k}") for k in range(NB)]
        block = ctx.enter_context(nc.Block())
        u_rows, v_rows = A["peer_u"].rearrange("l e d -> (l e) d"), A["peer_v"].rearrange("l e d -> (l e) d")

        @block.gpsimd
        def _(pool):
            pool.memset(same[:, :, :], 0.0).then_inc(filled, 1)
            pool.memset(row[:, :, :], 1.0).then_inc(filled, 1)
            pool.wait_ge(filled, 2)
            pool.affine_select(out=same[:, :, :], in_=same[:, :, :], compare_op=ALU.not_equal, fill=1.0, base=0,
                               pattern=[[1, TS], [-1, TS]], channel_multiplier=0).then_inc(made, 1)
            pool.affine_select(out=row[:, :, :], in_=row[:, :, :], compare_op=ALU.is_equal, fill=0.0, base=0,
                               pattern=[[-1, TS], [0, P]], channel_multiplier=1).then_inc(made, 1)
            pool.wait_ge(set_, 2)
            for b in range(TS):
                if b >= NB:
                    pool.wait_ge(dotted, b - NB + 1)
                pool.indirect_dma_start(u[:, b % NB, :], None, u_rows, bass.IndirectOffsetOnAxis(idsT[:, b:b + 1], 0)).then_inc(u_in[b % NB], 16)
                if b >= NB:
                    pool.wait_ge(mixed, b - NB + 1)
                pool.indirect_dma_start(v[:, b % NB, :], None, v_rows, bass.IndirectOffsetOnAxis(idsT[:, b:b + 1], 0)).then_inc(v_in[b % NB], 16)

        @block.tensor
        def _(pe):
            pe.transpose(psT[:, 0, :], ids_f[:, :], K["ident"][0:TS, 0:TS])
            pe.transpose(psT[:, 1, :], gate[:, :], K["ident"][0:TS, 0:TS]).then_inc(turned, 1)
            pe.wait_ge(made, 2)
            for b in range(TS + 1):
                if b < TS:
                    if b:
                        pe.wait_ge(dotted, b)
                    for c in range(2):
                        last = pe.matmul(psH[:, c, :], row[:, b, :], h2[:, c * 512:(c + 1) * 512], start=True, stop=True)
                    last.then_inc(h_spread, 1)
                if b:
                    pe.wait_ge(weighted, b)
                    pe.wait_ge(v_in[(b - 1) % NB], 16 * ((b - 1) // NB + 1))
                    for c in range(2):
                        last = pe.matmul(psY[:, c, :], coefs[:, b - 1, :], v[:, (b - 1) % NB, c * 512:(c + 1) * 512], start=(b == 1), stop=(b == TS), skip_group_check=True)
                    last.then_inc(mixed, 1)

        @block.scalar
        def _(act):
            for b in range(TS):
                act.wait_ge(dotted, b + 1)
                act.activation(coef[:, b:b + 1], coef[:, b:b + 1], ACT.Gelu).then_inc(gelued, 1)
            act.wait_ge(y_done, 1)
            act.dma_start(outs["y_s"].rearrange("b t d -> (b t) d"), y[:, :]).then_inc(stored, 16)
            act.wait_ge(stored, 16)

        @block.vector
        def _(dve):
            then = Chain(dve, chain)
            dve.wait_ge(turned, 1)
            dve.tensor_copy(idsT[:, :], psT[:, 0, :]).then_inc(set_, 1)
            dve.tensor_copy(gateT[:, :], psT[:, 1, :]).then_inc(set_, 1)
            dve.wait_ge(set_, 2)
            dve.wait_ge(made, 2)
            for b in range(TS):
                dve.wait_ge(h_spread, b + 1)
                dve.wait_ge(u_in[b % NB], 16 * (b // NB + 1))
                dve.tensor_tensor_reduce(u[:, b % NB, :], u[:, b % NB, :], psH[:, :, :].rearrange("p c n -> p (c n)"), 1.0, 0.0,
                                         ALU.mult, ALU.add, coef[:, b:b + 1]).then_inc(dotted, 1)
                dve.wait_ge(gelued, b + 1)
                then(dve.tensor_tensor(coef[:, b:b + 1], coef[:, b:b + 1], gateT[:, b:b + 1], ALU.mult))
                dve.tensor_scalar(coefs[:, b, :], same[:, b, :], coef[:, b:b + 1], None, ALU.mult).then_inc(weighted, 1)
            dve.wait_ge(mixed, TS)
            then(dve.tensor_tensor(y[:, :], psY[:, :, :].rearrange("p c n -> p (c n)"), K["ada"][0:TS, 5 * D:6 * D], ALU.mult))
            dve.tensor_tensor(y[:, :], y[:, :], x1, ALU.add).then_inc(y_done, 1)


def step(nc, A, outs, D_):
    with ExitStack() as whole:
        m = Mem(nc, whole, "all")
        K = {name: m.sb(name, shape) for name, shape in (
            ("ident", [P, P]), ("ones", [P, P]), ("bias", [P, P]), ("keep", [P, P]), ("swap", [ROPE, ROPE]),
            ("last", [TS + 1, P]), ("eps", [P, 1]), ("ada", [TS + 1, 6 * D]))}
        L = {"q_lat": m.sb("q_lat", [P, KL, TS, H]), "q_rope": m.sb("q_rope", [ROPE, TS, H]), "new": m.sb("new", [TS, TS, H]),
             "ckv_new": m.sb("ckv_new", [TS, LAT]), "o_lat": m.sb("o_lat", [P, TS, KL * H])}
        yT_s = m.sb("yT_s", [P, KI, TS])
        by_tile = lambda ap: ap.rearrange("t p d -> p t d")
        with ExitStack() as front:
            m = Mem(nc, front, "frt")
            constants(nc, K)
            conditioning(nc, A, K)
            S = {"x": m.sb("x", [P, KC, T]), "skip": m.sb("skip", [P, KI]), "g_ssm": m.sb("g_ssm", [P, KI]),
                 "acs": m.sb("acs", [SH, T]), "dt": m.sb("dt", [SH, T]), "a": m.sb("a", [SH, 1]), "decay_s": m.sb("decay_s", [SH, TS]),
                 "dt_tok": m.sb("dt_tok", [P, TT, SH]), "acs_tok": m.sb("acs_tok", [P, TT, SH])}
            with ExitStack() as part:
                part.enter_context(own_semaphores(nc))
                n = Mem(nc, part, "inp")
                h_hi, h_lo = n.sb("h_hi", [P, KD, T], F32R), n.sb("h_lo", [P, KD, T], F32R)
                with ExitStack() as rows_:
                    x = Mem(nc, rows_, "inx").sb("x", [P, TT + 1, D])
                    modulated(nc, K, "mod1", [(x[:, 0:TT, :], A["x_prompt"].rearrange("b (t p) d -> p (b t) d", p=P)),
                                              (x[0:TS, TT, :], A["x_sample"].rearrange("b t d -> (b t) d"))],
                              x, A["g_mix"], 0, D, x, (h_hi, h_lo))
                K["spread"] = n.sb("spread", [SH, DI])
                S["dt_raw"] = n.sb("dt_raw", [SH, T])
                head_channels(nc, K)
                convolution(nc, A, K, S, h_hi, h_lo, D_["proj"], outs)
                sample_scan(nc, A, K, S, h_hi, h_lo, D_["proj"], D_["acs"], outs)
                projection(nc, A, h_hi, h_lo, D_["proj"])
            with ExitStack() as part:
                part.enter_context(own_semaphores(nc))
                prompt_scan(nc, A, K, S, D_["acs"], outs)
            gated_norm(nc, A, K, S, D_["proj"], yT_s)
            oT = m.sb("oT", [P, H * T])
            with ExitStack() as part:
                part.enter_context(own_semaphores(nc))
                n = Mem(nc, part, "mla")
                M = {"ckvT": n.sb("ckvT", [P, KL, T]), "kpeT": n.sb("kpeT", [ROPE, T]), "kpe_sq": n.sb("kpe_sq", [ROPE, T]),
                     "ckv_s": L["ckv_new"], "cos": n.sb("cos", [ROPE, T]), "sin": n.sb("sin", [ROPE, T]),
                     "qs_n": n.sb("qs_n", [P, H * TS]), "qs_r": n.sb("qs_r", [ROPE, H * TS])}
                latents(nc, A, K, M, D_["proj"], outs)
                prompt_attention(nc, A, K, M, D_["proj"], oT)
                L["w_uk"] = n.sb("w_uk", [P, KL, H * NOPE])
                sample_queries(nc, A, K, M, L)
            mT = m.sb("mT", [P, KD, TP])
            merge(nc, A, K, "mrg", D_["proj"], 0, TP, oT[:, :].rearrange("p (h t) -> p h t", h=H)[:, :, 0:TP], S["x"][:, 0:KI, 0:TP], mT)
            x1 = m.sb("x1", [P, TT, D])
            residual(nc, A, K, "res", [P] * TT, 2 * D, mT, A["x_prompt"].rearrange("b (t p) d -> p (b t) d", p=P), x1)
            store(nc, "sx1", [(by_tile(D_["x1"]), x1)])
        with ExitStack() as part:
            part.enter_context(own_semaphores(nc))
            m = Mem(nc, part, "exp")
            h2, h2T = m.sb("h2", [P, TT, D]), m.sb("h2T", [P, KD, TP])
            modulated(nc, K, "mod2", [(h2[:, :, :], by_tile(D_["x1"]))], h2, A["g_ffn"], 3 * D, 4 * D, h2, h2T, samples=False)
            ids, gate = m.sb("ids", [P, TT, SL], I32), m.sb("gate", [P, TT, SL])
            head = lambda tile: (lambda h: tile[:, :, h * TK:(h + 1) * TK])
            choose(nc, A, K, "chs", P, TT, TP, h2T, head(ids), head(gate))
            store(nc, "sh2", [(by_tile(D_["h2"]), h2), (by_tile(D_["ids"]), ids), (by_tile(D_["gate"]), gate)])
        with ExitStack() as part:
            part.enter_context(own_semaphores(nc))
            L["w_uk"] = Mem(nc, part, "mix0").sb("w_uk", [P, KL, H * NOPE])
            load(nc, "ldw", [(L["w_uk"], A["w_uk"].rearrange("l (k p) h d -> p (l k) (h d)", p=P))])
            attend_and_mix(nc, A, K, L, D_, outs)
        with ExitStack() as part:
            part.enter_context(own_semaphores(nc))
            m = Mem(nc, part, "smp")
            oT = m.sb("oT", [P, H, TS])
            sample_values(nc, A, K, L, oT)
            mT, x1, h2, h2T = m.sb("mT", [P, KD, TS]), m.sb("x1", [TS, 1, D]), m.sb("h2", [TS, 1, D]), m.sb("h2T", [P, KD, TS])
            merge(nc, A, K, "mgs", D_["proj"], TP, TS, oT, yT_s, mT)
            residual(nc, A, K, "rss", [TS], 2 * D, mT, A["x_sample"].rearrange("b (t a) d -> b (t a) d", a=1), x1)
            modulated(nc, K, "mod3", [], x1, A["g_ffn"], 3 * D, 4 * D, h2, h2T, prompt=False)
            ids, gate = m.sb("ids", [TS, SL]), m.sb("gate", [TS, SL])
            head = lambda tile: (lambda h: tile[:, h * TK:(h + 1) * TK].unsqueeze(1))
            choose(nc, A, K, "chz", TS, 1, TS, h2T, head(ids), head(gate))
            sample_experts(nc, A, K, h2[:, 0, :], x1[:, 0, :], ids, gate, outs)


def copies(nc, tag, pairs, name):
    with ExitStack() as ctx:
        done = Mem(nc, ctx, tag).sem(name)
        block = ctx.enter_context(nc.Block())

        @block.sync
        def _(sp):
            for to, of in pairs:
                sp.dma_start(to, of).then_inc(done, 16)
            sp.wait_ge(done, 16 * len(pairs))


def store(nc, tag, pairs):
    copies(nc, tag, [(to, of[:]) for to, of in pairs], "stored")


def load(nc, tag, pairs):
    copies(nc, tag, [(to[:], of) for to, of in pairs], "loaded")


_INS = ['x_prompt', 'x_sample', 'c_prompt', 'c_sample', 'cache_ckv', 'cache_kpe', 'page_table', 'state_conv', 'state_ssm',
        'w_ada', 'b_ada', 'g_mix', 'w_in', 'g_q', 'g_ckv', 'w_uk', 'w_uv', 'g_k', 'conv_w', 'conv_b', 'dt_bias', 'a_log',
        'd_skip', 'g_ssm', 'w_br_a', 'w_br_b', 'w_out', 'g_ffn', 'peer_wq', 'peer_keys1', 'peer_keys2', 'peer_u', 'peer_v']
_OUTS = [('y_p', (1, TP, D)), ('y_s', (TS, 1, D)), ('ckv_p', (1, 1, TP, LAT)), ('kpe_p', (1, 1, TP, ROPE)),
         ('conv_p', (1, 1, CW - 1, CD)), ('ssm_p', (1, 1, SH, HD, N)), ('ckv_s', (1, TS, 1, LAT)), ('kpe_s', (1, TS, 1, ROPE)),
         ('conv_s', (1, TS, CW - 1, CD)), ('ssm_s', (1, TS, SH, HD, N))]


def rope_tables():
    half = ROPE // 2
    pos = np.concatenate([np.arange(TP), np.full(TS, PAST)]).astype(np.float32)
    inv = (10000.0 ** (-np.arange(half) / half)).astype(np.float32)
    angle = np.tile(inv[:, None] * pos[None, :], (2, 1))
    return np.cos(angle).astype(np.float32), np.sin(angle).astype(np.float32)


def kernel(**inputs):
    import numpy as _np
    import concourse.bacc as _bacc
    from concourse import mybir as _mybir
    from concourse.bass_utils import run_bass_kernel_spmd as _run

    nc = _bacc.Bacc("TRN2", target_bir_lowering=False, num_devices=1)
    arrays, A = {}, {}

    def give(name, a):
        arrays[f"in_{name}"] = a
        A[name] = nc.dram_tensor(f"in_{name}", a.shape, _mybir.dt.from_np(a.dtype), kind="ExternalInput").ap()

    for name in _INS:
        give(name, _np.ascontiguousarray(inputs[name]))
    cos, sin = rope_tables()
    give("rope_cos", cos)
    give("rope_sin", sin)
    outs = {name: nc.dram_tensor(f"out_{name}", shape, F32, kind="ExternalOutput").ap() for name, shape in _OUTS}
    D_ = {name: nc.dram_tensor(f"keep_{name}", shape, dt, kind="Internal").ap() for name, shape, dt in (
        ("proj", (C_GB + KD, P, T), F32), ("acs", (SH, TP), F32), ("x1", (TT, P, D), F32), ("h2", (TT, P, D), F32),
        ("ids", (TT, P, SL), I32), ("gate", (TT, P, SL), F32))}
    step(nc, A, outs, D_)
    r = _run(nc, [arrays], core_ids=[0])
    return tuple(r.results[0][f"out_{name}"] for name, _ in _OUTS)
```

```python
from contextlib import ExitStack, contextmanager

import numpy as np

import concourse.bass as bass
from concourse import mybir

F32 = mybir.dt.float32
I32 = mybir.dt.int32
F32R = mybir.dt.float32r
U32 = mybir.dt.uint32
ALU = mybir.AluOpType
ACT = mybir.ActivationFunctionType
X = mybir.AxisListType.X

P = 128
D = 1024
KD = D // P
TP = 512
TS = 8
T = TP + TS
TT = TP // P
H = 8
NOPE, ROPE, DV, LAT = 128, 64, 128, 512
DQK = NOPE + ROPE
KL = LAT // P
PAST, PAGE = 2048, 128
NT = PAST // PAGE
DI, HD, SH, G, N = 2048, 64, 32, 4, 128
KI = DI // P
CD = DI + 2 * G * N
KC = CD // P
CW = 4
PH, NK, DK, TK = 8, 128, 256, 16
SL = PH * TK
IN = H * DQK + LAT + ROPE + DI + CD + SH + 2 * D
EPS = 1e-6
HALF = T // 2
NEG = -1e30

C_Q, C_CKV, C_KPE, C_Z, C_XBC, C_DT, C_GA, C_GB = 0, 12, 16, 17, 33, 57, 58, 66


class Chain:

    def __init__(self, eng, sem):
        self.eng, self.sem, self.n = eng, sem, 0

    def __call__(self, ins):
        self.n += 1
        ins.then_inc(self.sem, 1)
        self.eng.wait_ge(self.sem, self.n)


class Mem:

    def __init__(self, nc, ctx, tag):
        self.nc, self.ctx, self.tag = nc, ctx, tag

    def sb(self, name, shape, dt=F32):
        return self.ctx.enter_context(self.nc.sbuf_tensor(f"{self.tag}_{name}", shape, dt))

    def ps(self, name, shape, dt=F32):
        return self.ctx.enter_context(self.nc.psum_tensor(f"{self.tag}_{name}", shape, dt))

    def sem(self, name):
        return self.nc.alloc_semaphore(f"{self.tag}_{name}")


@contextmanager
def own_semaphores(nc):
    before = nc.snapshot_sems()
    yield
    nc.clear_and_free_semaphores(nc.allocated_since(before))
    nc.all_engine_barrier()


def rows(t):
    return P if t < TT else TS


def constants(nc, K):
    with ExitStack() as ctx:
        m = Mem(nc, ctx, "cst")
        filled, made = m.sem("filled"), m.sem("made")
        block = ctx.enter_context(nc.Block())

        @block.gpsimd
        def _(pool):
            for tile, value in ((K["ident"], 0.0), (K["ones"], 1.0), (K["bias"], 0.0), (K["keep"], 1.0),
                                (K["swap"], 0.0), (K["last"], 0.0), (K["eps"], EPS)):
                pool.memset(tile[:], value).then_inc(filled, 1)
            pool.wait_ge(filled, 7)
            pool.affine_select(out=K["ident"][:, :], in_=K["ident"][:, :], compare_op=ALU.not_equal, fill=1.0,
                               base=0, pattern=[[-1, P]], channel_multiplier=1).then_inc(made, 1)
            pool.affine_select(out=K["bias"][:, :], in_=K["bias"][:, :], compare_op=ALU.is_ge, fill=NEG,
                               base=0, pattern=[[-1, P]], channel_multiplier=1).then_inc(made, 1)
            pool.affine_select(out=K["keep"][:, :], in_=K["keep"][:, :], compare_op=ALU.is_ge, fill=0.0,
                               base=0, pattern=[[1, P]], channel_multiplier=-1).then_inc(made, 1)
            pool.affine_select(out=K["swap"][:, :], in_=K["swap"][:, :], compare_op=ALU.not_equal, fill=-1.0,
                               base=-ROPE // 2, pattern=[[-1, ROPE]], channel_multiplier=1).then_inc(made, 1)
            pool.affine_select(out=K["last"][:, :], in_=K["last"][:, :], compare_op=ALU.not_equal, fill=1.0,
                               base=-TS, pattern=[[0, P]], channel_multiplier=1).then_inc(made, 1)
            pool.wait_ge(made, 5)
            pool.affine_select(out=K["swap"][:, :], in_=K["swap"][:, :], compare_op=ALU.not_equal, fill=1.0,
                               base=ROPE // 2, pattern=[[-1, ROPE]], channel_multiplier=1).then_inc(made, 1)
            pool.wait_ge(made, 6)


def head_channels(nc, K):
    with ExitStack() as ctx:
        m = Mem(nc, ctx, "hch")
        made = m.sem("made")
        block = ctx.enter_context(nc.Block())

        @block.gpsimd
        def _(pool):
            pool.memset(K["spread"][:, :], 1.0).then_inc(made, 1)
            pool.wait_ge(made, 1)
            pool.affine_select(out=K["spread"][:, :], in_=K["spread"][:, :], compare_op=ALU.is_ge, fill=0.0,
                               base=0, pattern=[[1, DI]], channel_multiplier=-HD).then_inc(made, 1)
            pool.wait_ge(made, 2)
            pool.affine_select(out=K["spread"][:, :], in_=K["spread"][:, :], compare_op=ALU.is_ge, fill=0.0,
                               base=HD - 1, pattern=[[-1, DI]], channel_multiplier=HD)


def conditioning(nc, A, K):
    NG = 6 * D // 512
    with ExitStack() as ctx:
        m = Mem(nc, ctx, "ada")
        c_rows, cT = m.sb("c_rows", [TS + 1, D]), m.sb("cT", [P, KD, TS + 1])
        bias = m.sb("bias", [TS + 1, 6 * D])
        w = m.sb("w", [P, 2, KD, 512])
        psT, psA = m.ps("psT", [P, KD, TS + 1]), m.ps("psA", [TS + 1, 2, 512])
        c_in, bias_in = m.sem("c_in"), m.sem("bias_in")
        w_in = [m.sem(f"w_in{b}") for b in range(2)]
        turned, cT_ready = m.sem("turned"), m.sem("cT_ready")
        summed = [m.sem(f"summed{b}") for b in range(2)]
        added = [m.sem(f"added{b}") for b in range(2)]
        block = ctx.enter_context(nc.Block())
        w_view = A["w_ada"].rearrange("l (k p) n -> p (l k) n", p=P)

        @block.sync
        def _(sp):
            sp.dma_start(c_rows[0:TS, :], A["c_sample"]).then_inc(c_in, 16)
            sp.dma_start(c_rows[TS:TS + 1, :], A["c_prompt"]).then_inc(c_in, 16)
            sp.dma_start(bias[:, :], A["b_ada"].to_broadcast([TS + 1, 6 * D])).then_inc(bias_in, 16)
            with sp.Fori(0, NG // 2) as i:
                for b in range(2):
                    sp.wait_ge(summed[b], i)
                    sp.dma_start(w[:, b], w_view[:, :, bass.ds(i * 1024 + b * 512, 512)]).then_inc(w_in[b], 16)

        @block.tensor
        def _(pe):
            pe.wait_ge(c_in, 32)
            for k in range(KD):
                last = pe.transpose(psT[:, k, :], c_rows[:, k * P:(k + 1) * P], K["ident"][0:TS + 1, 0:TS + 1])
            last.then_inc(turned, 1)
            pe.wait_ge(cT_ready, 1)
            with pe.Fori(0, NG // 2) as i:
                for b in range(2):
                    pe.wait_ge(w_in[b], i * 16 + 16)
                    pe.wait_ge(added[b], i)
                    for k in range(KD):
                        last = pe.matmul(psA[:, b, :], cT[:, k, :], w[:, b, k, :], start=(k == 0), stop=(k == KD - 1))
                    last.then_inc(summed[b], 1)

        @block.vector
        def _(dve):
            dve.wait_ge(turned, 1)
            dve.tensor_copy(cT[:, :, :], psT[:, :, :]).then_inc(cT_ready, 1)
            dve.wait_ge(bias_in, 16)
            with dve.Fori(0, NG // 2) as i:
                for b in range(2):
                    dve.wait_ge(summed[b], i + 1)
                    at = bass.ds(i * 1024 + b * 512, 512)
                    dve.tensor_tensor(K["ada"][:, at], psA[:, b, :], bias[:, at], ALU.add).then_inc(added[b], 1)


def modulated(nc, K, tag, load, x, gain, shift_at, scale_at, out, outT, prompt=True, samples=True):
    NP = TT if prompt else 0
    tiles = [P] * NP + [TS] * samples
    NA = len(tiles)
    halves = isinstance(outT, tuple)
    with ExitStack() as ctx:
        m = Mem(nc, ctx, tag)
        gain_bc = m.sb("gain", [P, D])
        mul_p, add_p, mul_s = m.sb("mul_p", [P, D]), m.sb("add_p", [P, D]), m.sb("mul_s", [TS, D])
        squares = m.sb("squares", [P, D])
        ss, ms, rms, rstd = (m.sb(n, [P, NA]) for n in ("ss", "ms", "rms", "rstd"))
        psB = m.ps("psB", [P, 4, 512])
        psT = m.ps("psT", [P, 2, 4, P])
        x_in, gain_in, spread = m.sem("x_in"), m.sem("gain_in"), m.sem("spread")
        summed, meaned, rooted = m.sem("summed"), m.sem("meaned"), m.sem("rooted")
        rounded = m.sem("rounded")
        normed, turned, copied, chain = m.sem("normed"), m.sem("turned"), m.sem("copied"), m.sem("chain")
        stats = [(P, slice(0, NP))] * prompt + [(TS, slice(NP, NA))] * samples
        block = ctx.enter_context(nc.Block())

        @block.sync
        def _(sp):
            sp.dma_start(gain_bc[:, :], gain.to_broadcast([P, D])).then_inc(gain_in, 16)
            for dst, src in load:
                sp.dma_start(dst, src).then_inc(x_in, 16)

        @block.scalar
        def _(act):
            act.wait_ge(x_in, 16 * len(load)) if load else None
            for t, n in enumerate(tiles):
                if t:
                    act.wait_ge(summed, t)
                act.activation(squares[0:n, :], x[0:n, t, :], ACT.Square, accum_out=ss[0:n, t:t + 1]).then_inc(summed, 1)
            act.wait_ge(meaned, len(stats))
            for n, cols in stats:
                act.activation(rms[0:n, cols], ms[0:n, cols], ACT.Sqrt).then_inc(rooted, 1)
            for j in range(2 * NA if halves else 0):
                t, c = j // 2, j % 2
                act.wait_ge(turned, j + 1)
                act.activation(outT[0][:, 4 * c:4 * c + 4, t * P:t * P + tiles[t]], psT[:, j % 2, :, 0:tiles[t]], ACT.Copy).then_inc(rounded, 1)

        @block.tensor
        def _(pe):
            for j, at in enumerate((shift_at, scale_at)):
                for c in range(2):
                    last = pe.matmul(psB[:, 2 * j + c, :], K["last"][:, :], K["ada"][:, at + c * 512:at + (c + 1) * 512],
                                     start=True, stop=True)
            last.then_inc(spread, 1)
            for t, n in enumerate(tiles):
                pe.wait_ge(normed, t + 1)
                for c in range(2):
                    j = 2 * t + c
                    if j >= 2:
                        pe.wait_ge(copied, j - 1)
                    for k in range(4):
                        last = pe.transpose(psT[:, j % 2, k, 0:n], out[0:n, t, (4 * c + k) * P:(4 * c + k + 1) * P],
                                            K["ident"][0:n, 0:n])
                    last.then_inc(turned, 1)

        @block.vector
        def _(dve):
            then = Chain(dve, chain)
            dve.wait_ge(gain_in, 16)
            dve.wait_ge(spread, 1)
            dve.tensor_copy(add_p[:, :].rearrange("p (c n) -> p c n", c=2), psB[:, 0:2, :])
            dve.scalar_tensor_tensor(mul_p[:, :].rearrange("p (c n) -> p c n", c=2), psB[:, 2:4, :], 1.0,
                                     gain_bc[:, :].rearrange("p (c n) -> p c n", c=2), ALU.add, ALU.mult)
            dve.scalar_tensor_tensor(mul_s[:, :], K["ada"][0:TS, scale_at:scale_at + D], 1.0, gain_bc[0:TS, :],
                                     ALU.add, ALU.mult)
            dve.wait_ge(summed, NA)
            for n, cols in stats:
                dve.tensor_scalar(ms[0:n, cols], ss[0:n, cols], 1.0 / D, EPS, ALU.mult, ALU.add).then_inc(meaned, 1)
            dve.wait_ge(rooted, len(stats))
            for n, cols in stats:
                then(dve.reciprocal(rstd[0:n, cols], rms[0:n, cols]))

            def copy(j):
                t, c = j // 2, j % 2
                n = tiles[t]
                place = (slice(None), slice(4 * c, 4 * c + 4), slice(t * P, t * P + n))
                if halves:
                    lower(dve, outT[0][place], outT[1][place], psT[:, j % 2, :, 0:n], rounded, copied, j + 1)
                else:
                    dve.wait_ge(turned, j + 1)
                    dve.tensor_copy(outT[place], psT[:, j % 2, :, 0:n]).then_inc(copied, 1)

            for t, n in enumerate(tiles):
                mul, add = (mul_p, add_p[:, :]) if t < NP else (mul_s, K["ada"][0:TS, shift_at:shift_at + D])
                then(dve.scalar_tensor_tensor(out[0:n, t, :], x[0:n, t, :], rstd[0:n, t:t + 1], mul[0:n, :],
                                              ALU.mult, ALU.mult))
                dve.tensor_tensor(out[0:n, t, :], out[0:n, t, :], add, ALU.add).then_inc(normed, 1)
                if t:
                    copy(2 * t - 2)
                    copy(2 * t - 1)
            copy(2 * NA - 2)
            copy(2 * NA - 1)


def lower(dve, hi, lo, x, hi_made, lo_made, value):
    dve.wait_ge(hi_made, value)
    dve.tensor_tensor(lo, x, hi.bitcast(F32), ALU.subtract).then_inc(lo_made, 1)


def products(pe, out, w_parts, x_parts, first, last):
    (w_hi, w_lo), (x_hi, x_lo) = w_parts, x_parts
    pe.matmul(out, w_hi, x_hi, start=first, stop=False)
    pe.matmul(out, w_hi, x_lo, start=False, stop=False)
    return pe.matmul(out, w_lo, x_hi, start=False, stop=last)


def weights_in(sp, w, w_view, w_in, lowered, columns, first, end):
    for c, at in list(enumerate(columns))[first:end]:
        if c >= 2:
            sp.wait_ge(lowered, c - 1)
        sp.dma_start(w[:, c % 2], w_view[:, :, at:at + P]).then_inc(w_in[c % 2], 16)


def round_weights(pool, w, w_hi, w_in, multiplied, rounded, c):
    pool.wait_ge(w_in[c % 2], 16 * (c // 2 + 1))
    if c >= 4:
        pool.wait_ge(multiplied, c - 3)
    pool.tensor_copy(w_hi[:, c % 4], w[:, c % 2]).then_inc(rounded, 1)


def chunk_product(pe, out, c, w_hi, w_lo, h_hi, h_lo):
    for k in range(KD):
        for s in range(2):
            cols = slice(s * HALF, (s + 1) * HALF)
            last = products(pe, out[:, s, 0:HALF], (w_hi[:, c % 4, k, :], w_lo[:, c % 4, k, :]),
                            (h_hi[:, k, cols], h_lo[:, k, cols]), k == 0, k == KD - 1)
    return last


def chunks_from(first, n):
    return [first + P * j for j in range(n)]


SCALE = float(DQK) ** -0.5


class Steps:

    def __init__(self, eng, sem, n, turn):
        self.eng, self.sem, self.size, self.base, self.n = eng, sem, n, turn * n, 0

    def __call__(self, ins):
        self.n += 1
        ins.then_inc(self.sem, 1)
        self.eng.wait_ge(self.sem, self.base + self.n)

    def full(self):
        assert self.n == self.size, self.n


def latents(nc, A, K, M, proj, outs):
    with ExitStack() as ctx:
        m = Mem(nc, ctx, "lat")
        raw, sq = m.sb("raw", [P, KL, T]), m.sb("sq", [P, KL, T])
        rstd, turned = m.sb("rstd", [P, 2, HALF]), m.sb("turned", [ROPE, 2, HALF])
        gain = m.sb("gain", [P, KL])
        by_token, kpe_by_token = m.sb("by_token", [P, 2, LAT]), m.sb("kpe_by_token", [P, 2, ROPE])
        psN, psR = m.ps("psN", [P, 2, 512]), m.ps("psR", [ROPE, 2, 512])
        psT, psK = m.ps("psT", [P, 2, 512]), m.ps("psK", [P, 2, 512])
        raw_in, squared, summed, swapped = m.sem("raw_in"), m.sem("squared"), m.sem("summed"), m.sem("swapped")
        rooted, ready, chain = m.sem("rooted"), m.sem("ready"), m.sem("chain")
        moved, copied = m.sem("moved"), m.sem("copied")
        stored = [m.sem(f"stored{b}") for b in range(2)]
        block = ctx.enter_context(nc.Block())
        flat = proj.rearrange("c p t -> (c p) t")
        halves = lambda ap: ap.rearrange("p (s t) -> p s t", s=2)

        @block.sync
        def _(sp):
            sp.dma_start(raw[:, :, :], proj[C_CKV:C_CKV + KL].rearrange("c p t -> p c t")).then_inc(raw_in, 16)
            sp.dma_start(M["kpeT"][:, :], proj[C_KPE, 0:ROPE, :]).then_inc(raw_in, 16)
            sp.dma_start(gain[:, :], A["g_ckv"].rearrange("l (k p) -> p (l k)", p=P), allow_slow_non_contiguous=True).then_inc(raw_in, 16)
            sp.dma_start(M["cos"][:, :], A["rope_cos"]).then_inc(raw_in, 16)
            sp.dma_start(M["sin"][:, :], A["rope_sin"]).then_inc(raw_in, 16)
            for t in range(TT + 1):
                n, b = rows(t), t % 2
                sp.wait_ge(copied, 2 * t + 2)
                where = (outs["ckv_p"][0, 0, t * P:t * P + n, :], outs["kpe_p"][0, 0, t * P:t * P + n, :]) if t < TT else \
                    (outs["ckv_s"][0, :, 0, :], outs["kpe_s"][0, :, 0, :])
                sp.dma_start(where[0], by_token[0:n, b, :]).then_inc(stored[b], 16)
                sp.dma_start(where[1], kpe_by_token[0:n, b, :]).then_inc(stored[b], 16)
            sp.wait_ge(stored[0], 96)
            sp.wait_ge(stored[1], 64)

        @block.scalar
        def _(act):
            act.wait_ge(raw_in, 80)
            act.activation(sq[:, :, :], raw[:, :, :], ACT.Square).then_inc(squared, 1)
            act.wait_ge(summed, 1)
            act.activation(rstd[:, :, :], psN[:, :, 0:HALF], ACT.Sqrt, scale=1.0 / LAT, bias=K["eps"][:, :]).then_inc(rooted, 1)
            act.wait_ge(ready, 1)
            act.activation(M["kpe_sq"][:, :], M["kpeT"][:, :], ACT.Square).then_inc(rooted, 1)

        @block.tensor
        def _(pe):
            pe.wait_ge(raw_in, 80)
            for s in range(2):
                last = pe.matmul(psR[:, s, 0:HALF], K["swap"][:, :], M["kpeT"][:, s * HALF:(s + 1) * HALF], start=True, stop=True)
            last.then_inc(swapped, 1)
            pe.wait_ge(squared, 1)
            for s in range(2):
                for k in range(KL):
                    last = pe.matmul(psN[:, s, 0:HALF], K["ones"][:, :], sq[:, k, s * HALF:(s + 1) * HALF],
                                     start=(k == 0), stop=(k == KL - 1))
            last.then_inc(summed, 1)
            pe.wait_ge(ready, 2)
            for t in range(TT + 1):
                n, b = rows(t), t % 2
                if t >= 2:
                    pe.wait_ge(copied, 2 * t - 2)
                for k in range(KL):
                    pe.transpose(psT[0:n, b, k * P:(k + 1) * P], M["ckvT"][:, k, t * P:t * P + n], K["ident"][:, :])
                pe.transpose(psK[0:n, b, 0:ROPE], M["kpeT"][:, t * P:t * P + n], K["ident"][0:ROPE, 0:ROPE]).then_inc(moved, 1)

        @block.vector
        def _(dve):
            then = Chain(dve, chain)
            dve.wait_ge(raw_in, 80)
            dve.wait_ge(swapped, 1)
            dve.tensor_tensor(turned[:, :, :], psR[:, :, 0:HALF], halves(M["sin"][:, :]), ALU.mult)
            then(dve.tensor_tensor(M["kpeT"][:, :], M["kpeT"][:, :], M["cos"][:, :], ALU.mult))
            dve.tensor_tensor(halves(M["kpeT"][:, :]), halves(M["kpeT"][:, :]), turned[:, :, :], ALU.add).then_inc(ready, 1)
            dve.wait_ge(rooted, 1)
            then(dve.reciprocal(rstd[:, :, :], rstd[:, :, :]))
            for k in range(KL):
                last = dve.scalar_tensor_tensor(halves(M["ckvT"][:, k, :]), halves(raw[:, k, :]), gain[:, k:k + 1],
                                                rstd[:, :, :], ALU.mult, ALU.mult)
            last.then_inc(ready, 1)
            for t in range(TT + 1):
                n, b = rows(t), t % 2
                dve.wait_ge(moved, t + 1)
                if t >= 2:
                    dve.wait_ge(stored[b], 32 * (t // 2))
                dve.tensor_copy(by_token[0:n, b, :], psT[0:n, b, :]).then_inc(copied, 1)
                dve.tensor_copy(kpe_by_token[0:n, b, :], psK[0:n, b, 0:ROPE]).then_inc(copied, 1)
                if t == TT:
                    dve.wait_ge(copied, 2 * t + 2)
                    dve.tensor_copy(M["ckv_s"][:, :], by_token[0:n, b, :])


def prompt_attention(nc, A, K, M, proj, oT):
    with ExitStack() as ctx:
        m = Mem(nc, ctx, "att")
        q_n, q_r = m.sb("q_n", [P, 2, T]), m.sb("q_r", [ROPE, 2, T])
        w_uk, w_uv = m.sb("w_uk", [P, 2, KL, NOPE]), m.sb("w_uv", [P, 2, KL, DV])
        turned, sq_n, sq_r = m.sb("turned", [ROPE, T]), m.sb("sq_n", [P, T]), m.sb("sq_r", [ROPE, T])
        sq_k = m.sb("sq_k", [P, TP])
        root_q, root_k = m.sb("root_q", [P, T]), m.sb("root_k", [P, TP])
        k_n, k_r, v = m.sb("k_n", [P, TP]), m.sb("k_r", [ROPE, TP]), m.sb("v", [P, TT, DV])
        probs, probsT = m.sb("probs", [P, TT, TP]), m.sb("probsT", [P, 2, TT, P])
        top, shift, total, share = (m.sb(n, [P, TT]) for n in ("top", "shift", "total", "share"))
        bank = [m.ps(f"bank{b}", [P, 512]) for b in range(8)]
        psV, psT, psO = bank[4], bank[5:7], bank[7]
        gq_n, gq_r, gk_n, gk_r = m.sb("gq_n", [P, 1]), m.sb("gq_r", [ROPE, 1]), m.sb("gk_n", [P, 1]), m.sb("gk_r", [ROPE, 1])
        gains_in, chain = m.sem("gains_in"), m.sem("chain")
        head_in = [m.sem(f"head_in{b}") for b in range(2)]
        head_done = [m.sem(f"head_done{b}") for b in range(2)]
        (swapped, keyed, valued, q_sq, r_roped, r_sq, k_sq, q_summed, k_summed, q_rooted, k_rooted, prepared, v_copied,
         scored, shifted, exped, shared, turned_p, copied_p, weighed) = (m.sem(n) for n in (
             "swapped", "keyed", "valued", "q_sq", "r_roped", "r_sq", "k_sq", "q_summed", "k_summed", "q_rooted",
             "k_rooted", "prepared", "v_copied", "scored", "shifted", "exped", "shared", "turned_p", "copied_p", "weighed"))
        block = ctx.enter_context(nc.Block())
        q_view = proj.rearrange("c p t -> (c p) t")

        @block.sync
        def _(sp):
            for tile, src in ((gq_n, A["g_q"][0, 0:NOPE]), (gq_r, A["g_q"][0, NOPE:DQK]),
                              (gk_n, A["g_k"][0, 0:NOPE]), (gk_r, A["g_k"][0, NOPE:DQK])):
                sp.dma_start(tile[:, :], src.rearrange("(p a) -> p a", a=1)).then_inc(gains_in, 16)

            for h in range(H):
                b = h % 2
                if h >= 2:
                    sp.wait_ge(head_done[b], h // 2)
                sp.dma_start(q_n[:, b, :], q_view[h * DQK:h * DQK + NOPE, :]).then_inc(head_in[b], 16)
                sp.dma_start(q_r[:, b, :], q_view[h * DQK + NOPE:(h + 1) * DQK, :]).then_inc(head_in[b], 16)
                sp.dma_start(w_uk[:, b], A["w_uk"].rearrange("l (k p) h d -> p (l k) (h d)", p=P)[:, :, h * NOPE:(h + 1) * NOPE]).then_inc(head_in[b], 16)
                sp.dma_start(w_uv[:, b], A["w_uv"].rearrange("l (k p) h d -> p (l k) (h d)", p=P)[:, :, h * DV:(h + 1) * DV]).then_inc(head_in[b], 16)

        @block.tensor
        def _(pe):
            def keys(h):
                b = h % 2
                pe.wait_ge(head_in[b], 64 * (h // 2 + 1))
                if h:
                    pe.wait_ge(exped, h * TT)
                for k in range(KL):
                    last = pe.matmul(bank[2][:, :], w_uk[:, b, k, :], M["ckvT"][:, k, 0:TP], start=(k == 0), stop=(k == KL - 1))
                last.then_inc(keyed, 1)
                for s in range(2):
                    last = pe.matmul(bank[s][0:ROPE, 0:HALF], K["swap"][:, :], q_r[:, b, s * HALF:(s + 1) * HALF], start=True, stop=True)
                last.then_inc(swapped, 1)
                if h:
                    pe.wait_ge(v_copied, h)
                for t in range(TT):
                    for k in range(KL):
                        last = pe.matmul(psV[:, t * DV:(t + 1) * DV], M["ckvT"][:, k, t * P:(t + 1) * P], w_uv[:, b, k, :],
                                         start=(k == 0), stop=(k == KL - 1))
                last.then_inc(valued, 1)

            def sums(h):
                pe.wait_ge(k_sq, h + 1)
                pe.matmul(bank[3][:, :], K["ones"][:, :], sq_k[:, :], start=True, stop=False)
                pe.matmul(bank[3][:, :], K["ones"][0:ROPE, :], M["kpe_sq"][:, 0:TP], start=False, stop=True).then_inc(k_summed, 1)
                pe.wait_ge(q_sq, h + 1)
                pe.wait_ge(r_sq, h + 1)
                for s in range(2):
                    pe.matmul(bank[s][:, 0:HALF], K["ones"][:, :], sq_n[:, s * HALF:(s + 1) * HALF], start=True, stop=False)
                    last = pe.matmul(bank[s][:, 0:HALF], K["ones"][0:ROPE, :], sq_r[:, s * HALF:(s + 1) * HALF], start=False, stop=True)
                last.then_inc(q_summed, 1)

            def scores(h):
                b = h % 2
                pe.wait_ge(prepared, h + 1)
                for q in range(TT):
                    w = (q + 1) * P
                    pe.matmul(bank[q][:, 0:w], q_n[:, b, q * P:w], k_n[:, 0:w], start=True, stop=False)
                    pe.matmul(bank[q][:, 0:w], q_r[:, b, q * P:w], k_r[:, 0:w], start=False, stop=True).then_inc(scored, 1)

            def weighing(h):
                def turn(q):
                    pe.wait_ge(shared, h * TT + (q + 1))
                    if q >= 2:
                        pe.wait_ge(copied_p, h * TT + (q - 1))
                    for k in range(q + 1):
                        last = pe.transpose(psT[q % 2][:, k * P:(k + 1) * P], probs[:, q, k * P:(k + 1) * P], K["ident"][:, :])
                    last.then_inc(turned_p, 1)

                def weigh(q):
                    pe.wait_ge(copied_p, h * TT + (q + 1))
                    if q == 0:
                        pe.wait_ge(v_copied, h + 1)
                        if h:
                            pe.wait_ge(head_done[(h - 1) % 2], (h - 1) // 2 + 1)
                    for k in range(q + 1):
                        last = pe.matmul(psO[:, q * P:(q + 1) * P], v[:, k, :], probsT[:, q % 2, k, :], start=(k == 0), stop=(k == q))
                    last.then_inc(weighed, 1)

                turn(0)
                turn(1)
                weigh(0)
                turn(2)
                weigh(1)
                turn(3)
                weigh(2)
                weigh(3)

            keys(0)
            sums(0)
            for h in range(H):
                scores(h)
                if h + 1 < H:
                    keys(h + 1)
                    sums(h + 1)
                weighing(h)

        @block.scalar
        def _(act):
            def squares(h):
                b = h % 2
                act.wait_ge(head_in[b], 64 * (h // 2 + 1))
                act.activation(sq_n[:, :], q_n[:, b, :], ACT.Square).then_inc(q_sq, 1)
                act.wait_ge(keyed, h + 1)
                act.activation(sq_k[:, :], bank[2][:, :], ACT.Square).then_inc(k_sq, 1)
                act.wait_ge(r_roped, h + 1)
                act.activation(sq_r[:, :], q_r[:, b, :], ACT.Square).then_inc(r_sq, 1)

            def roots(h):
                act.wait_ge(k_summed, h + 1)
                act.activation(root_k[:, :], bank[3][:, :], ACT.Sqrt, scale=1.0 / DQK, bias=K["eps"][:, :]).then_inc(k_rooted, 1)
                act.wait_ge(q_summed, h + 1)
                for s in range(2):
                    act.activation(root_q[:, s * HALF:(s + 1) * HALF], bank[s][:, 0:HALF], ACT.Sqrt, scale=1.0 / DQK,
                                   bias=K["eps"][:, :]).then_inc(q_rooted, 1)

            def exponentials(h):
                act.wait_ge(valued, h + 1)
                if h:
                    act.wait_ge(weighed, h * TT)
                act.activation(v[:, :, :].rearrange("p t d -> p (t d)"), psV[:, :], ACT.Copy).then_inc(v_copied, 1)
                for q in range(TT):
                    w = (q + 1) * P
                    act.wait_ge(shifted, h * TT + (q + 1))
                    act.activation(probs[:, q, 0:w], bank[q][:, 0:w], ACT.Exp, bias=shift[:, q:q + 1], scale=SCALE,
                                   accum_out=total[:, q:q + 1]).then_inc(exped, 1)

            def copies_(h):
                for q in range(TT):
                    w = (q + 1) * P
                    act.wait_ge(turned_p, h * TT + (q + 1))
                    if q >= 2:
                        act.wait_ge(weighed, h * TT + (q - 1))
                    act.activation(probsT[:, q % 2, 0:q + 1, :].rearrange("p k q -> p (k q)"), psT[q % 2][:, 0:w], ACT.Copy).then_inc(copied_p, 1)

            squares(0)
            roots(0)
            for h in range(H):
                exponentials(h)
                if h + 1 < H:
                    squares(h + 1)
                    roots(h + 1)
                copies_(h)

        @block.vector
        def _(dve):
            dve.wait_ge(gains_in, 64)

            then = Chain(dve, chain)

            def rope(h):
                b = h % 2
                dve.wait_ge(head_in[b], 64 * (h // 2 + 1))
                dve.wait_ge(swapped, h + 1)
                for s in range(2):
                    dve.tensor_tensor(turned[:, s * HALF:(s + 1) * HALF], bank[s][0:ROPE, 0:HALF], M["sin"][:, s * HALF:(s + 1) * HALF], ALU.mult)
                then(dve.tensor_tensor(q_r[:, b, :], q_r[:, b, :], M["cos"][:, :], ALU.mult))
                then(dve.tensor_tensor(q_r[:, b, :], q_r[:, b, :], turned[:, :], ALU.add))
                dve.sem_inc(r_roped, 1)

            def normalise(h):
                b = h % 2
                dve.wait_ge(k_rooted, h + 1)
                then(dve.reciprocal(root_k[:, :], root_k[:, :]))
                dve.scalar_tensor_tensor(k_n[:, :], bank[2][:, :], gk_n[:, :], root_k[:, :], ALU.mult, ALU.mult)
                dve.scalar_tensor_tensor(k_r[:, :], M["kpeT"][:, 0:TP], gk_r[:, :], root_k[0:ROPE, :], ALU.mult, ALU.mult)
                dve.wait_ge(q_rooted, h * 2 + 2)
                then(dve.reciprocal(root_q[:, :], root_q[:, :]))
                dve.scalar_tensor_tensor(q_n[:, b, :], q_n[:, b, :], gq_n[:, :], root_q[:, :], ALU.mult, ALU.mult)
                then(dve.scalar_tensor_tensor(q_r[:, b, :], q_r[:, b, :], gq_r[:, :], root_q[0:ROPE, :], ALU.mult, ALU.mult))
                dve.sem_inc(prepared, 1)
                dve.tensor_copy(M["qs_n"][:, h * TS:(h + 1) * TS], q_n[:, b, TP:T])
                dve.tensor_copy(M["qs_r"][:, h * TS:(h + 1) * TS], q_r[:, b, TP:T])

            def maxima(h):
                for q in range(TT):
                    w = (q + 1) * P
                    dve.wait_ge(scored, h * TT + (q + 1))
                    then(dve.tensor_tensor(bank[q][:, w - P:w], bank[q][:, w - P:w], K["bias"][:, :], ALU.add))
                    then(dve.tensor_reduce(top[:, q:q + 1], bank[q][:, 0:w], X, ALU.max))
                    dve.tensor_scalar(shift[:, q:q + 1], top[:, q:q + 1], -SCALE, None, ALU.mult).then_inc(shifted, 1)
                dve.wait_ge(exped, h * TT + TT)
                then(dve.reciprocal(share[:, :], total[:, :]))
                for q in range(TT):
                    w = (q + 1) * P
                    dve.tensor_scalar(probs[:, q, 0:w], probs[:, q, 0:w], share[:, q:q + 1], None, ALU.mult).then_inc(shared, 1)

            def keep(h):
                dve.wait_ge(weighed, h * TT + TT)
                then(dve.tensor_copy(oT[:, h * T:h * T + TP], psO[:, :]))
                dve.sem_inc(head_done[h % 2], 1)

            rope(0)
            normalise(0)
            for h in range(H):
                maxima(h)
                if h + 1 < H:
                    rope(h + 1)
                    normalise(h + 1)
                keep(h)


XB, XC_ = KI, KI + G
NR = TS * (CW - 1)
LAST = CW - 1 + TS


def convolution(nc, A, K, S, h_hi, h_lo, proj, outs):
    with ExitStack() as ctx:
        m = Mem(nc, ctx, "cnv")
        NB = 3
        NP = NR + CW + 1
        w, w_hi, w_lo = m.sb("w", [P, 2, KD, P]), m.sb("w_hi", [P, 4, KD, P], F32R), m.sb("w_lo", [P, 4, KD, P], F32R)
        held = m.sb("held", [NP, CD])
        params = m.sb("params", [P, KC, NP])
        raw, y = m.sb("raw", [P, NB, CW - 1 + T]), m.sb("y", [P, NB, T])
        rows_out = m.sb("rows_out", [LAST, 2, 512])
        ps, psP, psR = m.ps("ps", [P, 2, 2, 512]), m.ps("psP", [P, 2, 512]), m.ps("psR", [LAST, 2, 512])
        w_in = [m.sem(f"w_in{b}") for b in range(2)]
        rounded, lowered, multiplied, drained = (m.sem(n) for n in ("rounded", "lowered", "multiplied", "drained"))
        held_in, padded, turned, placed = m.sem("held_in"), m.sem("padded"), m.sem("turned"), m.sem("placed")
        began, summed, done, chain = m.sem("began"), m.sem("summed"), m.sem("done"), m.sem("chain")
        rows_stored = [m.sem(f"rows_stored{b}") for b in range(2)]
        rows_turned, rows_copied, stored = m.sem("rows_turned"), m.sem("rows_copied"), m.sem("stored")
        block = ctx.enter_context(nc.Block())
        PC = KC // 2
        w_view = A["w_in"].rearrange("l (k p) n -> p (l k) n", p=P)
        AT_KPE, AT_XBC, AT_DT = H * DQK + LAT, IN - 2 * D - SH - CD, IN - 2 * D - SH
        columns = chunks_from(AT_XBC, KC) + [AT_DT, AT_KPE]

        @block.sync
        def _(sp):
            weights_in(sp, w, w_view, w_in, lowered, columns, 0, 2)
            sp.dma_start(held[0:NR, :], A["state_conv"].rearrange("l b w c -> (l b w) c")).then_inc(held_in, 16)
            sp.dma_start(held[NR:NR + CW, :], A["conv_w"].rearrange("l w c -> (l w) c")).then_inc(held_in, 16)
            sp.dma_start(held[NR + CW:NP, :], A["conv_b"]).then_inc(held_in, 16)
            weights_in(sp, w, w_view, w_in, lowered, columns, 2, KC + 2)
            sp.dma_start(outs["conv_s"][0, :, 0:CW - 2, :], A["state_conv"][0, :, 1:CW - 1, :]).then_inc(stored, 16)
            sp.wait_ge(drained, KC + 2)
            sp.dma_start(proj[C_KPE], y[:, 0, :]).then_inc(stored, 16)
            sp.wait_ge(stored, 32)

        @block.gpsimd
        def _(pool):
            pool.memset(raw[:, :, 0:CW - 1], 0.0).then_inc(padded, 1)
            for c in range(KC + 2):
                round_weights(pool, w, w_hi, w_in, multiplied, rounded, c)

        @block.tensor
        def _(pe):
            pe.wait_ge(held_in, 48)
            for c in range(KC):
                last = pe.transpose(psP[:, c // PC, (c % PC) * NP:(c % PC) * NP + NP], held[:, c * P:(c + 1) * P], K["ident"][0:NP, 0:NP])
            last.then_inc(turned, 1)

            def turn_rows(c):
                pe.wait_ge(drained, c + 1)
                if c >= 8:
                    pe.wait_ge(rows_copied, c // 4 - 1)
                pe.transpose(psR[:, c // 4 % 2, (c % 4) * P:(c % 4 + 1) * P], raw[:, c % NB, TP:], K["ident"][:, :]).then_inc(rows_turned, 1)

            for c in range(KC + 2):
                pe.wait_ge(lowered, c + 1)
                if c >= 2:
                    pe.wait_ge(drained, c - 1)
                chunk_product(pe, ps[:, c % 2], c, w_hi, w_lo, h_hi, h_lo).then_inc(multiplied, 1)
                if 1 <= c <= KC:
                    turn_rows(c - 1)

        @block.scalar
        def _(act):
            act.wait_ge(placed, 1)
            act.wait_ge(padded, 1)
            b0 = NR + CW
            for c in range(KC + 1):
                if c < KC:
                    s = c % NB
                    act.wait_ge(multiplied, c + 1)
                    if c >= NB:
                        act.wait_ge(summed, c - NB + 1)
                        act.wait_ge(rows_turned, c - NB + 1)
                        act.wait_ge(done, c - NB + 1)
                    act.activation(raw[:, s, CW - 1:].rearrange("p (s t) -> p s t", s=2), ps[:, c % 2, :, 0:HALF], ACT.Copy).then_inc(drained, 1)
                    act.wait_ge(drained, c + 1)
                    act.activation(y[:, s, 0:TP], raw[:, s, 0:TP], ACT.Identity, scale=params[:, c, NR:NR + 1],
                                   bias=params[:, c, b0:b0 + 1])
                    act.activation(y[:, s, TP:], params[:, c, 0:NR:CW - 1], ACT.Identity, scale=params[:, c, NR:NR + 1],
                                   bias=params[:, c, b0:b0 + 1]).then_inc(began, 1)
                if c:
                    act.wait_ge(summed, c)
                    act.activation(S["x"][:, c - 1, :], y[:, (c - 1) % NB, :], ACT.Silu).then_inc(done, 1)
                if c and c % 4 == 0:
                    g = c // 4 - 1
                    cols = slice(g * 512, (g + 1) * 512)
                    act.wait_ge(rows_copied, g + 1)
                    act.dma_start(outs["conv_p"][0, 0, :, cols], rows_out[0:CW - 1, g % 2, :]).then_inc(rows_stored[g % 2], 16)
                    act.dma_start(outs["conv_s"][0, :, CW - 2, cols], rows_out[CW - 1:LAST, g % 2, :]).then_inc(rows_stored[g % 2], 16)
            act.wait_ge(done, KC)
            act.wait_ge(multiplied, KC + 1)
            act.activation(S["dt_raw"][:, :].rearrange("p (s t) -> p s t", s=2), ps[0:SH, KC % 2, :, 0:HALF], ACT.Copy).then_inc(drained, 1)
            act.wait_ge(multiplied, KC + 2)
            act.activation(y[:, 0, :].rearrange("p (s t) -> p s t", s=2), ps[:, (KC + 1) % 2, :, 0:HALF], ACT.Copy).then_inc(drained, 1)
            for b in range(2):
                act.wait_ge(rows_stored[b], 32 * (KC // 8))

        @block.vector
        def _(dve):
            then = Chain(dve, chain)
            AHEAD = 3

            def lower_chunk(n):
                lower(dve, w_hi[:, n % 4], w_lo[:, n % 4], w[:, n % 2], rounded, lowered, n + 1)

            for n in range(AHEAD):
                lower_chunk(n)
            dve.wait_ge(turned, 1)
            dve.tensor_copy(params[:, :, :].rearrange("p (h c) n -> p h (c n)", h=2), psP[:, :, 0:PC * NP]).then_inc(placed, 1)
            dve.wait_ge(placed, 1)
            dve.wait_ge(padded, 1)
            for c in range(KC):
                if c + AHEAD < KC + 2:
                    lower_chunk(c + AHEAD)
                s = c % NB
                dve.wait_ge(began, c + 1)
                for t in range(1, CW):
                    tap = params[:, c, NR + t:NR + t + 1]
                    dve.scalar_tensor_tensor(y[:, s, 0:TP], raw[:, s, t:t + TP], tap, y[:, s, 0:TP], ALU.mult, ALU.add)
                    held_t = params[:, c, t:NR:CW - 1] if t < CW - 1 else raw[:, s, CW - 1 + TP:]
                    last = dve.scalar_tensor_tensor(y[:, s, TP:], held_t, tap, y[:, s, TP:], ALU.mult, ALU.add)
                    if t < CW - 1:
                        then(last)
                last.then_inc(summed, 1)
                if c % 4 == 3:
                    g = c // 4
                    dve.wait_ge(rows_turned, c + 1)
                    if g >= 2:
                        dve.wait_ge(rows_stored[g % 2], 32 * (g // 2))
                    dve.tensor_copy(rows_out[:, g % 2, :], psR[:, g % 2, :]).then_inc(rows_copied, 1)


def prompt_scan(nc, A, K, S, h_hi, h_lo, proj, acs_dram, outs):
    HP = SH // G
    GATES = 2 * D // P
    EACH = GATES // TT
    with ExitStack() as ctx:
        m = Mem(nc, ctx, "scn")
        w, w_hi, w_lo = m.sb("w", [P, 2, KD, P]), m.sb("w_hi", [P, 4, KD, P], F32R), m.sb("w_lo", [P, 4, KD, P], F32R)
        out = m.sb("out", [P, 2, T])
        ps = m.ps("ps", [P, 2, 2, 512])
        w_in = [m.sem(f"w_in{b}") for b in range(2)]
        out_stored = [m.sem(f"out_stored{b}") for b in range(2)]
        rounded, lowered, multiplied, drained = (m.sem(n) for n in ("rounded", "lowered", "multiplied", "drained"))
        w_view = A["w_in"].rearrange("l (k p) n -> p (l k) n", p=P)
        seg, ce = m.sb("seg", [P, SH, P]), m.sb("ce", [P, SH, P])
        x_tok, b_tok, xw = m.sb("x_tok", [P, DI]), m.sb("b_tok", [P, G * N]), m.sb("xw", [P, DI])
        cb = m.sb("cb", [P, G, P])
        state = m.sb("state", [P, DI])
        state_out = xw[:, 0:1024].rearrange("p (b n) -> p b n", b=2)
        to_end, end = m.sb("to_end", [P, SH]), m.sb("end", [P, SH])
        bank = [m.ps(f"bank{b}", [P, 512]) for b in range(4)]
        read_in, turned, copied, cb_made = m.sem("read_in"), m.sem("turned"), m.sem("copied"), m.sem("cb_made")
        cb_masked, seg_made, decayed, exped, weighted = (m.sem(n) for n in ("cb_masked", "seg_made", "decayed", "exped", "weighted"))
        ce_made, x_weighted, summed, y_done, grown, state_done = (m.sem(n) for n in ("ce_made", "x_weighted", "summed", "y_done", "grown", "state_done"))
        end_exped, end_in, chain = m.sem("end_exped"), m.sem("end_in"), m.sem("chain")
        out_turned, out_copied = m.sem("out_turned"), m.sem("out_copied")
        stored = [m.sem(f"stored{b}") for b in range(2)]
        block = ctx.enter_context(nc.Block())
        acs_all = acs_dram.rearrange("(a h) t -> a h t", a=1)
        heads_of = lambda ap, g: ap[:, g * HP:(g + 1) * HP, :]

        TOKENS, CB, Y, GROWTH, USES = 0, 5, 6, 10, 14

        def bank_of(c, use):
            return bank[(c * USES + use) % 4]

        def was_read(c, use):
            if use < CB:
                return copied, 5 * c + use + 1
            if use < Y:
                return cb_masked, c + 1
            if use < GROWTH:
                return y_done, 4 * c + use - Y + 1
            return state_done, 4 * c + use - GROWTH + 1

        def bank_free(pe, c, use):
            before = c * USES + use - 4
            if before >= 0:
                pe.wait_ge(*was_read(before // USES, before % USES))

        @block.sync
        def _(sp):
            columns = chunks_from(IN - 2 * D, GATES)
            weights_in(sp, w, w_view, w_in, lowered, columns, 0, 2)
            sp.dma_start(ce[:, :, :], acs_all[:, :, 0:P].to_broadcast([P, SH, P])).then_inc(read_in, 16)
            weights_in(sp, w, w_view, w_in, lowered, columns, 2, GATES)
            for q in range(4):
                sp.wait_ge(out_copied, q + 1)
                sp.dma_start(outs["ssm_p"][0, 0].rearrange("(k a) p n -> (a p) k n", a=2)[:, 4 * q:4 * q + 4, :],
                             state_out[:, q % 2, :].rearrange("p (k n) -> p k n", k=4)).then_inc(stored[q % 2], 16)
            sp.wait_ge(stored[0], 32)
            sp.wait_ge(stored[1], 32)

        @block.gpsimd
        def _(pool):
            for n in range(GATES):
                round_weights(pool, w, w_hi, w_in, multiplied, rounded, n)

        @block.tensor
        def _(pe):
            def gates(n):
                pe.wait_ge(lowered, n + 1)
                if n >= 2:
                    pe.wait_ge(drained, n - 1)
                chunk_product(pe, ps[:, n % 2], n, w_hi, w_lo, h_hi, h_lo).then_inc(multiplied, 1)

            for c in range(TT):
                at = slice(c * P, (c + 1) * P)
                for q in range(5):
                    bank_free(pe, c, TOKENS + q)
                    if q < 4 and c:
                        pe.wait_ge(y_done, 4 * c)
                    for k in range(4):
                        last = pe.transpose(bank_of(c, TOKENS + q)[:, k * P:(k + 1) * P], S["x"][:, 4 * q + k, at], K["ident"][:, :])
                    last.then_inc(turned, 1)
                bank_free(pe, c, CB)
                for g in range(G):
                    last = pe.matmul(bank_of(c, CB)[:, g * P:(g + 1) * P], S["x"][:, XB + g, at], S["x"][:, XC_ + g, at], start=True, stop=True)
                last.then_inc(cb_made, 1)
                gates(EACH * c)
                gates(EACH * c + 1)
                pe.wait_ge(copied, 5 * c + 5)
                for q in range(4):
                    pe.wait_ge(weighted, 4 * c + q + 1)
                    bank_free(pe, c, Y + q)
                    if c:
                        pe.wait_ge(ce_made, 4 * c + q + 1)
                        pe.wait_ge(state_done, 4 * c)
                    for h in range(8 * q, 8 * q + 8):
                        to = bank_of(c, Y + q)[HD * (h % 2):HD * (h % 2) + HD, (h // 2 % 4) * P:(h // 2 % 4 + 1) * P]
                        last = pe.matmul(to, x_tok[:, h * HD:(h + 1) * HD], seg[:, h, :], start=True, stop=(c == 0))
                        if c:
                            last = pe.matmul(to, state[:, h * HD:(h + 1) * HD], ce[:, h, :], start=False, stop=True)
                    last.then_inc(summed, 1)
                gates(EACH * c + 2)
                pe.wait_ge(x_weighted, c + 1)
                for g in range(G):
                    bank_free(pe, c, GROWTH + g)
                    pe.matmul(bank_of(c, GROWTH + g)[:, :], b_tok[:, g * N:(g + 1) * N], xw[:, g * 512:(g + 1) * 512], start=True, stop=True).then_inc(grown, 1)
                gates(EACH * c + 3)
            for q in range(4):
                bank_free(pe, TT, q)
                pe.wait_ge(state_done, 4 * TT)
                if q >= 2:
                    pe.wait_ge(out_copied, q - 1)
                for k in range(4):
                    last = pe.transpose(bank_of(TT, q)[:, k * P:(k + 1) * P], state[:, (4 * q + k) * P:(4 * q + k + 1) * P], K["ident"][:, :])
                last.then_inc(out_turned, 1)

        @block.scalar
        def _(act):
            def drain(n):
                act.wait_ge(multiplied, n + 1)
                if n >= 2:
                    act.wait_ge(out_stored[n % 2], 16 * (n // 2))
                act.activation(out[:, n % 2].rearrange("p (s t) -> p s t", s=2), ps[:, n % 2, :, 0:HALF], ACT.Copy).then_inc(drained, 1)
                act.wait_ge(drained, n + 1)
                act.dma_start(proj[C_GA + n], out[:, n % 2]).then_inc(out_stored[n % 2], 16)

            for c in range(TT):
                for q in range(5):
                    act.wait_ge(turned, 5 * c + q + 1)
                    if c and q == 0:
                        act.wait_ge(summed, 4 * c)
                        act.wait_ge(x_weighted, c)
                        act.wait_ge(grown, 4 * c)
                    act.activation(x_tok[:, q * 512:(q + 1) * 512] if q < 4 else b_tok[:, :], bank_of(c, TOKENS + q)[:, :], ACT.Copy).then_inc(copied, 1)
                act.wait_ge(seg_made, c + 1)
                act.activation(seg[:, :, :], seg[:, :, :], ACT.Exp).then_inc(decayed, 1)
                act.wait_ge(end_in, c + 1)
                act.activation(to_end[:, :], to_end[:, :], ACT.Exp).then_inc(end_exped, 1)
                act.activation(end[:, :], ce[:, :, P - 1], ACT.Exp).then_inc(end_exped, 1)
                act.wait_ge(end_exped, 2 * c + 2)
                act.activation(ce[:, :, :], ce[:, :, :], ACT.Exp).then_inc(exped, 1)
                drain(EACH * c)
                drain(EACH * c + 1)
                if c + 1 < TT:
                    act.wait_ge(summed, 4 * c + 4)
                    act.dma_start(ce[:, :, :], acs_all[:, :, (c + 1) * P:(c + 2) * P].to_broadcast([P, SH, P])).then_inc(read_in, 16)
                drain(EACH * c + 2)
                drain(EACH * c + 3)
            for b in range(2):
                act.wait_ge(out_stored[b], 16 * (GATES // 2))

        @block.vector
        def _(dve):
            then = Chain(dve, chain)

            def lower_to(n_end):
                while lower_to.n < min(n_end, GATES):
                    n = lower_to.n
                    lower(dve, w_hi[:, n % 4], w_lo[:, n % 4], w[:, n % 2], rounded, lowered, n + 1)
                    lower_to.n += 1
            lower_to.n = 0

            lower_to(2)
            for c in range(TT):
                at = slice(c * P, (c + 1) * P)
                dve.wait_ge(read_in, 16 * c + 16)
                for h in range(SH):
                    last = dve.tensor_scalar(seg[:, h, :], ce[:, h, :], S["acs_tok"][:, c, h:h + 1], 0.0, ALU.subtract, ALU.min)
                last.then_inc(seg_made, 1)
                dve.tensor_tensor(to_end[:, :], ce[:, :, P - 1], S["acs_tok"][:, c, :], ALU.subtract).then_inc(end_in, 1)
                lower_to(EACH * c + 3)
                dve.wait_ge(cb_made, c + 1)
                if c:
                    dve.wait_ge(weighted, 4 * c)
                dve.tensor_tensor(cb[:, :, :], bank_of(c, CB)[:, :].rearrange("p (g i) -> p g i", g=G),
                                  K["keep"][:, :].rearrange("p (a i) -> p a i", a=1).to_broadcast([P, G, P]), ALU.mult).then_inc(cb_masked, 1)
                dve.wait_ge(cb_masked, c + 1)
                dve.wait_ge(decayed, c + 1)
                for q in range(4):
                    for h in range(8 * q, 8 * q + 8):
                        last = dve.scalar_tensor_tensor(seg[:, h, :], seg[:, h, :], S["dt_tok"][:, c, h:h + 1], cb[:, h // HP, :], ALU.mult, ALU.mult)
                    last.then_inc(weighted, 1)
                    if q == 2:
                        lower_to(EACH * c + 4)
                if c:
                    dve.wait_ge(exped, c + 1)
                    for g in range(G):
                        dve.tensor_tensor(heads_of(ce, g), heads_of(ce, g),
                                          S["x"][:, XC_ + g:XC_ + g + 1, at].to_broadcast([P, HP, P]), ALU.mult).then_inc(ce_made, 1)
                else:
                    dve.sem_inc(ce_made, G)
                dve.wait_ge(end_exped, 2 * c + 2)
                then(dve.tensor_tensor(to_end[:, :], to_end[:, :], S["dt_tok"][:, c, :], ALU.mult))
                dve.wait_ge(copied, 5 * c + 4)
                dve.tensor_tensor(xw[:, :].rearrange("p (h d) -> p h d", h=SH), x_tok[:, :].rearrange("p (h d) -> p h d", h=SH),
                                  to_end[:, :].rearrange("p (h a) -> p h a", a=1).to_broadcast([P, SH, HD]), ALU.mult).then_inc(x_weighted, 1)
                for q in range(4):
                    dve.wait_ge(summed, 4 * c + q + 1)
                    for k in range(4 * q, 4 * q + 4):
                        last = dve.scalar_tensor_tensor(S["x"][:, k, at], S["x"][:, k, at], S["skip"][:, k:k + 1],
                                                        bank_of(c, Y + q)[:, (k % 4) * P:(k % 4 + 1) * P], ALU.mult, ALU.add)
                    last.then_inc(y_done, 1)
                lower_to(EACH * c + 5)
                view = lambda ap: ap.rearrange("p (h d) -> p h d", d=HD)
                if c:
                    then(dve.tensor_tensor(view(state[:, :]), view(state[:, :]),
                                           end[:, :].rearrange("p (h a) -> p h a", a=1).to_broadcast([P, SH, HD]), ALU.mult))
                for g in range(G):
                    dve.wait_ge(grown, 4 * c + g + 1)
                    part, new = state[:, g * 512:(g + 1) * 512], bank_of(c, GROWTH + g)[:, :]
                    (dve.tensor_tensor(part, part, new, ALU.add) if c else dve.tensor_copy(part, new)).then_inc(state_done, 1)
                lower_to(EACH * c + 6)
            for q in range(4):
                dve.wait_ge(out_turned, q + 1)
                if q >= 2:
                    dve.wait_ge(stored[q % 2], 16)
                dve.tensor_copy(state_out[:, q % 2, :], bank_of(TT, q)[:, :]).then_inc(out_copied, 1)


def sample_scan(nc, A, K, S, h_hi, h_lo, proj, acs_dram, outs):
    ORDER = 9
    with ExitStack() as ctx:
        m = Mem(nc, ctx, "stp")
        w, w_hi, w_lo = m.sb("w", [P, 2, KD, P]), m.sb("w_hi", [P, 4, KD, P], F32R), m.sb("w_lo", [P, 4, KD, P], F32R)
        out = m.sb("out", [P, 2, T])
        ps = m.ps("ps", [P, 2, 2, 512])
        w_in = [m.sem(f"w_in{b}") for b in range(2)]
        out_stored = [m.sem(f"out_stored{b}") for b in range(2)]
        rounded, lowered, multiplied, drained = (m.sem(n) for n in ("rounded", "lowered", "multiplied", "drained"))
        w_view = A["w_in"].rearrange("l (k p) n -> p (l k) n", p=P)
        CHUNKS = list(range(C_Q, C_KPE)) + list(range(C_Z, C_XBC))
        columns = chunks_from(0, C_KPE) + chunks_from(H * DQK + LAT + ROPE, KI)
        bias, a_log = m.sb("bias", [SH, 1]), m.sb("a_log", [SH, 1])
        psT = m.ps("psT", [P, 2, TT, SH])
        loaded, biased, magnitude, exped, a_made, ready = (m.sem(n) for n in ("loaded", "biased", "magnitude", "exped", "a_made", "ready"))
        turned, acs_stored, chain = m.sem("turned"), m.sem("acs_stored"), m.sem("chain")
        NB = 2
        st, tmp = m.sb("st", [P, NB, KI, N]), m.sb("tmp", [P, KI, N])
        NR_ = 2 * TS + 1
        rates_in, rates, dtx = m.sb("rates_in", [SH, NR_]), m.sb("rates", [P, KI, NR_]), m.sb("dtx", [P, KI, TS])
        y = m.sb("y", [P, KI, TS])
        psS, psB = m.ps("psS", [P, KI, NR_]), m.ps("psB", [P, 2, 512])
        wide = m.sb("wide", [P, 2 * G, P])
        x = S["dt_raw"]
        s, s2, p_ = (tmp[0:SH].rearrange("p k n -> p (k n)")[:, j * T:(j + 1) * T] for j in range(3))
        e = wide[0:SH].rearrange("p g n -> p (g n)")[:, 0:T]
        st_in = [m.sem(f"st_in{b}") for b in range(NB)]
        stored = [m.sem(f"stored{b}") for b in range(NB)]
        set_, spread, widened, bc_made, decayed, updated, summed, dtx_made = (m.sem(n) for n in (
            "set", "spread", "widened", "bc_made", "decayed", "updated", "summed", "dtx_made"))
        block = ctx.enter_context(nc.Block())
        view_in = A["state_ssm"][0].rearrange("b (k a) p n -> b (a p) k n", a=2)
        view_out = outs["ssm_s"][0].rearrange("b (k a) p n -> b (a p) k n", a=2)
        TURN, SPREAD = 5, 6
        sequence_at = {8 + 3 * b: b for b in range(TS)}

        @block.sync
        def _(sp):
            weights_in(sp, w, w_view, w_in, lowered, columns, 0, 2)
            sp.dma_start(bias[:, :], A["dt_bias"].rearrange("l h -> h l")).then_inc(loaded, 16)
            sp.dma_start(a_log[:, :], A["a_log"].rearrange("l h -> h l")).then_inc(loaded, 16)
            sp.dma_start(rates_in[:, 2 * TS:], A["d_skip"].rearrange("l h -> h l")).then_inc(loaded, 16)
            weights_in(sp, w, w_view, w_in, lowered, columns, 2, len(CHUNKS))

        @block.scalar
        def _(act):
            act.wait_ge(loaded, 48)
            act.activation(S["a"][:, :], a_log[:, :], ACT.Exp).then_inc(a_made, 1)
            act.wait_ge(biased, 1)
            act.activation(e[:, :], x[:, :], ACT.Abs).then_inc(magnitude, 1)
            act.wait_ge(magnitude, 1)
            act.activation(e[:, :], e[:, :], ACT.Exp, scale=-1.0).then_inc(exped, 1)
            for c, chunk in enumerate(CHUNKS):
                act.wait_ge(multiplied, c + 1)
                if c >= 2:
                    act.wait_ge(out_stored[c % 2], 16 * (c // 2))
                act.activation(out[:, c % 2].rearrange("p (s t) -> p s t", s=2), ps[:, c % 2, :, 0:HALF], ACT.Copy).then_inc(drained, 1)
                act.wait_ge(drained, c + 1)
                act.dma_start(proj[chunk], out[:, c % 2]).then_inc(out_stored[c % 2], 16)
                if c == TURN - 1:
                    act.wait_ge(ready, 1)
                    act.activation(S["decay_s"][:, :], S["acs"][:, TP:], ACT.Exp).then_inc(exped, 1)
            for b in range(2):
                act.wait_ge(out_stored[b], 16 * (len(CHUNKS) // 2))

        @block.gpsimd
        def _(pool):
            for c in range(len(CHUNKS)):
                round_weights(pool, w, w_hi, w_in, multiplied, rounded, c)
                if c + 1 in sequence_at:
                    b = sequence_at[c + 1]
                    if b >= NB:
                        pool.wait_ge(updated, b - NB + 1)
                        pool.dma_start(view_out[b - NB], st[:, b % NB]).then_inc(stored[b % NB], 16)
                        pool.wait_ge(stored[b % NB], 16 * (b // NB))
                        pool.wait_ge(summed, b - NB + 1)
                    pool.dma_start(st[:, b % NB], view_in[b]).then_inc(st_in[b % NB], 16)
            for b in range(TS - NB, TS):
                pool.wait_ge(updated, b + 1)
                pool.dma_start(view_out[b], st[:, b % NB]).then_inc(stored[b % NB], 16)
            pool.wait_ge(ready, 1)
            pool.dma_start(acs_dram, S["acs"][:, 0:TP]).then_inc(acs_stored, 16)
            pool.wait_ge(acs_stored, 16)
            for b in range(NB):
                pool.wait_ge(stored[b], 16 * (TS // NB))

        @block.tensor
        def _(pe):
            for c in range(len(CHUNKS)):
                pe.wait_ge(lowered, c + 1)
                if c >= 2:
                    pe.wait_ge(drained, c - 1)
                chunk_product(pe, ps[:, c % 2], c, w_hi, w_lo, h_hi, h_lo).then_inc(multiplied, 1)
                if c == TURN:
                    pe.wait_ge(ready, 1)
                    for t in range(TT):
                        pe.transpose(psT[:, 0, t, :], S["dt"][:, t * P:(t + 1) * P], K["ident"][0:SH, 0:SH])
                        last = pe.transpose(psT[:, 1, t, :], S["acs"][:, t * P:(t + 1) * P], K["ident"][0:SH, 0:SH])
                    last.then_inc(turned, 1)
                if c == SPREAD:
                    pe.wait_ge(set_, 2)
                    for k in range(KI):
                        last = pe.matmul(psS[:, k, :], K["spread"][:, k * P:(k + 1) * P], rates_in[:, :], start=True, stop=True)
                    last.then_inc(spread, 1)
                if c in sequence_at:
                    b = sequence_at[c]
                    pe.wait_ge(widened, b + 1)
                    if b:
                        pe.wait_ge(summed, b)
                    for j in range(2):
                        for g in range(G):
                            last = pe.matmul(psB[:, j, g * P:(g + 1) * P], wide[:, G * j + g, :], K["ident"][:, :], start=True, stop=True)
                    last.then_inc(bc_made, 1)

        @block.vector
        def _(dve):
            then = Chain(dve, chain)

            def lower_to(end):
                while lower_to.c < min(end, len(CHUNKS)):
                    c = lower_to.c
                    lower(dve, w_hi[:, c % 4], w_lo[:, c % 4], w[:, c % 2], rounded, lowered, c + 1)
                    lower_to.c += 1
            lower_to.c = 0

            lower_to(2)
            dve.wait_ge(loaded, 48)
            dve.tensor_scalar(x[:, :], S["dt_raw"][:, :], bias[:, :], None, ALU.add).then_inc(biased, 1)
            dve.wait_ge(exped, 1)
            then(dve.tensor_scalar(s[:, :], e[:, :], 2.0, None, ALU.add))
            then(dve.reciprocal(s[:, :], s[:, :]))
            lower_to(4)
            then(dve.tensor_tensor(s[:, :], s[:, :], e[:, :], ALU.mult))
            then(dve.tensor_tensor(s2[:, :], s[:, :], s[:, :], ALU.mult))
            then(dve.tensor_scalar(p_[:, :], s2[:, :], 2.0 / (2 * ORDER + 1), None, ALU.mult))
            for k in range(ORDER - 1, 0, -1):
                then(dve.scalar_tensor_tensor(p_[:, :], p_[:, :], 2.0 / (2 * k + 1), s2[:, :], ALU.add, ALU.mult))
            lower_to(5)
            then(dve.scalar_tensor_tensor(p_[:, :], p_[:, :], 2.0, s[:, :], ALU.add, ALU.mult))
            then(dve.scalar_tensor_tensor(S["dt"][:, :], x[:, :], 0.0, p_[:, :], ALU.max, ALU.add))
            dve.wait_ge(a_made, 1)
            then(dve.tensor_scalar(S["a"][:, :], S["a"][:, :], -1.0, None, ALU.mult))
            then(dve.tensor_scalar(p_[:, :], S["dt"][:, :], S["a"][:, :], None, ALU.mult))
            for c in range(TT):
                dve.tensor_tensor_scan(S["acs"][:, c * P:(c + 1) * P], K["ones"][0:SH, :], p_[:, c * P:(c + 1) * P], 0.0, ALU.mult, ALU.add)
            dve.tensor_copy(S["acs"][:, TP:], p_[:, TP:]).then_inc(ready, 1)
            lower_to(6)
            dve.tensor_copy(rates_in[:, 0:TS], S["dt"][:, TP:]).then_inc(set_, 1)
            dve.wait_ge(exped, 2)
            dve.tensor_copy(rates_in[:, TS:2 * TS], S["decay_s"][:, :]).then_inc(set_, 1)
            lower_to(8)
            dve.wait_ge(turned, 1)
            dve.tensor_copy(S["dt_tok"][:, :, :], psT[:, 0, :, :])
            dve.tensor_copy(S["acs_tok"][:, :, :], psT[:, 1, :, :])
            dve.wait_ge(spread, 1)
            then(dve.tensor_copy(rates[:, :, :], psS[:, :, :]))
            dve.tensor_copy(S["skip"][:, :], rates[:, :, 2 * TS])
            then(dve.tensor_tensor(dtx[:, :, :], S["x"][:, 0:KI, TP:], rates[:, :, 0:TS], ALU.mult))
            for b in range(TS):
                at = {seq: c for c, seq in sequence_at.items()}[b]
                dve.tensor_copy(wide[:, :, :], S["x"][:, XB:XB + 2 * G, TP + b:TP + b + 1].to_broadcast([P, 2 * G, P])).then_inc(widened, 1)
                lower_to(at + 2)
                dve.wait_ge(st_in[b % NB], 16 * (b // NB + 1))
                then(dve.tensor_tensor(st[:, b % NB], st[:, b % NB], rates[:, :, TS + b:TS + b + 1].to_broadcast([P, KI, N]), ALU.mult))
                dve.wait_ge(bc_made, b + 1)
                for g in range(G):
                    ks = slice(4 * g, 4 * g + 4)
                    last = dve.tensor_tensor(tmp[:, ks, :], psB[:, 0, g * P:(g + 1) * P].rearrange("p (a n) -> p a n", a=1).to_broadcast([P, 4, N]),
                                             dtx[:, ks, b:b + 1].to_broadcast([P, 4, N]), ALU.mult)
                then(last)
                dve.tensor_tensor(st[:, b % NB], st[:, b % NB], tmp[:, :, :], ALU.add).then_inc(updated, 1)
                dve.wait_ge(updated, b + 1)
                lower_to(at + 4)
                for g in range(G):
                    ks = slice(4 * g, 4 * g + 4)
                    last = dve.tensor_tensor(tmp[:, ks, :], st[:, b % NB, ks, :],
                                             psB[:, 1, g * P:(g + 1) * P].rearrange("p (a n) -> p a n", a=1).to_broadcast([P, 4, N]), ALU.mult)
                last.then_inc(summed, 1)
                dve.wait_ge(summed, b + 1)
                then(dve.tensor_reduce(y[:, :, b:b + 1], tmp[:, :, :], X, ALU.add))
            lower_to(len(CHUNKS))
            then(dve.tensor_tensor(dtx[:, :, :], S["x"][:, 0:KI, TP:], S["skip"][:, :].rearrange("p (k a) -> p k a", a=1).to_broadcast([P, KI, TS]), ALU.mult))
            dve.tensor_tensor(S["x"][:, 0:KI, TP:], dtx[:, :, :], y[:, :, :], ALU.add)


def gated_norm(nc, A, K, S, proj):
    with ExitStack() as ctx:
        m = Mem(nc, ctx, "gtn")
        NB = 3
        z, sq = m.sb("z", [P, NB, T]), m.sb("sq", [P, NB, T])
        rstd = m.sb("rstd", [P, 2, HALF])
        ps = m.ps("ps", [P, 2, 512])
        z_in = [m.sem(f"z_in{b}") for b in range(NB)]
        gated, silued, squared, added, rooted, chain = (m.sem(n) for n in ("gated", "silued", "squared", "added", "rooted", "chain"))
        gain_in = m.sem("gain_in")
        block = ctx.enter_context(nc.Block())

        @block.sync
        def _(sp):
            sp.dma_start(S["g_ssm"][:, :], A["g_ssm"].rearrange("l (k p) -> p (l k)", p=P), allow_slow_non_contiguous=True).then_inc(gain_in, 16)
            for k in range(KI):
                if k >= NB:
                    sp.wait_ge(gated, k - NB + 1)
                sp.dma_start(z[:, k % NB, :], proj[C_Z + k]).then_inc(z_in[k % NB], 16)

        @block.scalar
        def _(act):
            for k in range(KI + 1):
                if k < KI:
                    act.wait_ge(z_in[k % NB], 16 * (k // NB + 1))
                    act.activation(z[:, k % NB, :], z[:, k % NB, :], ACT.Silu).then_inc(silued, 1)
                if k:
                    act.wait_ge(gated, k)
                    if k > NB:
                        act.wait_ge(added, k - NB)
                    act.activation(sq[:, (k - 1) % NB, :], S["x"][:, k - 1, :], ACT.Square).then_inc(squared, 1)
            act.wait_ge(added, KI)
            act.activation(rstd[:, :, :], ps[:, :, 0:HALF], ACT.Sqrt, scale=1.0 / DI, bias=K["eps"][:, :]).then_inc(rooted, 1)

        @block.tensor
        def _(pe):
            for k in range(KI):
                pe.wait_ge(squared, k + 1)
                for s in range(2):
                    last = pe.matmul(ps[:, s, 0:HALF], K["ones"][:, :], sq[:, k % NB, s * HALF:(s + 1) * HALF],
                                     start=(k == 0), stop=(k == KI - 1))
                last.then_inc(added, 1)

        @block.vector
        def _(dve):
            then = Chain(dve, chain)
            for k in range(KI):
                dve.wait_ge(silued, k + 1)
                dve.tensor_tensor(S["x"][:, k, :], S["x"][:, k, :], z[:, k % NB, :], ALU.mult).then_inc(gated, 1)
            dve.wait_ge(rooted, 1)
            then(dve.reciprocal(rstd[:, :, :], rstd[:, :, :]))
            dve.wait_ge(gain_in, 16)
            for k in range(KI):
                v = S["x"][:, k, :].rearrange("p (s t) -> p s t", s=2)
                last = dve.scalar_tensor_tensor(v, v, S["g_ssm"][:, k:k + 1], rstd[:, :, :], ALU.mult, ALU.mult)


WQ = 2 * P
BIG = -3.0e38


def merge(nc, A, K, proj, oT, yT, mT, parts, W, x1):
    with ExitStack() as ctx:
        m = Mem(nc, ctx, "mrg")
        wa, wb = m.sb("wa", [P, 2, H, P]), m.sb("wb", [P, 2, KI, P])
        gate, part = m.sb("gate", [P, 2, 2, T]), m.sb("part", [P, TP])
        psA, psB = m.ps("psA", [P, 2, 512]), m.ps("psB", [P, 2, 2, 512])
        w_in, gate_in, opened, summed, used = ([m.sem(f"{n}{b}") for b in range(2)]
                                               for n in ("w_in", "gate_in", "opened", "summed", "used"))
        chain = m.sem("chain")
        block = ctx.enter_context(nc.Block())

        def chunks(eng, body):
            with eng.Fori(0, KD // 2) as i:
                for b in range(2):
                    body(i, b, i * 2 + b)

        @block.sync
        def _(sp):
            def load(i, b, d):
                at = bass.ds(d * P, P)
                sp.wait_ge(summed[b], i)
                sp.dma_start(wa[:, b], A["w_br_a"].rearrange("l (k p) n -> p (l k) n", p=P)[:, :, at]).then_inc(w_in[b], 16)
                sp.dma_start(wb[:, b], A["w_br_b"].rearrange("l (k p) n -> p (l k) n", p=P)[:, :, at]).then_inc(w_in[b], 16)
                sp.wait_ge(used[b], i)
                for j, c in enumerate((C_GA, C_GB)):
                    sp.dma_start(gate[:, b, j, :], proj.rearrange("c p t -> p c t")[:, bass.ds(d + c, 1), :]).then_inc(gate_in[b], 16)
            chunks(sp, load)

        @block.tensor
        def _(pe):
            def product(i, b, d):
                pe.wait_ge(w_in[b], i * 32 + 32)
                pe.wait_ge(used[b], i)
                for k in range(H):
                    pe.matmul(psA[:, b, :], wa[:, b, k, :], oT[:, k, :], start=(k == 0), stop=(k == H - 1))
                for k in range(KI):
                    for s in range(2):
                        last = pe.matmul(psB[:, b, s, 0:HALF], wb[:, b, k, :], yT[:, k, s * HALF:(s + 1) * HALF], start=(k == 0), stop=(k == KI - 1))
                last.then_inc(summed[b], 1)
            chunks(pe, product)

        @block.scalar
        def _(act):
            def open_(i, b, d):
                act.wait_ge(gate_in[b], i * 32 + 32)
                act.activation(gate[:, b], gate[:, b], ACT.Sigmoid).then_inc(opened[b], 1)
            chunks(act, open_)
            act.dma_start(W["w_out"][:], A["w_out"].rearrange("l (k p) n -> p (l k) n", p=P)).then_inc(W["w_out_in"], 16)
            act.dma_start(x1[:], A["x_prompt"].rearrange("b (t p) d -> p (b t) d", p=P)).then_inc(W["x_in"], 16)

        @block.vector
        def _(dve):
            def sum_(i, b, d):
                then = Steps(dve, chain, 4, d)
                row = lambda tile: tile[:, bass.ds(d, 1), :].rearrange("p a t -> p (a t)")
                gate_b = gate[:, b, 1, :]
                dve.wait_ge(opened[b], i + 1)
                dve.wait_ge(summed[b], i + 1)
                then(dve.tensor_tensor(gate_b.rearrange("p (s t) -> p s t", s=2), psB[:, b, :, 0:HALF], gate_b.rearrange("p (s t) -> p s t", s=2), ALU.mult))
                then(dve.tensor_tensor(part[:, :], psA[:, b, :], gate[:, b, 0, 0:TP], ALU.mult))
                then(dve.tensor_tensor(row(mT), part[:, :], gate_b[:, 0:TP], ALU.add))
                dve.tensor_scalar(row(parts["b"]), gate_b[:, TP:], 1.0, None, ALU.mult)
                then(dve.tensor_scalar(row(parts["gate_a"]), gate[:, b, 0, TP:], 1.0, None, ALU.mult))
                dve.sem_inc(used[b], 1)
                then.full()
            chunks(dve, sum_)


def residual(nc, A, K, mT, W, x1):
    w = W["w_out"]
    with ExitStack() as ctx:
        m = Mem(nc, ctx, "res")
        gate = m.sb("gate", [P, D])
        ps, psG = m.ps("ps", [P, 2, 2, 512]), m.ps("psG", [P, 2, 512])
        spread, summed, used, chain = (m.sem(k) for k in ("spread", "summed", "used", "chain"))
        block = ctx.enter_context(nc.Block())

        @block.tensor
        def _(pe):
            for c in range(2):
                last = pe.matmul(psG[:, c, :], K["last"][:, :], K["ada"][:, 2 * D + c * 512:2 * D + (c + 1) * 512], start=True, stop=True)
            last.then_inc(spread, 1)
            pe.wait_ge(W["w_out_in"], 16)
            for t in range(TT):
                if t >= 2:
                    pe.wait_ge(used, t - 1)
                for c in range(2):
                    for k in range(KD):
                        last = pe.matmul(ps[:, t % 2, c, :], mT[:, k, t * P:(t + 1) * P], w[:, k, c * 512:(c + 1) * 512], start=(k == 0), stop=(k == KD - 1))
                last.then_inc(summed, 1)

        @block.vector
        def _(dve):
            then = Chain(dve, chain)
            dve.wait_ge(spread, 1)
            then(dve.tensor_copy(gate[:, :], psG[:, :, :].rearrange("p c n -> p (c n)")))
            dve.wait_ge(W["x_in"], 16)
            for t in range(TT):
                dve.wait_ge(summed, t + 1)
                flat = ps[:, t % 2].rearrange("p c n -> p (c n)")
                then(dve.tensor_tensor(flat, flat, gate[:, :], ALU.mult))
                dve.tensor_tensor(x1[:, t, :], x1[:, t, :], flat, ALU.add).then_inc(used, 1)


def search_buffers(m, NTI):
    return {"s": m.sb("s", [P, NTI, 2, NK]), "s2": m.sb("s2", [P, NTI, 2, NK]),
            "v": m.sb("v", [P, NTI, 2, TK]), "at": m.sb("at", [P, NTI, 2, TK], U32), "at_f": m.sb("at_f", [P, 2, NTI, TK]),
            "cand": m.sb("cand", [P, NTI, TK, TK]), "cand2": m.sb("cand2", [P, NTI, TK, TK]),
            "best": m.sb("best", [P, NTI, TK]), "j": m.sb("j", [P, NTI, TK], U32),
            "part": m.sb("part", [P, 2, NTI, TK], U32), "part_f": m.sb("part_f", [P, 2, NTI, TK]),
            "picked": m.sb("picked", [P, 2, NTI, TK]), "total": m.sb("total", [P, NTI]),
            "count_i": m.sb("count_i", [P, TK], I32), "count": m.sb("count", [P, TK])}


def search(dve, then, find, n, NTI, ids, gate, shifted, exped, h):
    s, s2, v, at, at_f, cand, cand2, best, j, part, part_f, picked, total, count = (find[k] for k in (
        "s", "s2", "v", "at", "at_f", "cand", "cand2", "best", "j", "part", "part_f", "picked", "total", "count"))
    bc = lambda ap, axis, shape: ap.unsqueeze(axis).to_broadcast(shape)

    def top(rows_):
        for src, _, vals, _ in rows_:
            last = dve.max(vals[:, 0:8], src)
        then(last)
        for src, src2, vals, places in rows_:
            dve.max_index(places[:, 0:8], vals[:, 0:8], src)
            last = dve.match_replace(src2, vals[:, 0:8], src, BIG)
        then(last)
        for _, src2, vals, _ in rows_:
            last = dve.max(vals[:, 8:16], src2)
        then(last)
        for _, src2, vals, places in rows_:
            last = dve.max_index(places[:, 8:16], vals[:, 8:16], src2)
        then(last)

    top([(s[0:n, t, side, :], s2[0:n, t, side, :], v[0:n, t, side, :], at[0:n, t, side, :])
         for t in range(NTI) for side in range(2)])
    shape = [n, NTI, TK, TK]
    for side in range(2):
        dve.tensor_copy(at_f[0:n, side], at[0:n, :, side, :])
    then(dve.tensor_tensor(cand[0:n], bc(v[0:n, :, 0, :], 3, shape), bc(v[0:n, :, 1, :], 2, shape), ALU.add))
    flat = lambda tile, t: tile[0:n, t].rearrange("p a b -> p (a b)")
    top([(flat(cand, t), flat(cand2, t), best[0:n, t, :], j[0:n, t, :]) for t in range(NTI)])
    dve.tensor_scalar(part[0:n, 0], j[0:n], 4, None, ALU.logical_shift_right)
    then(dve.tensor_scalar(part[0:n, 1], j[0:n], TK - 1, None, ALU.bitwise_and))
    then(dve.tensor_copy(part_f[0:n], part[0:n]))
    then(dve.tensor_copy(total[0:n, :], best[0:n, :, 0]))
    dve.tensor_tensor(best[0:n], best[0:n], bc(total[0:n, :], 2, [n, NTI, TK]), ALU.subtract).then_inc(shifted, 1)
    every = count[0:n, :].unsqueeze(1).unsqueeze(1).to_broadcast(shape)
    ones = (cand, cand2)
    for side in range(2):
        last = dve.tensor_tensor(ones[side][0:n], bc(part_f[0:n, side], 3, shape), every, ALU.is_equal)
    then(last)
    for side in range(2):
        last = dve.tensor_tensor(ones[side][0:n], ones[side][0:n], bc(at_f[0:n, side], 2, shape), ALU.mult)
    then(last)
    for side in range(2):
        last = dve.tensor_reduce(picked[0:n, side], ones[side][0:n], X, ALU.add)
    then(last)
    then(dve.scalar_tensor_tensor(ids, picked[0:n, 0], float(NK), picked[0:n, 1], ALU.mult, ALU.add))
    dve.wait_ge(exped, h + 1)
    then(dve.tensor_reduce(total[0:n, :], best[0:n], X, ALU.add))
    then(dve.reciprocal(total[0:n, :], total[0:n, :]))
    then(dve.tensor_tensor(gate, best[0:n], bc(total[0:n, :], 2, [n, NTI, TK]), ALU.mult))


def choose(nc, A, K, h2T, ids_out, gate_out):
    n, NTI, W = P, TT, TP
    with ExitStack() as ctx:
        m = Mem(nc, ctx, "chs")
        find = search_buffers(m, NTI)
        wq, keys, keysT = m.sb("wq", [P, KD, WQ]), m.sb("keys", [P, 2, P]), m.sb("keysT", [P, 2, P])
        qT = m.sb("qT", [P, 2, W])
        psK, psQ, psS = m.ps("psK", [P, 2, P]), m.ps("psQ", [P, 2, 512]), m.ps("psS", [P, NTI, 2, NK])
        (w_in, keys_in, turned, keys_copied, summed, q_copied, scored, s_copied, shifted, exped, chain, counted, count_made) = (
            m.sem(k) for k in ("w_in", "keys_in", "turned", "keys_copied", "summed", "q_copied", "scored", "s_copied",
                               "shifted", "exped", "chain", "counted", "count_made"))
        block = ctx.enter_context(nc.Block())

        @block.sync
        def _(sp):
            with sp.Fori(0, PH) as h:
                sp.wait_ge(summed, h)
                sp.dma_start(wq[:, :, :], A["peer_wq"].rearrange("l (k p) n -> p (l k) n", p=P)[:, :, bass.ds(h * WQ, WQ)]).then_inc(w_in, 16)
                sp.wait_ge(turned, h)
                for k, name in enumerate(("peer_keys1", "peer_keys2")):
                    sp.dma_start(keys[:, k, :], A[name].rearrange("l h n d -> n (l h) d")[:, bass.ds(h, 1), :]).then_inc(keys_in, 16)

        @block.gpsimd
        def _(pool):
            pool.iota(find["count_i"][:, :], pattern=[[1, TK]], base=0, channel_multiplier=0).then_inc(counted, 1)

        @block.tensor
        def _(pe):
            with pe.Fori(0, PH) as h:
                pe.wait_ge(keys_in, h * 32 + 32)
                pe.wait_ge(keys_copied, h)
                for k in range(2):
                    last = pe.transpose(psK[:, k, :], keys[:, k, :], K["ident"][:, :])
                last.then_inc(turned, 1)
                pe.wait_ge(w_in, h * 16 + 16)
                pe.wait_ge(q_copied, h)
                for side in range(2):
                    for k in range(KD):
                        last = pe.matmul(psQ[:, side, 0:W], wq[:, k, side * P:(side + 1) * P], h2T[:, k, :], start=(k == 0), stop=(k == KD - 1))
                last.then_inc(summed, 1)
                pe.wait_ge(keys_copied, h + 1)
                pe.wait_ge(q_copied, h + 1)
                pe.wait_ge(s_copied, h)
                for t in range(NTI):
                    for side in range(2):
                        last = pe.matmul(psS[0:n, t, side, :], qT[:, side, t * P:t * P + n], keysT[:, side, :], start=True, stop=True)
                last.then_inc(scored, 1)

        @block.scalar
        def _(act):
            with act.Fori(0, PH) as h:
                act.wait_ge(turned, h + 1)
                act.wait_ge(scored, h)
                act.activation(keysT[:, :, :], psK[:, :, :], ACT.Copy).then_inc(keys_copied, 1)
                act.wait_ge(summed, h + 1)
                act.activation(qT[:, :, :], psQ[:, :, 0:W], ACT.Copy).then_inc(q_copied, 1)
                act.wait_ge(shifted, h + 1)
                act.activation(find["best"][:], find["best"][:], ACT.Exp).then_inc(exped, 1)

        @block.vector
        def _(dve):
            dve.wait_ge(counted, 1)
            dve.tensor_copy(find["count"][:, :], find["count_i"][:, :]).then_inc(count_made, 1)
            dve.wait_ge(count_made, 1)
            then = Chain(dve, chain)
            for h in range(PH):
                dve.wait_ge(scored, h + 1)
                then(dve.tensor_copy(find["s"][:], psS[:]))
                dve.sem_inc(s_copied, 1)
                search(dve, then, find, n, NTI, ids_out(h), gate_out(h), shifted, exped, h)


GS = 4
UR, VR = GS, 8
SQUARES = 3
PAGE_LAG = 5


def sample_queries(nc, A, K, M, L, W):
    with ExitStack() as ctx:
        m = Mem(nc, ctx, "sqr")
        gk_n, gk_r = m.sb("gk_n", [P, 1]), m.sb("gk_r", [ROPE, 1])
        q_n = m.sb("q_n", [P, H * TS])
        w_ukT = m.sb("w_ukT", [P, 2, LAT])
        keys, sq = m.sb("keys", [TS, H, NOPE]), m.sb("sq", [TS, H, NOPE])
        kpe, kpe_sq = m.sb("kpe", [TS, ROPE]), m.sb("kpe_sq", [TS, ROPE])
        ss, kss, rstd = m.sb("ss", [TS, H]), m.sb("kss", [TS, 1]), m.sb("rstd", [TS, H])
        mask = m.sb("mask", [TS, TS, H])
        psT, psQ = m.ps("psT", [P, 2, LAT]), m.ps("psQ", [P, KL, TS, H])
        psK, psR, psE = m.ps("psK", [TS, 2, 512]), m.ps("psR", [TS, TS * H]), m.ps("psE", [TS, ROPE])
        loaded, scaled, turned, copied, q_head, q_copied = (m.sem(k) for k in ("loaded", "scaled", "turned", "copied", "q_head", "q_copied"))
        keyed, squared, rooted, scored, chain, masked, zeroed = (m.sem(k) for k in ("keyed", "squared", "rooted", "scored", "chain", "masked", "zeroed"))
        meaned = m.sem("meaned")
        block = ctx.enter_context(nc.Block())

        @block.sync
        def _(sp):
            sp.dma_start(gk_n[:, :], A["g_k"][0, 0:NOPE].rearrange("(p a) -> p a", a=1)).then_inc(loaded, 16)
            sp.dma_start(gk_r[:, :], A["g_k"][0, NOPE:DQK].rearrange("(p a) -> p a", a=1)).then_inc(loaded, 16)

        @block.gpsimd
        def _(pool):
            pool.memset(mask[:, :, :], 0.0).then_inc(zeroed, 1)
            pool.wait_ge(zeroed, 1)
            pool.affine_select(out=mask[:, :, :], in_=mask[:, :, :], compare_op=ALU.is_equal, fill=NEG, base=0,
                               pattern=[[-1, TS], [0, H]], channel_multiplier=1).then_inc(masked, 1)

        @block.tensor
        def _(pe):
            pe.wait_ge(W["w_uk_in"], 16)
            pe.wait_ge(scaled, 2)

            def turn(h):
                if h >= 2:
                    pe.wait_ge(copied, h - 1)
                for k in range(KL):
                    last = pe.transpose(psT[:, h % 2, k * P:(k + 1) * P], L["w_uk"][:, k, h * NOPE:(h + 1) * NOPE], K["ident"][:, :])
                last.then_inc(turned, 1)

            turn(0)
            for h in range(H):
                if h + 1 < H:
                    turn(h + 1)
                pe.wait_ge(copied, h + 1)
                for k in range(KL):
                    last = pe.matmul(psQ[:, k, :, h], w_ukT[:, h % 2, k * P:(k + 1) * P], q_n[:, h * TS:(h + 1) * TS], start=True, stop=True)
                last.then_inc(q_head, 1)
            for c in range(2):
                for k in range(KL):
                    last = pe.matmul(psK[:, c, :], M["ckvT"][:, k, TP:T], L["w_uk"][:, k, c * 512:(c + 1) * 512], start=(k == 0), stop=(k == KL - 1))
            pe.transpose(psE[:, :], M["kpeT"][:, TP:T], K["ident"][0:ROPE, 0:ROPE]).then_inc(keyed, 1)
            pe.wait_ge(q_copied, 1)
            for k in range(KL):
                pe.matmul(psR[:, :], M["ckvT"][:, k, TP:T], L["q_lat"][:, k].rearrange("p b h -> p (b h)"), start=(k == 0), stop=False)
            pe.matmul(psR[:, :], M["kpeT"][:, TP:T], L["q_rope"][:, :, :].rearrange("p b h -> p (b h)"), start=False, stop=True).then_inc(scored, 1)

        @block.scalar
        def _(act):
            for h in range(H):
                act.wait_ge(turned, h + 1)
                if h >= 2:
                    act.wait_ge(q_head, h - 1)
                act.activation(w_ukT[:, h % 2, :], psT[:, h % 2, :], ACT.Copy).then_inc(copied, 1)
            act.wait_ge(keyed, 1)
            act.activation(sq[:, :, :].rearrange("p h d -> p (h d)"), psK[:, :, :].rearrange("p c n -> p (c n)"), ACT.Square).then_inc(squared, 1)
            act.activation(kpe_sq[:, :], psE[:, :], ACT.Square, accum_out=kss[:, :]).then_inc(squared, 1)
            act.wait_ge(meaned, 1)
            act.activation(rstd[:, :], ss[:, :], ACT.Sqrt, scale=1.0 / DQK, bias=K["eps"][0:TS, :]).then_inc(rooted, 1)

        @block.vector
        def _(dve):
            then = Chain(dve, chain)
            dve.wait_ge(loaded, 32)
            dve.tensor_scalar(q_n[:, :], M["qs_n"][:, :], gk_n[:, :], None, ALU.mult).then_inc(scaled, 1)
            dve.tensor_scalar(L["q_rope"][:, :, :].rearrange("p b h -> p h b"), M["qs_r"][:, :].rearrange("p (h b) -> p h b", h=H),
                              gk_r[:, :], None, ALU.mult).then_inc(scaled, 1)
            dve.wait_ge(q_head, H)
            dve.tensor_copy(L["q_lat"][:, :, :, :], psQ[:, :, :, :]).then_inc(q_copied, 1)
            dve.wait_ge(squared, 2)
            then(dve.tensor_reduce(ss[:, :], sq[:, :, :], X, ALU.add))
            dve.tensor_scalar(ss[:, :], ss[:, :], kss[:, :], None, ALU.add).then_inc(meaned, 1)
            dve.wait_ge(rooted, 1)
            then(dve.reciprocal(rstd[:, :], rstd[:, :]))
            dve.wait_ge(scored, 1)
            dve.wait_ge(masked, 1)
            then(dve.tensor_tensor(L["new"][:, :, :], psR[:, :].rearrange("p (b h) -> p b h", h=H),
                                   rstd[:, :].unsqueeze(1).to_broadcast([TS, TS, H]), ALU.mult))
            dve.tensor_tensor(L["new"][:, :, :], L["new"][:, :, :], mask[:, :, :], ALU.add)


def attend_and_mix(nc, A, K, L, W, D_, outs):
    with ExitStack() as ctx:
        m = Mem(nc, ctx, "mix")
        ckv, kpe = m.sb("ckv", [P, 2, NT, LAT]), m.sb("kpe", [P, 2, NT, ROPE])
        ckvT, kpeT = m.sb("ckvT", [P, 2, KL, P]), m.sb("kpeT", [ROPE, 2, P])
        sq, kpe_sq = m.sb("sq", [P, H, NOPE]), m.sb("kpe_sq", [P, ROPE])
        q_lat, q_rope = m.sb("q_lat", [P, 2, KL, H]), m.sb("q_rope", [ROPE, 2, H])
        ss, kss, rstd = m.sb("ss", [P, 2, NT, H]), m.sb("kss", [P, 2, NT]), m.sb("rstd", [P, NT, H])
        s = m.sb("s", [P, NT + 1, H])
        top, top_row, diag8, part_sum, share = m.sb("top", [P, H]), m.sb("top_row", [H, 1]), m.sb("diag8", [H, H]), m.sb("part_sum", [P, H]), m.sb("share", [H, 1])
        o_lat = m.sb("o_lat", [H, LAT])
        table = m.sb("table", [1, TS * NT], I32)
        u, v = m.sb("u", [P, UR, D]), m.sb("v", [P, VR, D])
        h2, x1, acc = m.sb("h2", [P, 2, D]), m.sb("x1", [P, D]), m.sb("acc", [P, D])
        ids, gate, gate2 = m.sb("ids", [P, 2, SL], I32), m.sb("gate", [P, 2, SL]), m.sb("gate2", [P, D])
        dots, coef = m.sb("dots", [P, 2, SL]), m.sb("coef", [P, 2, SL])
        psT, psK, psN, psR, psO, psS = (m.ps("psT", [P, 512]), m.ps("psK", [ROPE, P]), m.ps("psN", [P, 2, 512]),
                                        m.ps("psR", [P, 512]), m.ps("psO", [H, 512]), m.ps("psS", [P, 512]))
        psTop, psBc, psSum, psOT = psS[0:H, 0:P], psS[:, 256:264], psS[0:H, 272:273], psS[:, 288:320]
        pages_in = [m.sem(f"pages_in{b}") for b in range(2)]
        pages_used = [m.sem(f"pages_used{b}") for b in range(2)]
        (table_in, q_set, turned, copied, keyed, squared, meaned, rooted, topped, top_turned,
         diag_made, top_spread, shifted, exped, summed, sums_made, sums_turned, weighed, scaled, o_turned, chain) = (m.sem(k) for k in (
             "table_in", "q_set", "turned", "copied", "keyed", "squared", "meaned", "rooted", "topped",
             "top_turned", "diag_made", "top_spread", "shifted", "exped", "summed", "sums_made", "sums_turned", "weighed", "scaled",
             "o_turned", "chain"))
        u_in, u_used = [m.sem(f"u_in{k}") for k in range(UR)], [m.sem(f"u_used{k}") for k in range(UR)]
        v_in, v_used = [m.sem(f"v_in{k}") for k in range(VR)], [m.sem(f"v_used{k}") for k in range(VR)]
        tile_in, tile_used = [m.sem(f"tile_in{k}") for k in range(2)], [m.sem(f"tile_used{k}") for k in range(2)]
        gelued, weighted, x1_in, y_made, y_stored, gate2_made, gate2_spread, held = (
            m.sem(k) for k in ("gelued", "weighted", "x1_in", "y_made", "y_stored", "gate2_made", "gate2_spread", "held"))
        block = ctx.enter_context(nc.Block())
        TURNS = TT // 2
        SLOTS = 2 * SL
        SEQS = TS // TURNS
        PAGES = SEQS * NT
        UROUNDS, VROUNDS, GROUPS = SLOTS // UR, SLOTS // VR, SLOTS // GS
        u_rows, v_rows = A["peer_u"].rearrange("l e d -> (l e) d"), A["peer_v"].rearrange("l e d -> (l e) d")

        page_slot = [g * (SLOTS - 14) // (PAGES - 1) for g in range(PAGES)]
        page_at = {x: g for g, x in enumerate(page_slot)}
        square_at = {x + SQUARES: g for g, x in enumerate(page_slot)}
        end = [page_slot[(q + 1) * NT - 1] + PAGE_LAG for q in range(SEQS)]
        ending = lambda x, behind: [q for q in range(SEQS) if end[q] + behind == x]
        LAST_SLOT = end[-1] + 16

        def hold(eng, sem, value):
            eng.wait_ge(sem, value)
            eng.sem_inc(held, 1)

        @block.sync
        def _(sp):
            sp.dma_start(table[:, :], A["page_table"].rearrange("b n -> (b n)").unsqueeze(0)).then_inc(table_in, 16)
            sp.wait_ge(table_in, 16)
            with sp.Fori(0, TURNS) as i:
                for q in range(SEQS):
                    b = q % 2
                    if q % 2 == 0:
                        half = q // 2
                        sp.wait_ge(tile_used[half], i)
                        for tile, name in ((ids, "ids"), (h2, "h2"), (gate, "gate")):
                            sp.dma_start(tile[:, half, :], D_[name][bass.ds(i * 2 + half, 1)].rearrange("a p s -> (a p) s")).then_inc(tile_in[half], 16)
                    sp.wait_ge(pages_used[b], i * (SEQS // 2) + q // 2)
                    for t in range(NT):
                        page = sp.value_load(table[0:1, bass.ds(i * PAGES + (q * NT + t), 1)], min_val=0, max_val=A["cache_ckv"].shape[1] - 1)
                        sp.dma_start(ckv[:, b, t, :], A["cache_ckv"][0, bass.ds(page, 1)].rearrange("a p c -> (a p) c")).then_inc(pages_in[b], 16)
                        sp.dma_start(kpe[:, b, t, :], A["cache_kpe"][0, bass.ds(page, 1)].rearrange("a p c -> (a p) c")).then_inc(pages_in[b], 16)

        @block.gpsimd
        def _(pool):
            with pool.Fori(0, TURNS) as i:
                for x in range(SLOTS):
                    half, slot = x // SL, x % SL
                    if slot == 0:
                        hold(pool, tile_in[half], i * 48 + 48)
                    for ring, n, used, landed, table_rows in ((u, UR, u_used, u_in, u_rows), (v, VR, v_used, v_in, v_rows)):
                        hold(pool, used[x % n], i * (SLOTS // n) + x // n)
                        pool.indirect_dma_start(ring[:, x % n, :], None, table_rows,
                                                bass.IndirectOffsetOnAxis(ids[:, half, slot:slot + 1], 0)).then_inc(landed[x % n], 16)

        @block.tensor
        def _(pe):
            pe.wait_ge(W["weights_in"], 32)
            for c in range(2):
                last = pe.matmul(psN[:, c, :], K["last"][:, :], K["ada"][:, 5 * D + c * 512:5 * D + (c + 1) * 512], start=True, stop=True)
            last.then_inc(gate2_spread, 1)
            pe.wait_ge(gate2_made, 1)
            with pe.Fori(0, TURNS) as i:

                def turn(g):
                    q, t = g // NT, g % NT
                    if t == 0:
                        pe.wait_ge(pages_in[q % 2], i * (SEQS // 2 * NT * 32) + (q // 2 + 1) * (NT * 32))
                    pe.wait_ge(copied, (i * PAGES + g) * 2)
                    for k in range(KL):
                        pe.transpose(psT[:, k * P:(k + 1) * P], ckv[:, q % 2, t, k * P:(k + 1) * P], K["ident"][:, :])
                    pe.transpose(psK[:, :], kpe[:, q % 2, t, :], K["ident"][:, :]).then_inc(turned, 1)

                turn(0)
                for x in range(LAST_SLOT):
                    if x in page_at:
                        g = page_at[x]
                        q, t = g // NT, g % NT
                        n = i * SEQS + q
                        if g + 1 < PAGES:
                            turn(g + 1)
                        pe.wait_ge(squared, (i * PAGES + g) * 2)
                        pe.wait_ge(copied, (i * PAGES + (g + 1)) * 2)
                        for c in range(2):
                            for k in range(KL):
                                last = pe.matmul(psN[:, c, :], ckvT[:, g % 2, k, :], L["w_uk"][:, k, c * 512:(c + 1) * 512], start=(k == 0), stop=(k == KL - 1))
                            last.then_inc(keyed, 1)
                        if t == 0:
                            pe.wait_ge(q_set, n * 2 + 2)
                            pe.wait_ge(topped, n)
                        for k in range(KL):
                            pe.matmul(psR[:, t * H:(t + 1) * H], ckvT[:, g % 2, k, :], q_lat[:, q % 2, k, :], start=(k == 0), stop=False)
                        pe.matmul(psR[:, t * H:(t + 1) * H], kpeT[:, g % 2, :], q_rope[:, q % 2, :], start=False, stop=True).then_inc(summed, 1)
                    for q in ending(x, 3):
                        pe.wait_ge(topped, i * SEQS + (q + 1))
                        pe.transpose(psTop, top[:, :], K["ident"][:, :]).then_inc(top_turned, 1)
                    for q in ending(x, 5):
                        pe.wait_ge(diag_made, i * SEQS + (q + 1))
                        pe.matmul(psBc, K["ones"][0:H, :], diag8[:, :], start=True, stop=True).then_inc(top_spread, 1)
                    for q in ending(x, 8):
                        pe.wait_ge(exped, i * SEQS + (q + 1))
                        pe.wait_ge(sums_made, i * SEQS + (q + 1))
                        pe.matmul(psSum, part_sum[:, :], K["ones"][:, 0:1], start=True, stop=True).then_inc(sums_turned, 1)
                        for t in range(NT):
                            pe.matmul(psO[:, :], s[:, t, :], ckv[:, q % 2, t, :], start=(t == 0), stop=False)
                        pe.matmul(psO[:, :], s[0:TS, NT, :], L["ckv_new"][:, :], start=False, stop=True).then_inc(weighed, 1)
                    for q in ending(x, 14):
                        hold(pe, scaled, i * SEQS + (q + 1))
                        for k in range(KL):
                            last = pe.transpose(psOT[:, k * H:(k + 1) * H], o_lat[:, k * P:(k + 1) * P], K["ident"][0:H, 0:H])
                        last.then_inc(o_turned, 1)

        @block.scalar
        def _(act):
            with act.Fori(0, TURNS) as i:

                def copy(g):
                    act.wait_ge(turned, i * PAGES + (g + 1))
                    act.wait_ge(summed, i * PAGES + max(g - 1, 0))
                    act.activation(ckvT[:, g % 2].rearrange("p k n -> p (k n)"), psT[:, :], ACT.Copy).then_inc(copied, 1)
                    act.activation(kpeT[:, g % 2, :], psK[:, :], ACT.Copy).then_inc(copied, 1)

                copy(0)
                for x in range(LAST_SLOT):
                    if x in page_at and page_at[x] + 1 < PAGES:
                        copy(page_at[x] + 1)
                    if x in square_at:
                        g = square_at[x]
                        q, t = g // NT, g % NT
                        act.wait_ge(squared, (i * PAGES + g) * 2)
                        act.activation(kpe_sq[:, :], kpe[:, q % 2, t, :], ACT.Square, accum_out=kss[:, q % 2, t:t + 1])
                        for c in range(2):
                            act.wait_ge(keyed, (i * PAGES + g) * 2 + (c + 1))
                            for h in range(H // 2):
                                last = act.activation(sq[:, c * (H // 2) + h, :], psN[:, c, h * NOPE:(h + 1) * NOPE], ACT.Square,
                                                      accum_out=ss[:, q % 2, t, c * (H // 2) + h:c * (H // 2) + h + 1])
                            last.then_inc(squared, 1)
                    for q in ending(x, 1):
                        act.wait_ge(meaned, i * SEQS + (q + 1))
                        act.activation(rstd[:, :, :], rstd[:, :, :], ACT.Sqrt, scale=1.0 / DQK, bias=K["eps"][:, :]).then_inc(rooted, 1)
                    for q in ending(x, 7):
                        act.wait_ge(shifted, i * SEQS + (q + 1))
                        act.activation(s[:, :, :], s[:, :, :], ACT.Exp, scale=SCALE).then_inc(exped, 1)
                    if x < SLOTS and x % GS == GS - 1:
                        half, at = x // SL, x % SL - (GS - 1)
                        act.wait_ge(u_used[x % UR], i * UROUNDS + (x // UR + 1))
                        act.activation(coef[:, half, at:at + GS], dots[:, half, at:at + GS], ACT.Gelu).then_inc(gelued, 1)
                    if x % SL == SL // 2:
                        act.wait_ge(y_stored, (i * 2 + x // SL) * 16)
                        act.dma_start(x1[:, :], D_["x1"][bass.ds(i * 2 + x // SL, 1)].rearrange("a p s -> (a p) s")).then_inc(x1_in, 16)
                    if x >= SL and x % SL == GS + 2:
                        act.wait_ge(y_made, i * 2 + x // SL)
                        act.dma_start(outs["y_p"][0, bass.ds((i * 2 + (x // SL - 1)) * P, P), :], x1[:, :]).then_inc(y_stored, 16)
            act.wait_ge(y_stored, TT * 16)

        @block.vector
        def _(dve):
            dve.wait_ge(gate2_spread, 1)
            dve.tensor_copy(gate2[:, :], psN[:, :, :].rearrange("p c n -> p (c n)")).then_inc(gate2_made, 1)
            dve.wait_ge(gate2_made, 1)
            with dve.Fori(0, TURNS) as i:
                then = Steps(dve, chain, SEQS * 7 + 2, i)

                def add(x):
                    half, slot = x // SL, x % SL
                    c = coef[:, half, slot:slot + 1]
                    dve.wait_ge(v_in[x % VR], (i * VROUNDS + (x // VR + 1)) * 16)
                    if slot == 0:
                        last = dve.tensor_scalar(acc[:, :], v[:, x % VR, :], c, None, ALU.mult)
                    else:
                        dve.wait_ge(v_used[(x - 1) % VR], i * VROUNDS + ((x - 1) // VR + 1))
                        last = dve.scalar_tensor_tensor(acc[:, :], v[:, x % VR, :], c, acc[:, :], ALU.mult, ALU.add)
                    last.then_inc(v_used[x % VR], 1)
                    if slot == SL - 1:
                        dve.wait_ge(v_used[x % VR], i * VROUNDS + (x // VR + 1))
                        dve.sem_inc(tile_used[half], 1)
                        then(dve.tensor_tensor(acc[:, :], acc[:, :], gate2[:, :], ALU.mult))
                        dve.wait_ge(x1_in, (i * 2 + half) * 16 + 16)
                        dve.tensor_tensor(x1[:, :], x1[:, :], acc[:, :], ALU.add).then_inc(y_made, 1)
                        dve.wait_ge(y_made, i * 2 + (half + 1))

                for x in range(LAST_SLOT):
                    if x in page_at and page_at[x] % NT == 0:
                        q = page_at[x] // NT
                        n = i * SEQS + q
                        dve.tensor_scalar(q_lat[:, q % 2], L["q_lat"][:, :, bass.ds(n, 1), :].rearrange("p k a h -> p k (a h)"), 1.0, None, ALU.mult).then_inc(q_set, 1)
                        dve.tensor_scalar(q_rope[:, q % 2], L["q_rope"][:, bass.ds(n, 1), :].rearrange("p a h -> p (a h)"), 1.0, None, ALU.mult).then_inc(q_set, 1)
                    for q in ending(x, 0):
                        dve.wait_ge(squared, (i * PAGES + (q + 1) * NT) * 2)
                        dve.tensor_tensor(rstd[:, :, :], ss[:, q % 2], kss[:, q % 2].unsqueeze(2).to_broadcast([P, NT, H]), ALU.add).then_inc(meaned, 1)
                    for q in ending(x, 2):
                        n = i * SEQS + q
                        dve.wait_ge(rooted, n + 1)
                        then(dve.reciprocal(rstd[:, :, :], rstd[:, :, :]))
                        dve.wait_ge(summed, (i * PAGES + (q + 1) * NT))
                        dve.tensor_tensor(s[:, 0:NT, :], psR[:, 0:NT * H].rearrange("p (t h) -> p t h", h=H), rstd[:, :, :], ALU.mult)
                        then(dve.memset(s[:, NT, :], NEG))
                        then(dve.tensor_scalar(s[0:TS, NT, :], L["new"][:, bass.ds(n, 1), :].rearrange("p a h -> p (a h)"), 1.0, None, ALU.mult))
                        dve.tensor_reduce(top[:, :], s[:, :, :].rearrange("p t h -> p h t"), X, ALU.max).then_inc(topped, 1)
                    for q in ending(x, 4):
                        dve.wait_ge(top_turned, i * SEQS + (q + 1))
                        then(dve.tensor_reduce(top_row[:, :], psTop, X, ALU.max))
                        dve.tensor_scalar(diag8[:, :], K["ident"][0:H, 0:H], top_row[:, :], None, ALU.mult).then_inc(diag_made, 1)
                    for q in ending(x, 6):
                        dve.wait_ge(top_spread, i * SEQS + (q + 1))
                        dve.tensor_tensor(s[:, :, :], s[:, :, :], psBc.unsqueeze(1).to_broadcast([P, NT + 1, H]), ALU.subtract).then_inc(shifted, 1)
                    for q in ending(x, 8):
                        dve.wait_ge(exped, i * SEQS + (q + 1))
                        dve.tensor_reduce(part_sum[:, :], s[:, :, :].rearrange("p t h -> p h t"), X, ALU.add).then_inc(sums_made, 1)
                    for q in ending(x, 13):
                        dve.wait_ge(sums_turned, i * SEQS + (q + 1))
                        then(dve.reciprocal(share[:, :], psSum))
                        dve.wait_ge(weighed, i * SEQS + (q + 1))
                        then(dve.tensor_scalar(o_lat[:, :], psO[:, :], share[:, :], None, ALU.mult))
                        dve.sem_inc(scaled, 1)
                        dve.sem_inc(pages_used[q % 2], 1)
                    for q in ending(x, 15):
                        dve.wait_ge(o_turned, i * SEQS + (q + 1))
                        then(dve.tensor_scalar(L["o_lat"][:, bass.ds(i * SEQS + q, 1), :].rearrange("p a k -> p (a k)"), psOT, 1.0, None, ALU.mult))
                    if x < SLOTS:
                        half, slot = x // SL, x % SL
                        if slot == 0:
                            dve.wait_ge(tile_in[half], i * 48 + 48)
                        dve.wait_ge(u_in[x % UR], (i * UROUNDS + (x // UR + 1)) * 16)
                        dve.tensor_tensor_reduce(u[:, x % UR, :], u[:, x % UR, :], h2[:, half, :], 1.0, 0.0, ALU.mult, ALU.add, dots[:, half, slot:slot + 1]).then_inc(u_used[x % UR], 1)
                    if GS <= x < SLOTS + GS:
                        if x % GS == 0:
                            g = x // GS - 1
                            half, at = g * GS // SL, g * GS % SL
                            dve.wait_ge(gelued, i * GROUPS + (g + 1))
                            dve.tensor_tensor(coef[:, half, at:at + GS], coef[:, half, at:at + GS], gate[:, half, at:at + GS], ALU.mult).then_inc(weighted, 1)
                            dve.wait_ge(weighted, i * GROUPS + (g + 1))
                        add(x - GS)
                then.full()


def sample_rows(nc, A, K, L, W, parts, x1):
    with ExitStack() as ctx:
        m = Mem(nc, ctx, "srw")
        oT, mT = m.sb("oT", [P, H, TS]), m.sb("mT", [P, KD, TS])
        psV, psM, psX = m.ps("psV", [P, H, TS]), m.ps("psM", [P, KD, TS]), m.ps("psX", [TS, 2, 512])
        valued, o_copied, merged, m_made, mixed, x_in, chain = (m.sem(n) for n in ("valued", "o_copied", "merged", "m_made", "mixed", "x_in", "chain"))
        block = ctx.enter_context(nc.Block())

        @block.sync
        def _(sp):
            sp.dma_start(x1[:, 0, :], A["x_sample"].rearrange("b t d -> (b t) d")).then_inc(x_in, 16)

        @block.tensor
        def _(pe):
            pe.wait_ge(W["w_uv_in"], 16)
            for h in range(H):
                for k in range(KL):
                    last = pe.matmul(psV[:, h, :], W["w_uv"][:, k, h * DV:(h + 1) * DV], L["o_lat"][:, :, k * H + h], start=(k == 0), stop=(k == KL - 1))
            last.then_inc(valued, 1)
            pe.wait_ge(o_copied, 1)
            pe.wait_ge(W["w_a_in"], 16)
            for d in range(KD):
                for h in range(H):
                    last = pe.matmul(psM[:, d, :], W["w_a"][:, h, d * P:(d + 1) * P], oT[:, h, :], start=(h == 0), stop=(h == H - 1))
            last.then_inc(merged, 1)
            pe.wait_ge(m_made, 1)
            pe.wait_ge(W["w_out_in"], 16)
            for c in range(2):
                for k in range(KD):
                    last = pe.matmul(psX[:, c, :], mT[:, k, :], W["w_out"][:, k, c * 512:(c + 1) * 512], start=(k == 0), stop=(k == KD - 1))
            last.then_inc(mixed, 1)

        @block.vector
        def _(dve):
            then = Chain(dve, chain)
            dve.wait_ge(valued, 1)
            dve.tensor_copy(oT[:, :, :], psV[:, :, :]).then_inc(o_copied, 1)
            dve.wait_ge(merged, 1)
            then(dve.tensor_tensor(mT[:, :, :], psM[:, :, :], parts["gate_a"][:, :, :], ALU.mult))
            dve.tensor_tensor(mT[:, :, :], mT[:, :, :], parts["b"][:, :, :], ALU.add).then_inc(m_made, 1)
            dve.wait_ge(mixed, 1)
            dve.wait_ge(W["ada_in"], 16)
            flat = psX[:, :, :].rearrange("p c n -> p (c n)")
            then(dve.tensor_tensor(flat, flat, K["ada"][0:TS, 2 * D:3 * D], ALU.mult))
            dve.wait_ge(x_in, 16)
            dve.tensor_tensor(x1[:, 0, :], x1[:, 0, :], flat, ALU.add)


def choose_samples(nc, A, K, W, h2T, ids, gate):
    PAIRS = PH * TS
    with ExitStack() as ctx:
        m = Mem(nc, ctx, "chz")
        STEP = P + TS
        q_wide = m.sb("q_wide", [P, 2, PH, STEP])
        keysT = m.sb("keysT", [P, PH * 2, NK])
        find = search_buffers(m, 1)
        psQ, psK, psS = m.ps("psQ", [P, PH, 2, TS]), m.ps("psK", [P, 4, 512]), m.ps("psS", [P, 1, 2, NK])
        zeroed, turned, keys_copied, summed, spread, scored = (m.sem(n) for n in ("zeroed", "turned", "keys_copied", "summed", "spread", "scored"))
        shifted, exped, chain, counted, count_made = (m.sem(n) for n in ("shifted", "exped", "chain", "counted", "count_made"))
        block = ctx.enter_context(nc.Block())

        @block.gpsimd
        def _(pool):
            pool.memset(q_wide[:, :, :, :], 0.0).then_inc(zeroed, 1)
            pool.iota(find["count_i"][:, :], pattern=[[1, TK]], base=0, channel_multiplier=0).then_inc(counted, 1)

        @block.tensor
        def _(pe):
            pe.wait_ge(W["keys_in"], 32)
            for j in range(PH * 2):
                last = pe.transpose(psK[:, j // 4, j % 4 * P:(j % 4 + 1) * P], W["keys"][:, j % 2, j // 2, :], K["ident"][:, :])
            last.then_inc(turned, 1)
            for h in range(PH):
                if h % (PH // 2) == 0:
                    pe.wait_ge(W["wq_in"][h // (PH // 2)], 16)
                w = W["wq"][h // (PH // 2)]
                for side in range(2):
                    at = h % (PH // 2) * WQ + side * P
                    for k in range(KD):
                        last = pe.matmul(psQ[:, h, side, :], w[:, k, at:at + P], h2T[:, k, :], start=(k == 0), stop=(k == KD - 1))
            last.then_inc(summed, 1)
            pe.wait_ge(spread, 4)
            pe.wait_ge(keys_copied, 1)
            for side in range(2):
                flat = q_wide[:, side].rearrange("p h e -> p (h e)")
                for h in range(PH):
                    last = pe.matmul(psS[:, 0, side, :], flat[:, h * P:(h + 1) * P], keysT[:, 2 * h + side, :], start=(h == 0), stop=(h == PH - 1))
            last.then_inc(scored, 1)

        @block.scalar
        def _(act):
            act.wait_ge(turned, 1)
            act.activation(keysT[:, :, :].rearrange("p j n -> p (j n)"), psK[:, :, :].rearrange("p c n -> p (c n)"), ACT.Copy).then_inc(keys_copied, 1)
            act.wait_ge(shifted, 1)
            act.activation(find["best"][:], find["best"][:], ACT.Exp).then_inc(exped, 1)

        @block.vector
        def _(dve):
            then = Chain(dve, chain)
            dve.wait_ge(counted, 1)
            dve.tensor_copy(find["count"][:, :], find["count_i"][:, :]).then_inc(count_made, 1)
            dve.wait_ge(count_made, 1)
            dve.wait_ge(zeroed, 1)
            dve.wait_ge(summed, 1)
            for side in range(2):
                for at in (0, PAIRS):
                    dve.tensor_copy(q_wide[:, side, :, at:at + TS], psQ[:, :, side, :]).then_inc(spread, 1)
            dve.wait_ge(scored, 1)
            then(dve.tensor_copy(find["s"][:], psS[:]))
            search(dve, then, find, P, 1, ids[:], gate[:], shifted, exped, 0)


def sample_experts(nc, A, K, h2, x1, ids, gate, outs):
    NB = TK // 2
    with ExitStack() as ctx:
        m = Mem(nc, ctx, "sex")
        u, v = m.sb("u", [P, NB, D]), m.sb("v", [P, NB, D])
        coef, coefs = m.sb("coef", [P, NB]), m.sb("coefs", [P, NB, TS])
        mine, mineT = m.sb("mine", [P, TS]), m.sb("mineT", [TS, P // TS, TS])
        ids_half, gate_half = m.sb("ids_half", [P, NB], I32), m.sb("gate_half", [P, NB])
        y = m.sb("y", [TS, D])
        psH, psY = m.ps("psH", [P, 2, 512]), m.ps("psY", [TS, 2, 512])
        set_, spread, dotted, gelued, weighted, mixed, y_done, chain, stored, mine_made = (m.sem(k) for k in (
            "set", "spread", "dotted", "gelued", "weighted", "mixed", "y_done", "chain", "stored", "mine_made"))
        u_in, v_in = [m.sem(f"u_in{k}") for k in range(NB)], [m.sem(f"v_in{k}") for k in range(NB)]
        block = ctx.enter_context(nc.Block())
        u_rows, v_rows = A["peer_u"].rearrange("l e d -> (l e) d"), A["peer_v"].rearrange("l e d -> (l e) d")

        @block.gpsimd
        def _(pool):
            pool.wait_ge(set_, 2)
            for rows_, landed, table in ((u, u_in, u_rows), (v, v_in, v_rows)):
                for k in range(NB):
                    pool.indirect_dma_start(rows_[:, k, :], None, table, bass.IndirectOffsetOnAxis(ids_half[:, k:k + 1], 0)).then_inc(landed[k], 16)

        @block.tensor
        def _(pe):
            pe.wait_ge(mine_made, 1)
            for c in range(2):
                last = pe.matmul(psH[:, c, :], mineT[:, :, :].rearrange("p j b -> p (j b)"), h2[:, c * 512:(c + 1) * 512], start=True, stop=True)
            last.then_inc(spread, 1)
            pe.wait_ge(weighted, 1)
            for k in range(NB):
                pe.wait_ge(v_in[k], 16)
                for c in range(2):
                    last = pe.matmul(psY[:, c, :], coefs[:, k, :], v[:, k, c * 512:(c + 1) * 512], start=(k == 0), stop=(k == NB - 1), skip_group_check=True)
            last.then_inc(mixed, 1)

        @block.scalar
        def _(act):
            act.wait_ge(dotted, NB)
            act.activation(coef[:, :], coef[:, :], ACT.Gelu).then_inc(gelued, 1)
            act.wait_ge(y_done, 1)
            act.dma_start(outs["y_s"].rearrange("b t d -> (b t) d"), y[:, :]).then_inc(stored, 16)
            act.wait_ge(stored, 16)

        @block.vector
        def _(dve):
            then = Chain(dve, chain)
            for lo, hi, cols in ((0, P // 2, slice(0, NB)), (P // 2, P, slice(NB, TK))):
                dve.tensor_copy(ids_half[lo:hi, :], ids[lo:hi, 0, cols]).then_inc(set_, 1)
                then(dve.tensor_copy(gate_half[lo:hi, :], gate[lo:hi, 0, cols]))
            dve.tensor_copy(mineT[:, :, :], K["ident"][0:TS, 0:TS].unsqueeze(1).to_broadcast([TS, P // TS, TS])).then_inc(mine_made, 1)
            then(dve.tensor_reduce(mine[:, :], K["ident"][:, :].rearrange("p (j b) -> p b j", b=TS), X, ALU.add))
            dve.wait_ge(spread, 1)
            for k in range(NB):
                dve.wait_ge(u_in[k], 16)
                dve.tensor_tensor_reduce(u[:, k, :], u[:, k, :], psH[:, :, :].rearrange("p c n -> p (c n)"), 1.0, 0.0,
                                         ALU.mult, ALU.add, coef[:, k:k + 1]).then_inc(dotted, 1)
            dve.wait_ge(gelued, 1)
            then(dve.tensor_tensor(coef[:, :], coef[:, :], gate_half[:, :], ALU.mult))
            dve.tensor_tensor(coefs[:, :, :], mine[:, :].unsqueeze(1).to_broadcast([P, NB, TS]),
                              coef[:, :].unsqueeze(2).to_broadcast([P, NB, TS]), ALU.mult).then_inc(weighted, 1)
            dve.wait_ge(mixed, 1)
            then(dve.tensor_tensor(y[:, :], psY[:, :, :].rearrange("p c n -> p (c n)"), K["ada"][0:TS, 5 * D:6 * D], ALU.mult))
            dve.tensor_tensor(y[:, :], y[:, :], x1, ALU.add).then_inc(y_done, 1)


def fetch(nc, tag, W, tiles):
    with ExitStack() as ctx:
        sems = {name: Mem(nc, ctx, tag).sem(name) for name in dict.fromkeys(n for n, _, _ in tiles)}
        block = ctx.enter_context(nc.Block())

        @block.sync
        def _(sp):
            for name, tile, src in tiles:
                sp.dma_start(tile, src).then_inc(sems[name], 16)
    W.update({name + "_in": sem for name, sem in sems.items()})


def step(nc, A, outs, D_):
    with ExitStack() as whole:
        m = Mem(nc, whole, "all")
        K = {name: m.sb(name, shape) for name, shape in (
            ("ident", [P, P]), ("ones", [P, P]), ("bias", [P, P]), ("keep", [P, P]), ("swap", [ROPE, ROPE]),
            ("last", [TS + 1, P]), ("eps", [P, 1]))}
        L = {"q_lat": m.sb("q_lat", [P, KL, TS, H]), "q_rope": m.sb("q_rope", [ROPE, TS, H]), "new": m.sb("new", [TS, TS, H]),
             "ckv_new": m.sb("ckv_new", [TS, LAT]), "o_lat": m.sb("o_lat", [P, TS, KL * H])}
        parts = {"gate_a": m.sb("gate_a", [P, KD, TS]), "b": m.sb("part_b", [P, KD, TS])}
        by_tile = lambda ap: ap.rearrange("t p d -> p t d")
        with ExitStack() as front:
            m = Mem(nc, front, "frt")
            constants(nc, K)
            S = {"x": m.sb("x", [P, KC, T]), "skip": m.sb("skip", [P, KI]), "g_ssm": m.sb("g_ssm", [P, KI]),
                 "acs": m.sb("acs", [SH, T]), "dt": m.sb("dt", [SH, T]), "a": m.sb("a", [SH, 1]), "decay_s": m.sb("decay_s", [SH, TS]),
                 "dt_tok": m.sb("dt_tok", [P, TT, SH]), "acs_tok": m.sb("acs_tok", [P, TT, SH])}
            with ExitStack() as part:
                part.enter_context(own_semaphores(nc))
                n = Mem(nc, part, "inp")
                h_hi, h_lo = n.sb("h_hi", [P, KD, T], F32R), n.sb("h_lo", [P, KD, T], F32R)
                with ExitStack() as rows_:
                    o = Mem(nc, rows_, "inx")
                    K["ada"] = o.sb("ada", [TS + 1, 6 * D])
                    conditioning(nc, A, K)
                    store(nc, "sad", [(D_["ada"], K["ada"])])
                    x = o.sb("x", [P, TT + 1, D])
                    modulated(nc, K, "mod1", [(x[:, 0:TT, :], A["x_prompt"].rearrange("b (t p) d -> p (b t) d", p=P)),
                                              (x[0:TS, TT, :], A["x_sample"].rearrange("b t d -> (b t) d"))],
                              x, A["g_mix"], 0, D, x, (h_hi, h_lo))
                with ExitStack() as steps:
                    o = Mem(nc, steps, "stx")
                    K["spread"] = o.sb("spread", [SH, DI])
                    S["dt_raw"] = o.sb("dt_raw", [SH, T])
                    head_channels(nc, K)
                    convolution(nc, A, K, S, h_hi, h_lo, D_["proj"], outs)
                    sample_scan(nc, A, K, S, h_hi, h_lo, D_["proj"], D_["acs"], outs)
                prompt_scan(nc, A, K, S, h_hi, h_lo, D_["proj"], D_["acs"], outs)
            gated_norm(nc, A, K, S, D_["proj"])
            oT = m.sb("oT", [P, H * T])
            with ExitStack() as part:
                part.enter_context(own_semaphores(nc))
                n = Mem(nc, part, "mla")
                M = {"ckvT": n.sb("ckvT", [P, KL, T]), "kpeT": n.sb("kpeT", [ROPE, T]), "kpe_sq": n.sb("kpe_sq", [ROPE, T]),
                     "ckv_s": L["ckv_new"], "cos": n.sb("cos", [ROPE, T]), "sin": n.sb("sin", [ROPE, T]),
                     "qs_n": n.sb("qs_n", [P, H * TS]), "qs_r": n.sb("qs_r", [ROPE, H * TS])}
                latents(nc, A, K, M, D_["proj"], outs)
                L["w_uk"], W = n.sb("w_uk", [P, KL, H * NOPE]), {}
                fetch(nc, "ft1", W, [("w_uk", L["w_uk"][:], A["w_uk"].rearrange("l (k p) h d -> p (l k) (h d)", p=P))])
                prompt_attention(nc, A, K, M, D_["proj"], oT)
                sample_queries(nc, A, K, M, L, W)
            K["ada"] = m.sb("ada", [TS + 1, 6 * D])
            load(nc, "lad", [(K["ada"], D_["ada"])])
            mT, x1 = m.sb("mT", [P, KD, TP]), m.sb("x1", [P, TT, D])
            W = {"w_out": m.sb("w_out", [P, KD, D])}
            W.update({name: m.sem(name) for name in ("w_out_in", "x_in")})
            merge(nc, A, K, D_["proj"], oT[:, :].rearrange("p (h t) -> p h t", h=H)[:, :, 0:TP], S["x"][:, 0:KI, :], mT, parts, W, x1)
            residual(nc, A, K, mT, W, x1)
            store(nc, "sx1", [(by_tile(D_["x1"]), x1)])
        with ExitStack() as part:
            part.enter_context(own_semaphores(nc))
            m = Mem(nc, part, "exp")
            K["ada"] = m.sb("ada", [TS + 1, 6 * D])
            load(nc, "lae", [(K["ada"], D_["ada"])])
            h2, h2T = m.sb("h2", [P, TT, D]), m.sb("h2T", [P, KD, TP])
            modulated(nc, K, "mod2", [(h2[:, :, :], by_tile(D_["x1"]))], h2, A["g_ffn"], 3 * D, 4 * D, h2, h2T, samples=False)
            ids, gate = m.sb("ids", [P, TT, SL], I32), m.sb("gate", [P, TT, SL])
            head = lambda tile: (lambda h: tile[:, :, h * TK:(h + 1) * TK])
            choose(nc, A, K, h2T, head(ids), head(gate))
            store(nc, "sh2", [(by_tile(D_["h2"]), h2), (by_tile(D_["ids"]), ids), (by_tile(D_["gate"]), gate)])
        with ExitStack() as part:
            part.enter_context(own_semaphores(nc))
            m = Mem(nc, part, "mx0")
            L["w_uk"], K["ada"] = m.sb("w_uk", [P, KL, H * NOPE]), m.sb("ada", [TS + 1, 6 * D])
            W = {}
            fetch(nc, "ft3", W, [("weights", K["ada"][:], D_["ada"]),
                                 ("weights", L["w_uk"][:], A["w_uk"].rearrange("l (k p) h d -> p (l k) (h d)", p=P))])
            attend_and_mix(nc, A, K, L, W, D_, outs)
        with ExitStack() as part:
            part.enter_context(own_semaphores(nc))
            m = Mem(nc, part, "smp")
            K["ada"] = m.sb("ada", [TS + 1, 6 * D])
            x1, h2, h2T = m.sb("x1", [TS, 1, D]), m.sb("h2", [TS, 1, D]), m.sb("h2T", [P, KD, TS])
            ids, gate = m.sb("ids", [P, 1, TK], I32), m.sb("gate", [P, 1, TK])
            W = {}
            flat = lambda name: A[name].rearrange("l (k p) h d -> p (l k) (h d)", p=P)
            wide = lambda name: A[name].rearrange("l (k p) n -> p (l k) n", p=P)
            with ExitStack() as queries:
                n = Mem(nc, queries, "smq")
                W["keys"] = n.sb("keys", [P, 2, PH, NK])
                W["wq"] = [n.sb("wq0", [P, KD, PH * WQ // 2])]
                with ExitStack() as values:
                    o = Mem(nc, values, "smv")
                    W["w_uv"], W["w_a"], W["w_out"] = o.sb("w_uv", [P, KL, H * DV]), o.sb("w_a", [P, H, D]), o.sb("w_out", [P, KD, D])
                    fetch(nc, "ft0", W, [("w_uv", W["w_uv"][:], flat("w_uv")), ("w_a", W["w_a"][:], wide("w_br_a")),
                                         ("ada", K["ada"][:], D_["ada"]), ("w_out", W["w_out"][:], wide("w_out")),
                                         ("keys", W["keys"][:, 0], A["peer_keys1"].rearrange("l h n d -> n (l h) d")),
                                         ("keys", W["keys"][:, 1], A["peer_keys2"].rearrange("l h n d -> n (l h) d")),
                                         ("wq0", W["wq"][0][:], wide("peer_wq")[:, :, 0:PH * WQ // 2])])
                    sample_rows(nc, A, K, L, W, parts, x1)
                W["wq"].append(n.sb("wq1", [P, KD, PH * WQ // 2]))
                fetch(nc, "ft2", W, [("wq1", W["wq"][1][:], wide("peer_wq")[:, :, PH * WQ // 2:])])
                W["wq_in"] = [W["wq0_in"], W["wq1_in"]]
                modulated(nc, K, "mod3", [], x1, A["g_ffn"], 3 * D, 4 * D, h2, h2T, prompt=False)
                choose_samples(nc, A, K, W, h2T, ids, gate)
            sample_experts(nc, A, K, h2[:, 0, :], x1[:, 0, :], ids, gate, outs)


def copies(nc, tag, pairs, name):
    with ExitStack() as ctx:
        done = Mem(nc, ctx, tag).sem(name)
        block = ctx.enter_context(nc.Block())

        @block.sync
        def _(sp):
            for to, of in pairs:
                sp.dma_start(to, of).then_inc(done, 16)
            sp.wait_ge(done, 16 * len(pairs))


def store(nc, tag, pairs):
    copies(nc, tag, [(to, of[:]) for to, of in pairs], "stored")


def load(nc, tag, pairs):
    copies(nc, tag, [(to[:], of) for to, of in pairs], "loaded")


_INS = ['x_prompt', 'x_sample', 'c_prompt', 'c_sample', 'cache_ckv', 'cache_kpe', 'page_table', 'state_conv', 'state_ssm',
        'w_ada', 'b_ada', 'g_mix', 'w_in', 'g_q', 'g_ckv', 'w_uk', 'w_uv', 'g_k', 'conv_w', 'conv_b', 'dt_bias', 'a_log',
        'd_skip', 'g_ssm', 'w_br_a', 'w_br_b', 'w_out', 'g_ffn', 'peer_wq', 'peer_keys1', 'peer_keys2', 'peer_u', 'peer_v']
_OUTS = [('y_p', (1, TP, D)), ('y_s', (TS, 1, D)), ('ckv_p', (1, 1, TP, LAT)), ('kpe_p', (1, 1, TP, ROPE)),
         ('conv_p', (1, 1, CW - 1, CD)), ('ssm_p', (1, 1, SH, HD, N)), ('ckv_s', (1, TS, 1, LAT)), ('kpe_s', (1, TS, 1, ROPE)),
         ('conv_s', (1, TS, CW - 1, CD)), ('ssm_s', (1, TS, SH, HD, N))]


def rope_tables():
    half = ROPE // 2
    pos = np.concatenate([np.arange(TP), np.full(TS, PAST)]).astype(np.float32)
    inv = (10000.0 ** (-np.arange(half) / half)).astype(np.float32)
    angle = np.tile(inv[:, None] * pos[None, :], (2, 1))
    return np.cos(angle).astype(np.float32), np.sin(angle).astype(np.float32)


def kernel(**inputs):
    import numpy as _np
    import concourse.bacc as _bacc
    from concourse import mybir as _mybir
    from concourse.bass_utils import run_bass_kernel_spmd as _run

    nc = _bacc.Bacc("TRN2", target_bir_lowering=False, num_devices=1)
    arrays, A = {}, {}

    def give(name, a):
        arrays[f"in_{name}"] = a
        A[name] = nc.dram_tensor(f"in_{name}", a.shape, _mybir.dt.from_np(a.dtype), kind="ExternalInput").ap()

    for name in _INS:
        give(name, _np.ascontiguousarray(inputs[name]))
    cos, sin = rope_tables()
    give("rope_cos", cos)
    give("rope_sin", sin)
    outs = {name: nc.dram_tensor(f"out_{name}", shape, F32, kind="ExternalOutput").ap() for name, shape in _OUTS}
    D_ = {name: nc.dram_tensor(f"keep_{name}", shape, dt, kind="Internal").ap() for name, shape, dt in (
        ("proj", (C_GB + KD, P, T), F32), ("acs", (SH, TP), F32), ("ada", (TS + 1, 6 * D), F32), ("x1", (TT, P, D), F32), ("h2", (TT, P, D), F32),
        ("ids", (TT, P, SL), I32), ("gate", (TT, P, SL), F32))}
    step(nc, A, outs, D_)
    r = _run(nc, [arrays], core_ids=[0])
    return tuple(r.results[0][f"out_{name}"] for name, _ in _OUTS)
```
